# Optimizing a Trainium2 kernel written in Bass

```python
import jax, jax.numpy as jnp
from jax import lax
import numpy as np

D_MODEL = 2048
BATCH = 1
SEQ = 512
DEPTH = 1
DEC_BATCH = 8
DEC_SEQ = 1
PAST_LEN = 4096
PAGE_SIZE = 128

GLA_HEADS = 4
GLA_KEY_W = D_MODEL // 2
GLA_VAL_W = D_MODEL
GLA_DK = GLA_KEY_W // GLA_HEADS
GLA_DV = GLA_VAL_W // GLA_HEADS
GLA_RANK = 16
GLA_GATE_NORM = 16.0
GLA_CHUNK = 64
GMLP_W = D_MODEL // 2
GMLP_GROUPS = 4
GMLP_DG = GMLP_W // GMLP_GROUPS
GMLP_CHUNK = 128
N_MEM = 256
XA_HEADS = 4
XA_W = D_MODEL // 2
XA_DH = XA_W // XA_HEADS
N_BRANCH = 3
PEER_HEADS = 8
PEER_KEY_DIM = 256
PEER_HALF = PEER_KEY_DIM // 2
N_KEYS = 128
N_EXPERTS = N_KEYS * N_KEYS
PEER_TOPK = 16
PEER_BLOCK = 128
EPS = 1e-6
IN_SIZES = (GLA_KEY_W, GLA_KEY_W, GLA_VAL_W, GLA_VAL_W, GLA_RANK, GMLP_W, GMLP_W, XA_W, N_BRANCH * D_MODEL)
IN_COLS = GLA_KEY_W * 2 + GLA_VAL_W * 2 + GLA_RANK + GMLP_W * 2 + XA_W + N_BRANCH * D_MODEL

kernel_name = "hybrid_gla_gmlp_peer_decode_step"

def rmsnorm(x, g):
    xf = x.astype(jnp.float32)
    y = xf * lax.rsqrt(jnp.mean(xf * xf, axis=-1, keepdims=True) + EPS) * g.astype(jnp.float32)
    return y.astype(x.dtype)

def layernorm(x, g, b):
    xf = x.astype(jnp.float32)
    mu = jnp.mean(xf, axis=-1, keepdims=True)
    var = jnp.mean(jnp.square(xf - mu), axis=-1, keepdims=True)
    y = (xf - mu) * lax.rsqrt(var + EPS) * g.astype(jnp.float32) + b.astype(jnp.float32)
    return y.astype(x.dtype)

def split_columns(z):
    parts, start = [], 0
    for size in IN_SIZES:
        parts.append(z[..., start:start + size])
        start += size
    return parts

def gla_chunked(q, k, v, log_a, s0):
    B, T = q.shape[0], q.shape[1]
    C = min(GLA_CHUNK, T)
    n = -(-T // C)
    pad = n * C - T

    def prep(a):
        a = jnp.pad(a.astype(jnp.float32), ((0, 0), (0, pad), (0, 0), (0, 0)))
        return a.reshape(B, n, C, GLA_HEADS, a.shape[-1]).transpose(1, 0, 3, 2, 4)

    qc, kc, vc, ac = prep(q), prep(k), prep(v), prep(log_a)
    causal = jnp.tril(jnp.ones((C, C), dtype=bool))[:, :, None]

    def step(s, inp):
        qi, ki, vi, ai = inp
        b = jnp.cumsum(ai, axis=2)
        b_last = b[:, :, -1:, :]
        o_inter = jnp.einsum('bhtk,bhkv->bhtv', qi * jnp.exp(b), s)
        diff = b[:, :, :, None, :] - b[:, :, None, :, :]
        decay = jnp.exp(jnp.where(causal, diff, -jnp.inf))
        scores = jnp.einsum('bhtk,bhtsk,bhsk->bhts', qi, decay, ki)
        o_intra = jnp.einsum('bhts,bhsv->bhtv', scores, vi)
        s_new = s * jnp.exp(b_last[:, :, 0, :, None]) + jnp.einsum('bhsk,bhsv->bhkv', ki * jnp.exp(b_last - b), vi)
        return s_new, o_inter + o_intra

    s_fin, o = lax.scan(step, s0.astype(jnp.float32), (qc, kc, vc, ac))
    o = o.transpose(1, 0, 3, 2, 4).reshape(B, n * C, GLA_HEADS, GLA_DV)[:, :T]
    return o, s_fin

def gmlp_spatial_gate(u, v, ln_g, ln_b, w_s, b_s):
    B, T, _ = v.shape
    C = min(GMLP_CHUNK, T)
    n = T // C
    vn = layernorm(v, ln_g, ln_b)
    vc = vn.reshape(B, n, C, GMLP_GROUPS, GMLP_DG)
    w = jnp.tril(w_s[:, :C, :C]).astype(v.dtype)
    mixed = jnp.einsum('gts,bnsgd->bntgd', w, vc) + b_s[:, :C].T.astype(v.dtype)[None, None, :, :, None]
    return u * mixed.reshape(B, T, GMLP_W), vn

def memory_kv(mem, mem_norm_g, w_mem_kv):
    B = mem.shape[0]
    kv = rmsnorm(mem, mem_norm_g) @ w_mem_kv
    k = kv[..., :XA_W].reshape(B, N_MEM, XA_HEADS, XA_DH)
    v = kv[..., XA_W:].reshape(B, N_MEM, XA_HEADS, XA_DH)
    return k, v

def memory_attention(q, mem_k, mem_v):
    s = jnp.einsum('bthd,bmhd->bhtm', q, mem_k.astype(q.dtype)).astype(jnp.float32) * (XA_DH ** -0.5)
    p = jax.nn.softmax(s, axis=-1).astype(q.dtype)
    return jnp.einsum('bhtm,bmhd->bthd', p, mem_v.astype(q.dtype))

def mixing_block(x, mem_k, mem_v, s0, norm_g, w_in, b_gate, w_alpha_up, b_alpha, gla_norm_g,
                 gmlp_ln_g, gmlp_ln_b, gmlp_w_s, gmlp_b_s, w_br_gla, w_br_gmlp, w_br_xattn, w_out):
    B, T, _ = x.shape
    h = rmsnorm(x, norm_g)
    z = h @ w_in
    q, k, v, r, a_low, gu, gv, xq, gates = split_columns(z)
    log_a = jax.nn.log_sigmoid((a_low @ w_alpha_up + b_alpha).astype(jnp.float32)) / GLA_GATE_NORM
    o, s_new = gla_chunked(q.reshape(B, T, GLA_HEADS, GLA_DK) * (GLA_DK ** -0.5),
                           k.reshape(B, T, GLA_HEADS, GLA_DK),
                           v.reshape(B, T, GLA_HEADS, GLA_DV),
                           log_a.reshape(B, T, GLA_HEADS, GLA_DK), s0)
    o = rmsnorm(o, gla_norm_g.reshape(GLA_HEADS, GLA_DV)).reshape(B, T, GLA_VAL_W)
    branch_a = (o * jax.nn.silu(r.astype(jnp.float32))).astype(x.dtype)
    branch_b, v_rows = gmlp_spatial_gate(jax.nn.gelu(gu, approximate=False), jax.nn.gelu(gv, approximate=False),
                                         gmlp_ln_g, gmlp_ln_b, gmlp_w_s, gmlp_b_s)
    branch_c = memory_attention(xq.reshape(B, T, XA_HEADS, XA_DH), mem_k, mem_v).reshape(B, T, XA_W)
    g = jax.nn.sigmoid((gates + b_gate).astype(jnp.float32)).reshape(B, T, N_BRANCH, D_MODEL).astype(x.dtype)
    merged = g[:, :, 0] * (branch_a @ w_br_gla) + g[:, :, 1] * (branch_b @ w_br_gmlp) + g[:, :, 2] * (branch_c @ w_br_xattn)
    return x + merged @ w_out, s_new, v_rows

def peer_ffn(h, w_q, sub_k1, sub_k2, u_tab, v_tab):
    B, T, D = h.shape
    N = B * T
    hf = h.reshape(N, D)
    q = (hf @ w_q).reshape(N, PEER_HEADS, 2, PEER_HALF).astype(jnp.float32)
    s1 = jnp.einsum('nhd,hkd->nhk', q[:, :, 0], sub_k1.astype(jnp.float32))
    s2 = jnp.einsum('nhd,hkd->nhk', q[:, :, 1], sub_k2.astype(jnp.float32))
    v1, i1 = lax.top_k(s1, PEER_TOPK)
    v2, i2 = lax.top_k(s2, PEER_TOPK)
    cand = (v1[..., :, None] + v2[..., None, :]).reshape(N, PEER_HEADS, PEER_TOPK * PEER_TOPK)
    sv, si = lax.top_k(cand, PEER_TOPK)
    e1 = jnp.take_along_axis(i1, si // PEER_TOPK, axis=-1)
    e2 = jnp.take_along_axis(i2, si % PEER_TOPK, axis=-1)
    idx = e1 * N_KEYS + e2
    gate = jax.nn.softmax(sv, axis=-1)
    n_blk = -(-N // PEER_BLOCK)
    pad = n_blk * PEER_BLOCK - N
    hp = jnp.pad(hf, ((0, pad), (0, 0))).reshape(n_blk, PEER_BLOCK, D)
    ip = jnp.pad(idx, ((0, pad), (0, 0), (0, 0))).reshape(n_blk, PEER_BLOCK, PEER_HEADS, PEER_TOPK)
    gp = jnp.pad(gate, ((0, pad), (0, 0), (0, 0))).reshape(n_blk, PEER_BLOCK, PEER_HEADS, PEER_TOPK)

    def block(args):
        hb, ib, gb = args
        a = jnp.einsum('nhkd,nd->nhk', u_tab[ib], hb)
        coef = (gb * jax.nn.gelu(a.astype(jnp.float32), approximate=False)).astype(hb.dtype)
        return jnp.einsum('nhk,nhkd->nd', coef, v_tab[ib])

    out = lax.map(block, (hp, ip, gp))
    return out.reshape(n_blk * PEER_BLOCK, D)[:N].reshape(B, T, D)

def setup_inputs(seed: int = 0) -> dict:
    key = jax.random.key(seed)
    ks = jax.random.split(key, 40)
    counter = [0]

    def nxt():
        k = ks[counter[0]]
        counter[0] += 1
        return k

    def nrm(shape, scale):
        return jax.random.normal(nxt(), shape, jnp.float32) * scale

    def gain(shape):
        return 1.0 + 0.1 * jax.random.normal(nxt(), shape, jnp.float32)

    return {
        "x_prompt": nrm((BATCH, SEQ, D_MODEL), 1.0),
        "x_sample": nrm((DEC_BATCH, DEC_SEQ, D_MODEL), 1.0),
        "mem_prompt": nrm((BATCH, N_MEM, D_MODEL), 1.0),
        "state_gla": nrm((DEPTH, DEC_BATCH, GLA_HEADS, GLA_DK, GLA_DV), 1.0),
        "cache_mem_k": nrm((DEPTH, DEC_BATCH, N_MEM, XA_HEADS, XA_DH), 1.0),
        "cache_mem_v": nrm((DEPTH, DEC_BATCH, N_MEM, XA_HEADS, XA_DH), 1.0),
        "norm_mix_g": gain((DEPTH, D_MODEL)),
        "w_in": nrm((DEPTH, D_MODEL, IN_COLS), D_MODEL ** -0.5),
        "b_gate": nrm((DEPTH, N_BRANCH * D_MODEL), 0.1),
        "w_alpha_up": nrm((DEPTH, GLA_RANK, GLA_KEY_W), GLA_RANK ** -0.5),
        "b_alpha": nrm((DEPTH, GLA_KEY_W), 0.5),
        "gla_norm_g": gain((DEPTH, GLA_VAL_W)),
        "gmlp_ln_g": gain((DEPTH, GMLP_W)),
        "gmlp_ln_b": nrm((DEPTH, GMLP_W), 0.02),
        "gmlp_w_s": nrm((DEPTH, GMLP_GROUPS, GMLP_CHUNK, GMLP_CHUNK), GMLP_CHUNK ** -0.5),
        "gmlp_b_s": gain((DEPTH, GMLP_GROUPS, GMLP_CHUNK)),
        "mem_norm_g": gain((DEPTH, D_MODEL)),
        "w_mem_kv": nrm((DEPTH, D_MODEL, 2 * XA_W), D_MODEL ** -0.5),
        "w_br_gla": nrm((DEPTH, GLA_VAL_W, D_MODEL), GLA_VAL_W ** -0.5),
        "w_br_gmlp": nrm((DEPTH, GMLP_W, D_MODEL), GMLP_W ** -0.5),
        "w_br_xattn": nrm((DEPTH, XA_W, D_MODEL), XA_W ** -0.5),
        "w_out": nrm((DEPTH, D_MODEL, D_MODEL), D_MODEL ** -0.5),
        "norm_ffn_g": gain((DEPTH, D_MODEL)),
        "peer_w_q": nrm((DEPTH, D_MODEL, PEER_HEADS * PEER_KEY_DIM), D_MODEL ** -0.5),
        "peer_sub_k1": nrm((DEPTH, PEER_HEADS, N_KEYS, PEER_HALF), PEER_HALF ** -0.5),
        "peer_sub_k2": nrm((DEPTH, PEER_HEADS, N_KEYS, PEER_HALF), PEER_HALF ** -0.5),
        "peer_u": nrm((DEPTH, N_EXPERTS, D_MODEL), D_MODEL ** -0.5),
        "peer_v": nrm((DEPTH, N_EXPERTS, D_MODEL), 0.5),
        "norm_final_g": gain((D_MODEL,)),
    }

def reference(x_prompt, x_sample, mem_prompt, state_gla, cache_mem_k, cache_mem_v,
              norm_mix_g, w_in, b_gate, w_alpha_up, b_alpha, gla_norm_g,
              gmlp_ln_g, gmlp_ln_b, gmlp_w_s, gmlp_b_s, mem_norm_g, w_mem_kv,
              w_br_gla, w_br_gmlp, w_br_xattn, w_out, norm_ffn_g,
              peer_w_q, peer_sub_k1, peer_sub_k2, peer_u, peer_v, norm_final_g):
    xp, xs = x_prompt, x_sample
    gla_p, gla_s, mk_p, mv_p, gv_s = [], [], [], [], []
    for l in range(DEPTH):
        block_w = (norm_mix_g[l], w_in[l], b_gate[l], w_alpha_up[l], b_alpha[l], gla_norm_g[l],
                   gmlp_ln_g[l], gmlp_ln_b[l], gmlp_w_s[l], gmlp_b_s[l],
                   w_br_gla[l], w_br_gmlp[l], w_br_xattn[l], w_out[l])
        mk, mv = memory_kv(mem_prompt, mem_norm_g[l], w_mem_kv[l])
        s0_p = jnp.zeros((xp.shape[0], GLA_HEADS, GLA_DK, GLA_DV), jnp.float32)
        xp, sp, _ = mixing_block(xp, mk, mv, s0_p, *block_w)
        xs, ss, vrows = mixing_block(xs, cache_mem_k[l], cache_mem_v[l], state_gla[l], *block_w)
        peer_w = (peer_w_q[l], peer_sub_k1[l], peer_sub_k2[l], peer_u[l], peer_v[l])
        xp = xp + peer_ffn(rmsnorm(xp, norm_ffn_g[l]), *peer_w)
        xs = xs + peer_ffn(rmsnorm(xs, norm_ffn_g[l]), *peer_w)
        gla_p.append(sp)
        gla_s.append(ss)
        mk_p.append(mk)
        mv_p.append(mv)
        gv_s.append(vrows)
    y_prompt = rmsnorm(xp, norm_final_g)
    y_sample = rmsnorm(xs, norm_final_g)
    return (y_prompt, y_sample, jnp.stack(gla_p), jnp.stack(gla_s), jnp.stack(mk_p), jnp.stack(mv_p), jnp.stack(gv_s))


_drawn_inputs = setup_inputs


def setup_inputs(seed=0):
    import zlib

    import numpy as np

    out = dict(_drawn_inputs(seed))
    spreads = {}
    factors = {'gmlp_ln_b': 2.766}
    for name, (base, spread) in spreads.items():
        noise = np.random.default_rng([zlib.crc32(name.encode()), seed]).standard_normal(out[name].shape)
        drawn = base * np.exp(spread * noise) if base else spread * noise
        out[name] = __import__('jax').numpy.asarray(drawn.astype(out[name].dtype))
    for name, factor in factors.items():
        out[name] = (out[name] * factor).astype(out[name].dtype)
    return out
```

```python
from contextlib import ExitStack

import numpy as np

import concourse.bass as bass
from concourse import mybir
from concourse.alu_op_type import AluOpType as ALU

ACT = mybir.ActivationFunctionType
AX = mybir.AxisListType
F32 = mybir.dt.float32
F32R = mybir.dt.float32r
U32 = mybir.dt.uint32

P = 128
D = 2048
KT = D // P
TP = 512
TS = 8
TN = TP + TS
HALF = TN // 2
MEM = 256
EPS = 1e-6
HEADS = 4
DK = 256
DV = 512
RANK = 16
CH = 128
NCH = TP // CH
SUB = 32
GATE_NORM = 16.0
CLAMP = 40.0 * GATE_NORM
PH = 8
NK = 128
TOP = 16
SLOTS = PH * TOP
RING = 8

N_MEM0 = 0
N_XQ = 16
N_Q = N_XQ + 8
N_K = N_Q + 8
N_V = N_K + 8
N_LOW = N_V + 16
N_GU = N_LOW + 1
N_GV = N_GU + 8
N_R = N_GV + 8
N_G = N_R + 16
N_BC = N_G + 48
N_BB = N_BC + 8
N_BA = N_BB + 8
N_OUT = N_BA + 16
N_WQ = N_OUT + 16
N_END = N_WQ + 16

C_MIX, C_FFN, C_MEM, C_BG, C_BA, C_GLA = 0, 16, 32, 48, 96, 104
NCOLS = 120

SBUF0 = 16512


def outputs_before(n):
    return n + max(0, min(n, N_BA) - N_BC)


def mixer_kernel(nc, ins, outs, upto=99):
    ctx = ExitStack()
    with ctx:
        def sb(name, shape, dt, at):
            return nc.alloc_sbuf_tensor_at("sb_" + name, shape, dt, offset=SBUF0 + at)

        def sem(name):
            return ctx.enter_context(nc.semaphore(name))

        def dram(name, shape):
            return nc.dram_tensor("dram_" + name, shape, F32).ap()

        R_C = 49152
        R_1 = 65536
        R_2 = R_1 + 66560
        R_3 = R_2 + 33280
        R_X = R_3 + 33280
        raw = sb("raw", [P, 2, D], F32, 0)
        split = sb("split", [P, 2, 2, D], F32R, 16384)
        ident = sb("ident", [P, P], F32, R_C)
        ones = sb("ones", [P, P], F32, R_C + 512)
        tri = sb("tri", [P, P], F32, R_C + 1024)
        pcols = sb("pcols", [P, NCOLS], F32, R_C + 1536)
        zst = sb("zst", [P, 2, TN], F32, R_C + 2048)
        gt = sb("gt", [P, 2, TN], F32, R_C + 6208)
        rstd = sb("rstd", [P, TN], F32, R_C + 10368)
        ssum = sb("ssum", [P, TN], F32, R_C + 12448)
        bcur = sb("bcur", [P, 2], F32, R_C + 14528)
        small = sb("small", [P, 400], F32, R_C + 14592)

        sqx = sb("sqx", [P, KT, TN], F32, R_1)
        memx = sb("memx", [P, KT, MEM], F32, R_1 + 33280)
        sqm = sb("sqm", [P, KT, MEM], F32, R_1 + 49664)
        memr = sb("memr", [P, 2, KT, MEM], F32R, R_2)
        hx = sb("hx", [P, KT, TN], F32, R_3)
        actr = sb("actr", [P, 2, KT, TN], F32R, R_1)

        xq = sb("xq", [P, 8, TN], F32, R_1)
        kvt = sb("kvt", [P, 16, MEM], F32, R_1 + 16640)
        kvtok = sb("kvtok", [P, 2, 2048], F32, R_1 + 33024)
        prob = sb("prob", [P, 2, 4, MEM], F32, R_1 + 49408)
        probt = sb("probt", [P, 2, 2, TP], F32, R_1 + 57600)
        br2 = sb("br2", [P, 2, 8, TN], F32R, R_2)
        kcache = sb("kcache", [P, 2, 8, MEM], F32, R_3)
        vcache = sb("vcache", [P, 2, 2, 1024], F32, R_3 + 16384)
        qmask = sb("qmask", [P, 2, 32 * 32], F32, R_X)
        prob_s = sb("prob_s", [32, MEM], F32, R_X + 8192)
        probt_s = sb("probt_s", [P, 2, 32], F32, R_X + 9216)
        merged = sb("merged", [P, KT, TN], F32, R_3)

        gv = sb("gv", [P, 8, TN], F32, R_1)
        gu = sb("gu", [P, 8, TN], F32, R_1 + 16640)
        vn = sb("vn", [P, 2, 1024], F32, R_1 + 33280)
        lnrow = sb("lnrow", [P, 2, 1024], F32, R_1 + 41472)
        wspat = sb("wspat", [P, HEADS, CH], F32, R_1 + 49664)
        gated = sb("gated", [P, 2, 8, CH], F32, R_1 + 51712)
        bspat = sb("bspat", [1, HEADS * CH], F32, R_1 + 59904)
        wfirst = sb("wfirst", [TS, HEADS], F32, R_1 + 61952)
        wdiag = sb("wdiag", [TS, HEADS, TS], F32, R_1 + 61984)
        bfirst = sb("bfirst", [1, HEADS, TS], F32, R_1 + 62112)

        state = sb("state", [P, 8, DV], F32, R_1)
        bcum = sb("bcum", [P, 8, TN], F32, R_1 + 16384)
        qc = sb("qc", [P, 8, CH], F32, R_1 + 33024)
        kc = sb("kc", [P, 8, CH], F32, R_1 + 37120)
        vc = sb("vc", [P, KT, CH], F32, R_1 + 41216)
        rc = sb("rc", [P, KT, CH], F32, R_1 + 49408)
        vtok = sb("vtok", [P, D], F32, R_1 + 57600)
        gx = sb("gx", [P, 8, TN], F32, R_2)
        gy = sb("gy", [P, 8, TN], F32, R_2 + 16640)
        qe = sb("qe", [P, 8, CH], F32, R_2)
        kd = sb("kd", [P, 8, CH], F32, R_2 + 4096)
        eb = sb("eb", [P, 8, CH], F32, R_2 + 8192)
        ki = sb("ki", [P, 2, 8, CH], F32, R_2 + 12288)
        kdtok = sb("kdtok", [P, 1024], F32, R_2 + 20480)
        scores_t = sb("scores_t", [P, HEADS, CH], F32, R_2 + 24576)
        qi = sb("qi", [P, 2, 8, SUB], F32, R_2 + 26624)
        norm_a = sb("norm_a", [P, HEADS, CH], F32, R_2 + 28672)
        low = sb("low", [RANK, TN], F32, R_X)
        w_up = sb("w_up", [RANK, 1024], F32, R_X + 2080)
        keep = sb("keep", [P, TP], F32, R_X + 6176)
        state2 = sb("state2", [P, 8, DV], F32, R_1 + 33024)
        states = [state, state2]
        qs = sb("qs", [P, 8, TS], F32, R_X + 8224)
        ks = sb("ks", [P, 8, TS], F32, R_X + 8480)
        vs = sb("vs", [P, KT, TS], F32, R_X + 8736)
        rs = sb("rs", [P, KT, TS], F32, R_X + 9248)
        es = sb("es", [P, 8, TS], F32, R_X + 9760)
        sqs = sb("sqs", [P, KT, TS], F32, R_X + 10016)
        norm_s = sb("norm_s", [P, HEADS, TS], F32, R_X + 10528)
        k8 = sb("k8", [TS, 1024], F32, R_2)
        v8 = sb("v8", [TS, D], F32, R_2 + 4096)
        k8one = sb("k8one", [TS, 2, 1024], F32, R_2 + 12288)
        bra = sb("bra", [P, KT, TN], F32, R_2)

        x1 = sb("x1", [P, KT, TN], F32, R_2)
        sq2 = sb("sq2", [P, KT, TN], F32, R_3)
        h2 = sb("h2", [P, KT, TN], F32, R_3)
        pq = sb("pq", [P, KT, TN], F32, R_2)
        keys = sb("keys", [P, PH, 2, NK], F32, R_X)
        stage_x = [sb("stage_x0", [P, D], F32, R_X), sb("stage_x1", [P, D], F32, R_C + 2048)]
        stage_s = [sb("stage_s0", [P, D], F32, 0), sb("stage_s1", [P, D], F32, 8192)]
        stage_h = [sb("stage_h0", [P, D], F32, 16384), sb("stage_h1", [P, D], F32, 24576)]

        u_ring = [sb(f"u_ring{i}", [P, D], F32, 65536 + 8192 * i) for i in range(RING)]
        v_ring = [sb(f"v_ring{i}", [P, D], F32, 65536 + 8192 * (RING + i)) for i in range(RING)]
        htok2 = sb("htok2", [TS, D], F32, 0)
        htok = sb("htok", [P, D], F32, 65536 + 8192 * 2 * RING)
        gfin = sb("gfin", [P, D], F32, 16384)
        sc = sb("sc", [P, PH, 2, NK], F32, 24576)
        acc = sb("acc", [P, D], F32, 32768)
        yout = sb("yout", [P, D], F32, 40960)
        R_S = 65536 + 8192 * (2 * RING + 1)
        top_v = sb("top_v", [P, 2, TOP], F32, R_S)
        top_i = sb("top_i", [P, 2, TOP], U32, R_S + 128)
        top_if = sb("top_if", [P, 2, TOP], F32, R_S + 256)
        rest = sb("rest", [P, 2, NK], F32, R_S + 384)
        cand = sb("cand", [P, TOP, TOP], F32, R_S + 1408)
        cand2 = sb("cand2", [P, TOP, TOP], F32, R_S + 2432)
        hot = sb("hot", [P, 2, TOP, TOP], F32, R_S + 3456)
        pos = sb("pos", [P, TOP], U32, R_S + 5504)
        pos2 = sb("pos2", [P, 2, TOP], U32, R_S + 5568)
        pos_f = sb("pos_f", [P, 2, TOP], F32, R_S + 5696)
        e_f = sb("e_f", [P, 2, TOP], F32, R_S + 5824)
        iota_u = sb("iota_u", [P, TOP], U32, R_S + 5952)
        iota_f = sb("iota_f", [P, TOP], F32, R_S + 6016)
        sel = sb("sel", [P, TS], F32, R_S + 6080)
        sums = sb("sums", [P, 16], F32, R_S + 6112)
        dots = sb("dots", [P, SLOTS], F32, R_S + 6176)
        gelus = sb("gelus", [P, SLOTS], F32, R_S + 6688)
        coef = sb("coef", [P, SLOTS], F32, R_S + 7200)
        idx_next = sb("idx_next", [P, SLOTS], U32, R_C + 2048)
        idx_cur = sb("idx_cur", [P, SLOTS], U32, R_C + 2560)
        gate_next = sb("gate_next", [P, PH, TOP], F32, R_C + 3072)
        gate_cur = sb("gate_cur", [P, SLOTS], F32, R_C + 3584)
        idx_s = sb("idx_s", [P, TS], U32, R_C + 4096)
        gate_s = sb("gate_s", [P, TS], F32, R_C + 4128)

        psum = ctx.enter_context(nc.psum_tensor("psum", [P, 8, 512], F32))

        z = dram("z", [N_BC, P, TN])

        bra_dram = dram("bra", [P, KT, TN])
        x1_dram = dram("x1", [TN, D])
        h2_dram = dram("h2", [TN, D])
        sc_dram = dram("sc", [(NCH + 1) * P, D])
        idx_dram = nc.dram_tensor("dram_idx", [TS, SLOTS], U32).ap()
        gate_dram = dram("gate", [TS, SLOTS])
        dbg = sem("dbg")
        const_loaded = sem("const_loaded")
        mem_loaded = sem("mem_loaded")
        x_loaded = sem("x_loaded")
        const_made = sem("const_made")
        raw_landed = [sem("raw_landed0"), sem("raw_landed1")]
        hi_ready = sem("hi_ready")
        lo_ready = sem("lo_ready")
        out_ready = sem("out_ready")
        evac_done = sem("evac_done")
        z_stored = [sem("z_stored0"), sem("z_stored1")]
        squares_ready = sem("squares_ready")
        sums_ready = sem("sums_ready")
        spread_ready = sem("spread_ready")
        root_in = sem("root_in")
        root_out = sem("root_out")
        normed = sem("normed")
        act_hi = sem("act_hi")
        act_lo = sem("act_lo")

        gate_landed = [sem("gate_landed0"), sem("gate_landed1")]
        xq_loaded = sem("xq_loaded")
        kvt_loaded = sem("kvt_loaded")
        kc_landed = [sem("kc_landed0"), sem("kc_landed1")]
        vc_landed = [sem("vc_landed0"), sem("vc_landed1")]
        kc_used = sem("kc_used")
        vc_used = sem("vc_used")
        qm_zeroed = sem("qm_zeroed")
        qm_ready = sem("qm_ready")
        att_scores = sem("att_scores")
        att_max = sem("att_max")
        att_exp = sem("att_exp")
        att_prob = sem("att_prob")
        att_turned = sem("att_turned")
        att_probt = sem("att_probt")
        att_out = sem("att_out")
        kv_turned = sem("kv_turned")
        kv_tok = sem("kv_tok")
        out_stored = sem("out_stored")
        br_hi = sem("br_hi")
        br_lo = sem("br_lo")

        gv_loaded = sem("gv_loaded")
        gu_loaded = sem("gu_loaded")
        sp_loaded = sem("sp_loaded")
        sp_masked = sem("sp_masked")
        sp_turned = sem("sp_turned")
        sp_var = sem("sp_var")
        sp_root = sem("sp_root")
        sp_vn = sem("sp_vn")
        sp_mixed = sem("sp_mixed")
        sp_gated = sem("sp_gated")
        vn_stored = sem("vn_stored")
        low_loaded = sem("low_loaded")
        keep_made = sem("keep_made")
        up_ready = sem("up_ready")
        up_read = sem("up_read")
        gx_ready = sem("gx_ready")
        gy_ready = sem("gy_ready")
        bcum_ready = sem("bcum_ready")
        chunk_loaded = sem("chunk_loaded")
        chunk_stored = sem("chunk_stored")
        eb_ready = sem("eb_ready")
        qe_ready = sem("qe_ready")
        kd_in = sem("kd_in")
        kd_exp = sem("kd_exp")
        kd_ready = sem("kd_ready")
        sub_in = sem("sub_in")
        sub_exp = sem("sub_exp")
        sub_ready = sem("sub_ready")
        sub_scored = sem("sub_scored")
        sc_ready = sem("sc_ready")
        v_turned = sem("v_turned")
        v_tok = sem("v_tok")
        kd_turned = sem("kd_turned")
        kd_tok = sem("kd_tok")
        o_ready = sem("o_ready")
        o_squared = sem("o_squared")
        o_summed = sem("o_summed")
        o_var = sem("o_var")
        o_root = sem("o_root")
        o_normed = sem("o_normed")
        o_read = sem("o_read")
        kv_ready = sem("kv_ready")
        kv_read = sem("kv_read")
        state_done = sem("state_done")
        state_out = [sem("state_out0"), sem("state_out1")]
        state_in = [sem("state_in0"), sem("state_in1")]
        samples_loaded = sem("samples_loaded")
        one_ready = sem("one_ready")
        bra_loaded = sem("bra_loaded")

        pq_ready = sem("pq_ready")
        stage_zero = sem("stage_zero")
        acc_s_loaded = sem("acc_s_loaded")
        merged_ready = sem("merged_ready")
        x1_loaded = sem("x1_loaded")
        x1_ready = sem("x1_ready")
        x1_turned = sem("x1_turned")
        x1_staged = sem("x1_staged")
        x1_stored = [sem("x1_stored0"), sem("x1_stored1")]
        keys_loaded = sem("keys_loaded")
        scored = sem("scored")
        sc_staged = sem("sc_staged")
        sc_stored = [sem("sc_stored0"), sem("sc_stored1")]
        h2_turned = sem("h2_turned")
        h2_staged = sem("h2_staged")
        h2_stored = [sem("h2_stored0"), sem("h2_stored1")]
        gfin_loaded = sem("gfin_loaded")
        peer_made = sem("peer_made")
        sc_loaded = sem("sc_loaded")
        sc_used = sem("sc_used")
        soft_in = sem("soft_in")
        soft_exp = sem("soft_exp")
        idx_ready = sem("idx_ready")
        htok_loaded = sem("htok_loaded")
        acc_loaded = sem("acc_loaded")
        u_landed = [sem(f"u_landed{i}") for i in range(RING)]
        v_landed = [sem(f"v_landed{i}") for i in range(RING)]
        slots_granted = sem("slots_granted")
        u_used = sem("u_used")
        v_used = sem("v_used")
        dots_ready = sem("dots_ready")
        gelu_ready = sem("gelu_ready")
        acc_ready = sem("acc_ready")
        y_squared = sem("y_squared")
        y_var = sem("y_var")
        y_root = sem("y_root")
        y_ready = sem("y_ready")
        y_stored = sem("y_stored")
        packed = sem("packed")
        unpacked = sem("unpacked")
        folded = sem("folded")

        block = ctx.enter_context(nc.Block())

        def load_block(sp, n, slot):
            if not isinstance(n, int) or n >= 2:
                sp.wait_ge(hi_ready, n - 1)
                sp.wait_ge(lo_ready, n - 1)
            src = ins["wstream"][bass.ds(n, 1), :, :].rearrange("a p c -> (a p) c")
            sp.dma_start(raw[:, slot, :], src).then_inc(raw_landed[slot], 16)

        def split_hi(act, n, slot, use, outs_done):
            act.wait_ge(raw_landed[slot], 16 * use)
            if not isinstance(outs_done, int) or outs_done > 0:
                act.wait_ge(out_ready, outs_done)
            nc.scalar.activation(split[:, slot, 0, :], raw[:, slot, :], ACT.Copy).then_inc(hi_ready, 1)

        def split_lo(dve, n, slot):
            dve.wait_ge(hi_ready, n + 1)
            nc.vector.tensor_tensor(split[:, slot, 1, :], raw[:, slot, :], split[:, slot, 0, :],
                                    ALU.subtract).then_inc(lo_ready, 1)

        def products(pe, slot, acts, kts, w0, pair, ntok, halves=2):
            for i, kt in enumerate(kts):
                w = [split[:, slot, x, w0 + i * P:w0 + (i + 1) * P] for x in range(2)]
                for a, b in ((0, 0), (0, 1), (1, 0)):
                    for half in range(halves):
                        last = nc.tensor.matmul(
                            psum[:, 2 * pair + half, 0:ntok], w[a], acts[:, b, kt, half * ntok:(half + 1) * ntok],
                            start=(i == 0 and a == 0 and b == 0), stop=(i == len(kts) - 1 and a == 1))
            return last

        def flat(ap):
            return ap.rearrange("p h t -> p (h t)")

        def pair_of(pair, ntok=HALF):
            return psum[:, 2 * pair:2 * pair + 2, 0:ntok]

        def in_halves(ap):
            return ap.rearrange("p (h t) -> p h t", h=2)

        PLAIN = [(N_MEM0, N_XQ, ACT.Copy, MEM), (N_XQ, N_LOW, ACT.Copy, TN), (N_LOW, N_GU, ACT.Copy, TN),
                 (N_GU, N_R, ACT.Gelu, TN), (N_R, N_G, ACT.Silu, TN), (N_G, N_BC, ACT.Sigmoid, TN)]

        def seg_loop(eng, n0, n1, body):
            if n1 - n0 == 1 or n0 == 0:
                k = 1 if n1 - n0 == 1 else 2
                for n in range(n0, n0 + k):
                    body(n, n % 2, (n - n % 2) // 2)
                n0 += k
            assert (n1 - n0) % 2 == 0
            if n0 < n1:
                with eng.Fori(0, (n1 - n0) // 2) as i:
                    for b in range(2):
                        n = n0 + b
                        body(i * 2 + n, n % 2, i + (n - n % 2) // 2)

        def sp_attention(sp):
            sp.wait_ge(z_stored[0], 16 * ((N_BC + 1) // 2))
            sp.wait_ge(z_stored[1], 16 * (N_BC // 2))
            sp.dma_start(xq[:], z[N_XQ:N_Q].rearrange("n p t -> p n t")).then_inc(xq_loaded, 16)
            for s in range(2):
                sp.dma_start(kcache[:, s], ins["kcache"][s]).then_inc(kc_landed[s], 16)
            sp.dma_start(kvt[:], z[0:16, :, 0:MEM].rearrange("n p t -> p n t")).then_inc(kvt_loaded, 16)
            for s in range(2):
                sp.dma_start(vcache[:, s], ins["vcache"][s]).then_inc(vc_landed[s], 16)
            for s in range(2, TS):
                sp.wait_ge(kc_used, s - 1)
                sp.dma_start(kcache[:, s % 2], ins["kcache"][s]).then_inc(kc_landed[s % 2], 16)
            for s in range(2, TS):
                sp.wait_ge(vc_used, s - 1)
                sp.dma_start(vcache[:, s % 2], ins["vcache"][s]).then_inc(vc_landed[s % 2], 16)
            sp.wait_ge(kv_tok, 8)
            for mt in range(2):
                sp.dma_start(outs["mem_k"][mt * P:(mt + 1) * P, :], kvtok[:, mt, 0:1024]).then_inc(out_stored, 16)
                sp.dma_start(outs["mem_v"][mt * P:(mt + 1) * P, :], kvtok[:, mt, 1024:2048]).then_inc(out_stored, 16)
            load_gates_ahead(sp)

        def load_gates_ahead(sp):
            for m in (N_BC, N_BC + 1):
                load_gate(sp, m, m % 2)

        def load_gate(sp, m, slot):
            src = z[bass.ds(m + (N_G - N_BC), 1), :, :].rearrange("a p t -> (a p) t")
            sp.dma_start(gt[:, slot, :], src).then_inc(gate_landed[slot], 16)

        def pool_constants(pool):
            nc.gpsimd.memset(ident[:], 0.0)
            nc.gpsimd.memset(tri[:], 1.0)
            pool.drain()
            nc.gpsimd.affine_select(out=ident[:], in_=ident[:], pattern=[[-1, P]], compare_op=ALU.not_equal,
                                    fill=1.0, base=0, channel_multiplier=1).then_inc(const_made, 1)
            nc.gpsimd.affine_select(out=tri[:], in_=tri[:], pattern=[[1, P]], compare_op=ALU.is_ge,
                                    fill=0.0, base=0, channel_multiplier=-1).then_inc(const_made, 1)

        def pool_attention(pool):
            pool.wait_ge(evac_done, N_XQ)
            nc.gpsimd.memset(qmask[:], 0.0).then_inc(qm_zeroed, 1)

        def pe_attention(pe):
            pe.wait_ge(evac_done, N_BC)
            pe.wait_ge(qm_ready, 1)
            for s in range(TS):
                pe.wait_ge(kc_landed[s % 2], 16 * (s // 2 + 1))
                for h in range(HEADS):
                    for dt in range(2):
                        i = s * HEADS + h
                        last = nc.tensor.matmul(psum[0:32, 7, 0:MEM], qmask[:, dt, i * 32:(i + 1) * 32],
                                                kcache[:, s % 2, 2 * h + dt, :],
                                                start=(i == 0 and dt == 0), stop=(i == 31 and dt == 1))
                last.then_inc(kc_used, 1)
            last = None
            pe.wait_ge(kvt_loaded, 16)
            pe.wait_ge(const_made, 3)
            for g in range(8):
                mt, f0 = g % 2, 4 * (g // 2)
                if g >= 2:
                    pe.wait_ge(kv_tok, g - 1)
                for j in range(4):
                    last = nc.tensor.transpose(psum[:, 4 + g % 2, j * P:(j + 1) * P],
                                               kvt[:, f0 + j, mt * P:(mt + 1) * P], ident[:])
                last.then_inc(kv_turned, 1)

            def scores(h):
                if h >= 2:
                    pe.wait_ge(att_exp, h)
                for tt in range(4):
                    for dt in range(2):
                        last = nc.tensor.matmul(
                            psum[:, 2 * (h % 2) + tt // 2, (tt % 2) * MEM:(tt % 2 + 1) * MEM],
                            xq[:, 2 * h + dt, tt * P:(tt + 1) * P], kvt[:, 2 * h + dt, :],
                            start=(dt == 0), stop=(dt == 1))
                last.then_inc(att_scores, 1)

            scores(0)
            scores(1)
            pe.wait_ge(att_prob, 1)
            pe.wait_ge(kv_tok, 8)
            for mt in range(2):
                last = nc.tensor.transpose(psum[:, 4, mt * 32:(mt + 1) * 32], prob_s[:, mt * P:(mt + 1) * P],
                                           ident[0:32, 0:32])
            last.then_inc(att_turned, 1)
            pe.wait_ge(att_probt, 1)
            for s in range(TS):
                pe.wait_ge(vc_landed[s % 2], 16 * (s // 2 + 1))
                for f in range(8):
                    for mt in range(2):
                        last = nc.tensor.matmul(psum[:, 7, f * TS + s:f * TS + s + 1],
                                                vcache[:, s % 2, mt, f * P:(f + 1) * P],
                                                probt_s[:, mt, s * HEADS + f // 2:s * HEADS + f // 2 + 1],
                                                start=(mt == 0), stop=(mt == 1))
                last.then_inc(vc_used, 1)
            for h in range(HEADS):
                pe.wait_ge(att_prob, h + 2)
                for mt in range(2):
                    for tt in range(4):
                        last = nc.tensor.transpose(psum[:, 4 + mt, tt * P:(tt + 1) * P],
                                                   prob[:, h % 2, tt, mt * P:(mt + 1) * P], ident[:])
                last.then_inc(att_turned, 1)
                if h + 2 < HEADS:
                    scores(h + 2)
                pe.wait_ge(att_probt, h + 2)
                pe.wait_ge(br_hi, h + 1)
                pe.wait_ge(br_lo, h + 1)
                for dt in range(2):
                    c0 = 1024 + h * 256 + dt * P
                    for mt in range(2):
                        last = nc.tensor.matmul(psum[:, 6 + dt, :], kvtok[:, mt, c0:c0 + P], probt[:, h % 2, mt, :],
                                                start=(mt == 0), stop=(mt == 1))
                last.then_inc(att_out, 1)

        def act_attention(act):
            act.wait_ge(att_max, 1)
            nc.scalar.activation(prob_s[:], psum[0:32, 7, 0:MEM], ACT.Exp, bias=small[0:32, 0:1], scale=1.0 / 16,
                                 accum_out=small[0:32, 8:9]).then_inc(att_exp, 1)
            def exps(h):
                act.wait_ge(att_max, h + 2)
                if h >= 2:
                    act.wait_ge(att_turned, h)
                for tt in range(4):
                    c = 16 + 16 * (h % 2) + tt
                    last = nc.scalar.activation(prob[:, h % 2, tt, :],
                                                psum[:, 2 * (h % 2) + tt // 2, (tt % 2) * MEM:(tt % 2 + 1) * MEM],
                                                ACT.Exp, bias=small[:, c:c + 1], scale=1.0 / 16,
                                                accum_out=small[:, c + 8:c + 9])
                last.then_inc(att_exp, 1)

            exps(0)
            exps(1)
            act.wait_ge(att_turned, 1)
            nc.scalar.activation(probt_s[:], psum[:, 4, 0:64].rearrange("p (m i) -> p m i", m=2),
                                 ACT.Copy).then_inc(att_probt, 1)
            act.wait_ge(vc_used, TS)
            act.wait_ge(out_ready, N_BC)
            nc.scalar.activation(br2[:, 0, :, TP:TN], psum[:, 7, 0:64].rearrange("p (f s) -> p f s", f=8),
                                 ACT.Copy).then_inc(br_hi, 1)
            for h in range(HEADS):
                act.wait_ge(att_turned, h + 2)
                nc.scalar.activation(probt[:, h % 2], psum[:, 4:6, :], ACT.Copy).then_inc(att_probt, 1)
                if h + 2 < HEADS:
                    exps(h + 2)
                act.wait_ge(att_out, h + 1)
                nc.scalar.activation(br2[:, 0, 2 * h:2 * h + 2, 0:TP], psum[:, 6:8, :], ACT.Copy).then_inc(br_hi, 1)

        def dve_attention(dve):
            dve.wait_ge(qm_zeroed, 1)
            dve.wait_ge(xq_loaded, 16)
            for dt in range(2):
                last = nc.vector.tensor_copy(
                    qmask[:, dt, ::33].rearrange("p (s h) -> p s h", h=HEADS),
                    xq[:, dt::2, TP:TN].rearrange("p h s -> p s h"))
            last.then_inc(qm_ready, 1)
            dve.wait_ge(kc_used, TS)
            nc.vector.tensor_reduce(small[0:32, 4:5], psum[0:32, 7, 0:MEM], AX.X, ALU.max, negate=True)
            dve.drain()
            nc.vector.tensor_scalar(small[0:32, 0:1], small[0:32, 4:5], 1.0 / 16, None, ALU.mult).then_inc(att_max, 1)
            for g in range(8):
                dve.wait_ge(kv_turned, g + 1)
                nc.vector.tensor_copy(kvtok[:, g % 2, 512 * (g // 2):512 * (g // 2 + 1)],
                                      psum[:, 4 + g % 2, :]).then_inc(kv_tok, 1)
            dve.wait_ge(att_exp, 1)
            nc.vector.reciprocal(small[0:32, 8:9], small[0:32, 8:9])
            dve.drain()
            nc.vector.tensor_scalar(prob_s[:], prob_s[:], small[0:32, 8:9], None, ALU.mult).then_inc(att_prob, 1)

            def maxima(h):
                c = 16 + 16 * (h % 2)
                dve.wait_ge(att_scores, h + 1)
                nc.vector.tensor_reduce(small[:, c + 4:c + 8],
                                        psum[:, 2 * (h % 2):2 * (h % 2) + 2, :].rearrange("p b (u m) -> p (b u) m", m=MEM),
                                        AX.X, ALU.max, negate=True)
                dve.drain()
                nc.vector.tensor_scalar(small[:, c:c + 4], small[:, c + 4:c + 8], 1.0 / 16, None,
                                        ALU.mult).then_inc(att_max, 1)

            def divide(h):
                c = 16 + 16 * (h % 2)
                dve.wait_ge(att_exp, h + 2)
                nc.vector.reciprocal(small[:, c + 8:c + 12], small[:, c + 8:c + 12])
                dve.drain()
                nc.vector.tensor_tensor(prob[:, h % 2], prob[:, h % 2],
                                        small[:, c + 8:c + 12].unsqueeze(2).to_broadcast([P, 4, MEM]),
                                        ALU.mult).then_inc(att_prob, 1)

            maxima(0)
            maxima(1)
            divide(0)
            divide(1)
            dve.wait_ge(br_hi, 1)
            nc.vector.tensor_tensor(br2[:, 1, :, TP:TN], psum[:, 7, 0:64].rearrange("p (f s) -> p f s", f=8),
                                    br2[:, 0, :, TP:TN], ALU.subtract).then_inc(br_lo, 1)
            for h in range(HEADS):
                if h + 2 < HEADS:
                    maxima(h + 2)
                    divide(h + 2)
                dve.wait_ge(br_hi, h + 2)
                nc.vector.tensor_tensor(br2[:, 1, 2 * h:2 * h + 2, 0:TP], psum[:, 6:8, :],
                                        br2[:, 0, 2 * h:2 * h + 2, 0:TP], ALU.subtract).then_inc(br_lo, 1)

        def merge_loop(eng, n0, n1, body):
            wide = n0 >= N_BA
            with eng.Fori(0, (n1 - n0) // 2) as i:
                for b in range(2):
                    n = n0 + b
                    if wide:
                        m = n + 16
                        o = [(i * 2 + m, m % 2, 0, i * 2 + b, i + (m - N_BC) // 2)]
                    else:
                        m = 2 * n - N_BC
                        o = [(i * 4 + m + j, (m + j) % 2, j * 1024, i * 4 + 2 * b + j, i * 2 + (m + j - N_BC) // 2)
                             for j in range(2)]
                    body(i * 2 + n, n % 2, i + (n - n % 2) // 2, o)

        def sp_merge(sp, n0, n1, gates=True):
            def body(n, slot, u, outs_):
                load_block(sp, n + 2, slot)
                for m, pair, _, _, _ in outs_:
                    sp.wait_ge(evac_done, m + 1)
                    if gates:
                        load_gate(sp, m + 2, pair)
            merge_loop(sp, n0, n1, body)

        def act_merge(act, n0, n1):
            def body(n, slot, u, outs_):
                split_hi(act, n + 1, 1 - slot, u + 1 + slot, outs_[0][0])
            merge_loop(act, n0, n1, body)

        def dve_merge(dve, n0, n1, first):
            def body(n, slot, u, outs_):
                split_lo(dve, n + 1, 1 - slot)
                for m, pair, _, j, use in outs_:
                    dve.wait_ge(out_ready, m + 1)
                    dve.wait_ge(gate_landed[pair], (use + 1) * 16)
                    at = merged[:, bass.ds(j, 1), :].rearrange("p a t -> p (a t)")
                    dst = at if first else zst[:, pair, :]
                    nc.vector.tensor_tensor(in_halves(dst), pair_of(pair), in_halves(gt[:, pair, :]),
                                            ALU.mult).then_inc(evac_done, 1)
                    if not first:
                        dve.drain()
                        nc.vector.tensor_tensor(at, at, zst[:, pair, :], ALU.add)
            merge_loop(dve, n0, n1, body)

        def pe_merge(pe, n0, n1, acts, kts):
            def body(n, slot, u, outs_):
                pe.wait_ge(hi_ready, n + 1)
                pe.wait_ge(lo_ready, n + 1)
                for m, pair, w0, _, _ in outs_:
                    pe.wait_ge(evac_done, m - 1)
                    products(pe, slot, acts, kts, w0, pair, HALF).then_inc(out_ready, 1)
            merge_loop(pe, n0, n1, body)

        def sp_phase0(sp):
            sp.dma_start(memx[:], ins["memT"]).then_inc(mem_loaded, 16)
            sp.dma_start(pcols[:], ins["pcols"]).then_inc(const_loaded, 16)
            load_block(sp, 0, 0)
            load_block(sp, 1, 1)
            sp.dma_start(hx[:], ins["xT"]).then_inc(x_loaded, 16)

        def sp_project(sp):
            for n0, n1, func, ntok in PLAIN:
                def body(n, slot, u, ntok=ntok):
                    load_block(sp, n + 2, slot)
                    sp.wait_ge(evac_done, n + 1)
                    dst = z[bass.ds(n, 1), :, 0:ntok].rearrange("a p t -> (a p) t")
                    sp.dma_start(dst, zst[:, slot, 0:ntok]).then_inc(z_stored[slot], 16)
                seg_loop(sp, n0, n1, body)

        def act_phase0(act):
            act.wait_ge(mem_loaded, 16)
            nc.scalar.activation(sqm[:], memx[:], ACT.Square).then_inc(squares_ready, 1)
            split_hi(act, 0, 0, 1, 0)
            act.wait_ge(root_in, 1)
            nc.scalar.activation(rstd[:, 0:MEM], ssum[:, 0:MEM], ACT.Sqrt).then_inc(root_out, 1)
            act.wait_ge(normed, 1)
            nc.scalar.activation(memr[:, 0], memx[:], ACT.Copy).then_inc(act_hi, 1)

        def act_norm_x(act, n):
            if n == 0:
                act.wait_ge(x_loaded, 16)
            if n < 4:
                nc.scalar.activation(sqx[:, 4 * n:4 * n + 4, :], hx[:, 4 * n:4 * n + 4, :], ACT.Square).then_inc(squares_ready, 1)
            if n == 6:
                act.wait_ge(root_in, 2)
                nc.scalar.activation(rstd[:], ssum[:], ACT.Sqrt).then_inc(root_out, 1)
            if 8 <= n < 12:
                act.wait_ge(normed, 2 + n - 8)
                q = slice(4 * (n - 8), 4 * (n - 8) + 4)
                nc.scalar.activation(actr[:, 0, q, :], hx[:, q, :], ACT.Copy).then_inc(act_hi, 1)

        def act_project(act):
            for n0, n1, func, ntok in PLAIN:
                def body(n, slot, u, func=func, ntok=ntok, n0=n0):
                    split_hi(act, n + 1, 1 - slot, u + 1 + slot, n)
                    if func == ACT.Sigmoid:
                        nc.scalar.activation(bcur[:, slot:slot + 1], pcols[:, bass.ds(n + (C_BG - N_G), 1)], ACT.Copy)
                        act.drain()
                    act.wait_ge(out_ready, n + 1)
                    if not isinstance(n, int) or n >= 2:
                        act.wait_ge(z_stored[slot], u * 16)
                    if ntok == MEM:
                        o, i = zst[:, slot, 0:MEM], psum[:, 2 * slot, 0:MEM]
                    else:
                        o, i = in_halves(zst[:, slot, :]), pair_of(slot)
                    bias = bcur[:, slot:slot + 1] if func == ACT.Sigmoid else 0.0
                    nc.scalar.activation(o, i, func, bias=bias).then_inc(evac_done, 1)
                    if n0 == 0:
                        act_norm_x(act, n)
                if n0 == 0:
                    for n in range(n1):
                        body(n, n % 2, n // 2)
                else:
                    seg_loop(act, n0, n1, body)

        def dve_phase0(dve):
            nc.vector.memset(ones[:], 1.0).then_inc(const_made, 1)
            split_lo(dve, 0, 0)
            dve.wait_ge(const_loaded, 16)
            dve.wait_ge(squares_ready, 1)
            nc.vector.tensor_reduce(ssum[:, 0:MEM], sqm[:].rearrange("p k t -> p t k"), AX.X, ALU.add).then_inc(sums_ready, 1)
            dve.wait_ge(spread_ready, 1)
            nc.vector.tensor_scalar(ssum[:, 0:MEM], psum[:, 4, 0:MEM], 1.0 / D, EPS, ALU.mult, ALU.add).then_inc(root_in, 1)
            dve.wait_ge(root_out, 1)
            nc.vector.reciprocal(rstd[:, 0:MEM], rstd[:, 0:MEM])
            dve.drain()
            for kt in range(KT):
                scale_tile(memx, kt, C_MEM, MEM)
            dve.drain().then_inc(normed, 1)
            dve.wait_ge(act_hi, 1)
            nc.vector.tensor_tensor(memr[:, 1], memx[:], memr[:, 0], ALU.subtract).then_inc(act_lo, 1)

        def scale_tile(src, kt, gain, n):
            nc.vector.scalar_tensor_tensor(out=src[:, kt, :], in0=src[:, kt, :], scalar=pcols[:, gain + kt:gain + kt + 1],
                                           in1=rstd[:, 0:n], op0=ALU.mult, op1=ALU.mult)

        def dve_norm_x(dve, n):
            if n in (4, 5):
                dve.wait_ge(squares_ready, 5)
                t = slice((n - 4) * HALF, (n - 3) * HALF)
                nc.vector.tensor_reduce(ssum[:, t], sqx[:, :, t].rearrange("p k t -> p t k"), AX.X, ALU.add).then_inc(sums_ready, 1)
            if n == 6:
                dve.wait_ge(spread_ready, 2)
                nc.vector.tensor_scalar(in_halves(ssum[:]), pair_of(2), 1.0 / D, EPS, ALU.mult, ALU.add).then_inc(root_in, 1)
            if n == 7:
                dve.wait_ge(root_out, 2)
                nc.vector.reciprocal(rstd[:], rstd[:])
                dve.drain()
                dve.wait_ge(act_lo, 1)
            if 8 <= n < 12:
                for kt in range(4 * (n - 8), 4 * (n - 8) + 4):
                    scale_tile(hx, kt, C_MIX, TN)
                dve.drain().then_inc(normed, 1)
            if 9 <= n < 13:
                q = slice(4 * (n - 9), 4 * (n - 9) + 4)
                dve.wait_ge(act_hi, 2 + n - 9)
                nc.vector.tensor_tensor(actr[:, 1, q, :], hx[:, q, :], actr[:, 0, q, :], ALU.subtract).then_inc(act_lo, 1)

        def dve_project(dve):
            for n0, n1, func, ntok in PLAIN:
                if n0 == 0:
                    for n in range(n1):
                        split_lo(dve, n + 1, 1 - n % 2)
                        dve_norm_x(dve, n)
                else:
                    seg_loop(dve, n0, n1, lambda n, slot, u: split_lo(dve, n + 1, 1 - slot))

        def pe_phase0(pe):
            pe.wait_ge(const_made, 3)
            pe.wait_ge(sums_ready, 1)
            nc.tensor.matmul(psum[:, 4, 0:MEM], ones[:], ssum[:, 0:MEM], start=True, stop=True).then_inc(spread_ready, 1)
            pe.wait_ge(act_hi, 1)
            pe.wait_ge(act_lo, 1)

        def pe_spread(pe, reduced):
            pe.wait_ge(sums_ready, reduced)
            for half in range(2):
                last = nc.tensor.matmul(psum[:, 4 + half, 0:HALF], ones[:], ssum[:, half * HALF:(half + 1) * HALF],
                                        start=True, stop=True)
            last.then_inc(spread_ready, 1)

        def pe_project(pe):
            for n0, n1, func, ntok in PLAIN:
                def body(n, slot, u, ntok=ntok):
                    pe.wait_ge(hi_ready, n + 1)
                    pe.wait_ge(lo_ready, n + 1)
                    if not isinstance(n, int) or n >= 2:
                        pe.wait_ge(evac_done, n - 1)
                    if ntok == MEM:
                        products(pe, slot, memr, range(KT), 0, slot, MEM, 1).then_inc(out_ready, 1)
                    else:
                        products(pe, slot, actr, range(KT), 0, slot, HALF).then_inc(out_ready, 1)
                if n0 == 0:
                    seg_loop(pe, 0, 6, body)
                    pe_spread(pe, 3)
                    seg_loop(pe, 6, N_XQ, body)
                    continue
                if n0 == N_XQ:
                    pe.wait_ge(act_hi, 5)
                    pe.wait_ge(act_lo, 5)
                seg_loop(pe, n0, n1, body)

        def unit(u):
            return (CH, slice(u * CH, (u + 1) * CH)) if u < NCH else (TS, slice(TP, TN))

        def sp_spatial(sp):
            sp.wait_ge(att_out, HEADS)
            sp.wait_ge(out_stored, 64)
            sp.dma_start(gv[:], z[N_GV:N_R].rearrange("n p t -> p n t")).then_inc(gv_loaded, 16)
            sp.dma_start(gu[:], z[N_GU:N_GV].rearrange("n p t -> p n t")).then_inc(gu_loaded, 16)
            sp.dma_start(lnrow[:, 0, :], ins["ln_g"].partition_broadcast(P)).then_inc(sp_loaded, 16)
            sp.dma_start(lnrow[:, 1, :], ins["ln_b"].partition_broadcast(P)).then_inc(sp_loaded, 16)
            sp.dma_start(wspat[:], ins["w_spatT"]).then_inc(sp_loaded, 16)
            sp.dma_start(bspat[:], ins["b_spat"]).then_inc(sp_loaded, 16)
            sp.dma_start(wfirst[:], ins["w_first"].partition_broadcast(TS)).then_inc(sp_loaded, 16)
            sp.wait_ge(sp_vn, 5)
            sp.dma_start(outs["gmlp_v"], vn[0:TS, 0, :]).then_inc(vn_stored, 16)

        def pool_spatial(pool):
            pool.wait_ge(sp_loaded, 80)
            nc.gpsimd.affine_select(out=wspat[:], in_=wspat[:], pattern=[[0, HEADS], [1, CH]], compare_op=ALU.is_ge,
                                    fill=0.0, base=0, channel_multiplier=-1).then_inc(sp_masked, 1)

        def pe_spatial(pe):
            pe.wait_ge(evac_done, outputs_before(N_BB))
            pe.wait_ge(gv_loaded, 16)

            def turn(u):
                rows, tok = unit(u)
                if u >= 2:
                    pe.wait_ge(sp_vn, u - 1)
                for f in range(8):
                    last = nc.tensor.transpose(psum[0:rows, 2 * (u % 2) + f // 4, (f % 4) * P:(f % 4 + 1) * P],
                                               gv[:, f, tok], ident[:])
                last.then_inc(sp_turned, 1)

            def mix(u):
                rows, tok = unit(u)
                pe.wait_ge(sp_vn, u + 1)
                if u >= 2:
                    pe.wait_ge(sp_gated, u - 1)
                for f in range(8):
                    g = f // 2
                    at = psum[:, 4 + 2 * (u % 2) + f // 4, (f % 4) * P:(f % 4) * P + rows]
                    w = wspat[:, g, :] if u < NCH else wdiag[:, g, :]
                    b = bspat[0:1, g * CH:(g + 1) * CH] if u < NCH else bfirst[0:1, g, :]
                    nc.tensor.matmul(at, vn[0:rows, u % 2, f * P:(f + 1) * P], w, start=True, stop=False)
                    last = nc.tensor.matmul(at, ones[0:1, :], b, start=False, stop=True)
                last.then_inc(sp_mixed, 1)

            turn(0)
            turn(1)
            pe.wait_ge(sp_masked, 2)
            for u in range(NCH + 1):
                mix(u)
                if u + 2 <= NCH:
                    turn(u + 2)

        def act_spatial(act):
            for u in range(NCH + 1):
                rows, tok = unit(u)
                act.wait_ge(sp_var, u + 1)
                nc.scalar.activation(small[0:rows, 14:15], small[0:rows, 13:14], ACT.Sqrt).then_inc(sp_root, 1)
                if u >= 1:
                    gated_hi(act, u - 1)
            gated_hi(act, NCH)

        def gated_hi(act, u):
            rows, tok = unit(u)
            act.wait_ge(sp_gated, u + 1)
            act.wait_ge(out_ready, outputs_before(N_BB))
            nc.scalar.activation(br2[:, 0, :, tok], gated[:, u % 2, :, 0:rows], ACT.Copy).then_inc(br_hi, 1)

        def dve_spatial(dve):
            dve.wait_ge(sp_loaded, 80)
            nc.vector.tensor_tensor(wdiag[:], ident[0:TS, 0:TS].unsqueeze(1).to_broadcast([TS, HEADS, TS]),
                                    wfirst[:].unsqueeze(2).to_broadcast([TS, HEADS, TS]), ALU.mult)
            nc.vector.tensor_copy(bfirst[:], bspat[:].rearrange("a (g t) -> a g t", t=CH)[:, :, 0:1]
                                  .to_broadcast([1, HEADS, TS]))
            dve.drain().then_inc(sp_masked, 1)

            def norm(u):
                rows, tok = unit(u)
                dve.wait_ge(sp_turned, u + 1)
                src = psum[0:rows, 2 * (u % 2):2 * (u % 2) + 2, :]
                for b in range(2):
                    nc.vector.bn_stats(small[0:rows, 6 * b:6 * b + 6], src[:, b, :])
                dve.drain()
                nc.vector.bn_aggr(small[0:rows, 12:14], small[0:rows, 0:12])
                dve.drain()
                nc.vector.tensor_scalar(small[0:rows, 13:14], small[0:rows, 13:14], EPS, None, ALU.add).then_inc(sp_var, 1)
                dve.wait_ge(sp_root, u + 1)
                nc.vector.reciprocal(small[0:rows, 15:16], small[0:rows, 14:15])
                dve.drain()
                if u >= 2:
                    dve.wait_ge(sp_mixed, u - 1)
                v = vn[0:rows, u % 2, :]
                nc.vector.tensor_scalar(v.rearrange("p (b f) -> p b f", b=2), src, small[0:rows, 12:13], small[0:rows, 15:16],
                                        ALU.subtract, ALU.mult)
                dve.drain()
                nc.vector.tensor_tensor(v, v, lnrow[0:rows, 0, :], ALU.mult)
                dve.drain()
                nc.vector.tensor_tensor(v, v, lnrow[0:rows, 1, :], ALU.add).then_inc(sp_vn, 1)

            def gate(u):
                rows, tok = unit(u)
                dve.wait_ge(sp_mixed, u + 1)
                if u >= 2:
                    dve.wait_ge(br_hi, 5 + u - 1)
                src = psum[:, 4 + 2 * (u % 2):6 + 2 * (u % 2), :].rearrange("p b (f t) -> p (b f) t", t=P)
                nc.vector.tensor_tensor(gated[:, u % 2, :, 0:rows], src[:, :, 0:rows], gu[:, :, tok],
                                        ALU.mult).then_inc(sp_gated, 1)

            def gated_lo(u):
                rows, tok = unit(u)
                dve.wait_ge(br_hi, 5 + u + 1)
                nc.vector.tensor_tensor(br2[:, 1, :, tok], gated[:, u % 2, :, 0:rows], br2[:, 0, :, tok],
                                        ALU.subtract).then_inc(br_lo, 1)

            dve.wait_ge(gu_loaded, 16)
            norm(0)
            for u in range(NCH + 1):
                if u < NCH:
                    norm(u + 1)
                if u >= 1:
                    gated_lo(u - 1)
                gate(u)
            gated_lo(NCH)

        def rows_of(i):
            return (32, 64, 128, 128)[i]

        def sp_gla(sp):
            sp.wait_ge(out_ready, outputs_before(N_BA))
            sp.wait_ge(vn_stored, 16)
            sp.dma_start(low[:], z[N_LOW, 0:RANK, :]).then_inc(low_loaded, 16)
            sp.dma_start(w_up[:], ins["w_up"]).then_inc(low_loaded, 16)
            for c in range(NCH):
                t = slice(c * CH, (c + 1) * CH)
                if c == 0:
                    sp.wait_ge(br_lo, 10)
                else:
                    sp.wait_ge(sub_ready, 4 * c)
                    sp.wait_ge(kd_ready, c)
                    sp.wait_ge(qe_ready, c)
                for dst, n in ((qc, N_Q), (kc, N_K)):
                    sp.dma_start(dst[:], z[n:n + 8, :, t].rearrange("n p t -> p n t")).then_inc(chunk_loaded, 16)
                if c > 0:
                    sp.wait_ge(o_normed, c)
                    sp.dma_start(bra_dram[:, :, (c - 1) * CH:c * CH], rc[:]).then_inc(chunk_stored, 16)
                    sp.wait_ge(chunk_stored, 16 * c)
                for dst, n in ((vc, N_V), (rc, N_R)):
                    sp.dma_start(dst[:], z[n:n + 16, :, t].rearrange("n p t -> p n t")).then_inc(chunk_loaded, 16)
            for dst, n, k in ((qs, N_Q, 8), (ks, N_K, 8), (vs, N_V, 16), (rs, N_R, 16)):
                sp.dma_start(dst[:], z[n:n + k, :, TP:TN].rearrange("n p t -> p n t")).then_inc(samples_loaded, 16)
            sp.wait_ge(o_normed, NCH)
            sp.dma_start(bra_dram[:, :, TP - CH:TP], rc[:]).then_inc(chunk_stored, 16)
            sp.wait_ge(state_done, NCH)
            sp.dma_start(outs["gla_p"].rearrange("h (k p) v -> p (h k) v", p=P), state[:]).then_inc(state_out[0], 16)
            for s in range(TS):
                if s == 1:
                    sp.wait_ge(kd_ready, NCH)
                    sp.wait_ge(sub_ready, 4 * NCH)
                if s != 1:
                    sp.wait_ge(state_out[s % 2], 16 * (s // 2 + 1 - s % 2))
                    if s >= 2:
                        sp.wait_ge(o_ready, NCH + s - 1)
                src = ins["state"][s].rearrange("h (k p) v -> p (h k) v", p=P)
                sp.dma_start(states[s % 2][:], src).then_inc(state_in[s % 2], 16)
                if s >= 1:
                    store_state(sp, s - 1)
            store_state(sp, TS - 1)
            sp.wait_ge(o_normed, NCH + 1)
            sp.dma_start(bra_dram[:, :, TP:TN], rs[:]).then_inc(chunk_stored, 16)
            sp.wait_ge(chunk_stored, 16 * (NCH + 1))
            sp.dma_start(bra[:], bra_dram[:]).then_inc(bra_loaded, 16)

        def store_state(sp, s):
            sp.wait_ge(state_done, NCH + s + 1)
            dst = outs["gla_s"][s].rearrange("h (k p) v -> p (h k) v", p=P)
            sp.dma_start(dst, states[s % 2][:]).then_inc(state_out[s % 2], 16)

        def pool_gla(pool):
            pool.wait_ge(br_lo, 10)
            nc.gpsimd.memset(keep[:], 1.0)
            pool.drain()
            nc.gpsimd.memset(keep[:].rearrange("p (c t) -> p c t", t=CH)[:, :, 0:1], 0.0).then_inc(keep_made, 1)

        def pe_gla(pe):
            pe.wait_ge(evac_done, outputs_before(N_BA))
            pe.wait_ge(low_loaded, 32)
            for f in range(8):
                if f >= 4:
                    pe.wait_ge(up_read, f - 3)
                for half in range(2):
                    last = nc.tensor.matmul(psum[:, 2 * (f % 4) + half, 0:HALF], w_up[:, f * P:(f + 1) * P],
                                            low[:, half * HALF:(half + 1) * HALF], start=True, stop=True)
                last.then_inc(up_ready, 1)
            pe.wait_ge(up_read, 8)
            for c in range(NCH):
                pe.wait_ge(chunk_loaded, 64 * (c + 1))
                if c > 0:
                    pe.wait_ge(o_read, c)
                for f in range(KT):
                    last = nc.tensor.transpose(psum[:, f // 4, (f % 4) * P:(f % 4 + 1) * P], vc[:, f, :], ident[:])
                last.then_inc(v_turned, 1)
                for i in range(4):
                    rows = rows_of(i)
                    pe.wait_ge(sub_ready, 4 * c + i + 1)
                    if i == 0 and c > 0:
                        pe.wait_ge(sc_ready, c)
                    for h in range(HEADS):
                        for dt in range(2):
                            last = nc.tensor.matmul(psum[0:rows, 4, h * CH + i * SUB:h * CH + (i + 1) * SUB],
                                                    ki[:, i % 2, 2 * h + dt, 0:rows], qi[:, i % 2, 2 * h + dt, :],
                                                    start=(dt == 0), stop=(dt == 1))
                    last.then_inc(sub_scored, 1)
                pe.wait_ge(kd_ready, c + 1)
                if c > 0:
                    pe.wait_ge(state_done, c)
                for f in range(8):
                    last = nc.tensor.transpose(psum[:, 5 + f // 4, (f % 4) * P:(f % 4 + 1) * P], kd[:, f, :], ident[:])
                last.then_inc(kd_turned, 1)
                pe.wait_ge(v_tok, c + 1)
                pe.wait_ge(sc_ready, c + 1)
                pe.wait_ge(qe_ready, c + 1)
                for h in range(HEADS):
                    for j in range(4):
                        at = psum[:, h, j * P:(j + 1) * P]
                        last = nc.tensor.matmul(at, vtok[:, h * DV + j * P:h * DV + (j + 1) * P], scores_t[:, h, :],
                                                start=True, stop=(c == 0))
                        if c > 0:
                            for dt in range(2):
                                last = nc.tensor.matmul(at, state[:, 2 * h + dt, j * P:(j + 1) * P],
                                                        qe[:, 2 * h + dt, :], start=False, stop=(dt == 1))
                last.then_inc(o_ready, 1)
                pe.wait_ge(kd_tok, c + 1)
                for f in range(8):
                    if f >= 2:
                        pe.wait_ge(kv_read, 8 * c + f - 1)
                    nc.tensor.matmul(psum[:, 5 + f % 2, :], kdtok[:, f * P:(f + 1) * P],
                                     vtok[:, (f // 2) * DV:(f // 2 + 1) * DV], start=True, stop=True).then_inc(kv_ready, 1)
                pe.wait_ge(o_squared, c + 1)
                for h in range(HEADS):
                    for j in range(4):
                        last = nc.tensor.matmul(psum[:, 7, h * CH:(h + 1) * CH], ones[:], vc[:, 4 * h + j, :],
                                                start=(j == 0), stop=(j == 3))
                last.then_inc(o_summed, 1)
            pe.wait_ge(samples_loaded, 64)
            pe.wait_ge(state_done, NCH)
            pe.wait_ge(o_read, NCH)
            for f in range(8):
                nc.tensor.transpose(psum[0:TS, f // 4, (f % 4) * P:(f % 4 + 1) * P], ks[:, f, :], ident[:])
            for f in range(KT):
                last = nc.tensor.transpose(psum[0:TS, 2 + f // 4, (f % 4) * P:(f % 4 + 1) * P], vs[:, f, :], ident[:])
            last.then_inc(v_turned, 1)
            pe.wait_ge(v_tok, NCH + 1)
            for s in range(TS):
                pe.wait_ge(one_ready, s + 1)
                for f in range(8):
                    n = s * 8 + f
                    if n >= 4:
                        pe.wait_ge(kv_read, 8 * NCH + n - 3)
                    nc.tensor.matmul(psum[:, f % 4, :], k8one[:, s % 2, f * P:(f + 1) * P],
                                     v8[:, (f // 2) * DV:(f // 2 + 1) * DV], start=True, stop=True).then_inc(kv_ready, 1)
                pe.wait_ge(state_done, NCH + s + 1)
                pe.wait_ge(qe_ready, NCH + 1)
                for h in range(HEADS):
                    for j in range(4):
                        f = 4 * h + j
                        for dt in range(2):
                            last = nc.tensor.matmul(psum[:, 6, f * TS + s:f * TS + s + 1],
                                                    states[s % 2][:, 2 * h + dt, j * P:(j + 1) * P],
                                                    qs[:, 2 * h + dt, s:s + 1], start=(dt == 0), stop=(dt == 1))
                last.then_inc(o_ready, 1)
            pe.wait_ge(o_squared, NCH + 1)
            for h in range(HEADS):
                for j in range(4):
                    last = nc.tensor.matmul(psum[:, 7, h * TS:(h + 1) * TS], ones[:], sqs[:, 4 * h + j, :],
                                            start=(j == 0), stop=(j == 3))
            last.then_inc(o_summed, 1)

        def act_gla(act):
            act.wait_ge(gx_ready, 1)
            nc.scalar.activation(gy[:], gx[:], ACT.Abs)
            act.drain()
            nc.scalar.activation(gy[:], gy[:], ACT.Exp, scale=-1.0)
            act.drain()
            nc.scalar.activation(gy[:], gy[:], ACT.Ln, bias=1.0).then_inc(gy_ready, 1)
            for c in range(NCH):
                t = slice(c * CH, (c + 1) * CH)
                act.wait_ge(bcum_ready, 1)
                if c > 0:
                    act.wait_ge(qe_ready, c)
                    act.wait_ge(state_done, c)
                nc.scalar.activation(eb[:], bcum[:, :, t], ACT.Exp, scale=1.0 / GATE_NORM).then_inc(eb_ready, 1)
                act.wait_ge(v_turned, c + 1)
                if c > 0:
                    act.wait_ge(kv_ready, 8 * c)
                nc.scalar.activation(vtok[:].rearrange("p (b f) -> p b f", b=4), psum[:, 0:4, :], ACT.Copy).then_inc(v_tok, 1)
                for i in range(4):
                    act.wait_ge(sub_in, 4 * c + i + 1)
                    nc.scalar.activation(qi[:, i % 2], qi[:, i % 2], ACT.Exp, scale=1.0 / GATE_NORM)
                    nc.scalar.activation(ki[:, i % 2, :, 0:rows_of(i)], ki[:, i % 2, :, 0:rows_of(i)], ACT.Exp,
                                         scale=1.0 / GATE_NORM).then_inc(sub_exp, 1)
                act.wait_ge(kd_in, c + 1)
                nc.scalar.activation(kd[:], kd[:], ACT.Exp, scale=1.0 / GATE_NORM).then_inc(kd_exp, 1)
                act.wait_ge(kd_turned, c + 1)
                nc.scalar.activation(kdtok[:].rearrange("p (b f) -> p b f", b=2), psum[:, 5:7, :], ACT.Copy).then_inc(kd_tok, 1)
                act.wait_ge(o_ready, c + 1)
                nc.scalar.activation(vc[:].rearrange("p (h j) t -> p h (j t)", h=4), psum[:, 0:4, :],
                                     ACT.Square).then_inc(o_squared, 1)
                act.wait_ge(o_var, c + 1)
                nc.scalar.activation(norm_a[:], norm_a[:], ACT.Sqrt).then_inc(o_root, 1)
            act.wait_ge(v_turned, NCH + 1)
            nc.scalar.activation(k8[:].rearrange("p (b f) -> p b f", b=2), psum[0:TS, 0:2, :], ACT.Copy)
            nc.scalar.activation(v8[:].rearrange("p (b f) -> p b f", b=4), psum[0:TS, 2:6, :], ACT.Copy).then_inc(v_tok, 1)
            nc.scalar.activation(es[:], bcum[:, :, TP:TN], ACT.Exp, scale=1.0 / GATE_NORM).then_inc(eb_ready, 1)
            act.wait_ge(o_ready, NCH + TS)
            nc.scalar.activation(sqs[:], psum[:, 6, 0:KT * TS].rearrange("p (f s) -> p f s", f=KT),
                                 ACT.Square).then_inc(o_squared, 1)
            act.wait_ge(o_var, NCH + 1)
            nc.scalar.activation(norm_s[:], norm_s[:], ACT.Sqrt).then_inc(o_root, 1)

        def dve_gla(dve):
            for f in range(8):
                dve.wait_ge(up_ready, f + 1)
                nc.vector.tensor_scalar(in_halves(gx[:, f, :]), pair_of(f % 4), pcols[:, C_BA + f:C_BA + f + 1], None,
                                        ALU.add).then_inc(up_read, 1)
            dve.drain().then_inc(gx_ready, 1)
            dve.wait_ge(gy_ready, 1)
            nc.vector.scalar_tensor_tensor(out=gx[:], in0=gx[:], scalar=0.0, in1=gy[:], op0=ALU.min, op1=ALU.subtract)
            dve.drain()
            dve.wait_ge(keep_made, 1)
            for f in range(8):
                nc.vector.tensor_tensor_scan(bcum[:, f, 0:TP], keep[:], gx[:, f, 0:TP], 0.0, ALU.mult, ALU.add)
            nc.vector.tensor_copy(bcum[:, :, TP:TN], gx[:, :, TP:TN])
            dve.drain().then_inc(bcum_ready, 1)
            nc.vector.memset(scores_t[:], 0.0)
            dve.drain()
            for c in range(NCH):
                t0 = c * CH
                b = bcum[:, :, t0:t0 + CH]
                dve.wait_ge(chunk_loaded, 64 * (c + 1))

                def sub_exponents(i):
                    rows = rows_of(i)
                    mid = bcum[:, :, t0 + i * SUB + SUB // 2 - 1:t0 + i * SUB + SUB // 2]
                    if 4 * c + i >= 2:
                        dve.wait_ge(sub_scored, 4 * c + i - 1)
                    nc.vector.tensor_tensor(qi[:, i % 2], bcum[:, :, t0 + i * SUB:t0 + (i + 1) * SUB],
                                            mid.to_broadcast([P, 8, SUB]), ALU.subtract)
                    nc.vector.tensor_tensor(ki[:, i % 2, :, 0:rows], mid.to_broadcast([P, 8, rows]),
                                            bcum[:, :, t0:t0 + rows], ALU.subtract)
                    dve.drain()
                    nc.vector.tensor_scalar(qi[:, i % 2], qi[:, i % 2], CLAMP, None, ALU.min)
                    nc.vector.tensor_scalar(ki[:, i % 2, :, 0:rows], ki[:, i % 2, :, 0:rows], CLAMP, None, ALU.min)
                    dve.drain().then_inc(sub_in, 1)

                def sub_products(i):
                    rows = rows_of(i)
                    dve.wait_ge(sub_exp, 4 * c + i + 1)
                    nc.vector.scalar_tensor_tensor(out=qi[:, i % 2], in0=qc[:, :, i * SUB:(i + 1) * SUB], scalar=DK ** -0.5,
                                                   in1=qi[:, i % 2], op0=ALU.mult, op1=ALU.mult)
                    nc.vector.tensor_tensor(ki[:, i % 2, :, 0:rows], ki[:, i % 2, :, 0:rows], kc[:, :, 0:rows], ALU.mult)
                    dve.drain().then_inc(sub_ready, 1)

                sub_exponents(0)
                sub_exponents(1)
                dve.wait_ge(eb_ready, c + 1)
                if c > 0:
                    dve.wait_ge(o_ready, c)
                nc.vector.scalar_tensor_tensor(out=qe[:], in0=qc[:], scalar=DK ** -0.5, in1=eb[:], op0=ALU.mult,
                                               op1=ALU.mult).then_inc(qe_ready, 1)
                sub_products(0)
                if c > 0:
                    dve.wait_ge(kd_turned, c)
                nc.vector.tensor_tensor(kd[:], b[:, :, CH - 1:CH].to_broadcast([P, 8, CH]), b,
                                        ALU.subtract).then_inc(kd_in, 1)
                sub_exponents(2)
                sub_products(1)
                sub_exponents(3)
                sub_products(2)
                sub_products(3)
                dve.wait_ge(kd_exp, c + 1)
                nc.vector.tensor_tensor(kd[:], kd[:], kc[:], ALU.mult).then_inc(kd_ready, 1)
                nc.vector.tensor_tensor(rc[:], rc[:], pcols[:, C_GLA:C_GLA + KT].unsqueeze(2).to_broadcast([P, KT, CH]), ALU.mult)
                dve.wait_ge(sub_scored, 4 * c + 4)
                if c > 0:
                    dve.wait_ge(o_ready, c)
                for i in range(4):
                    rows = rows_of(i)
                    sl = slice(i * SUB, (i + 1) * SUB)
                    nc.vector.tensor_tensor(scores_t[0:rows, :, sl],
                                            psum[0:rows, 4, :].rearrange("p (h t) -> p h t", h=HEADS)[:, :, sl],
                                            tri[0:rows, sl].unsqueeze(1).to_broadcast([rows, HEADS, SUB]), ALU.mult)
                dve.drain().then_inc(sc_ready, 1)
                dve.wait_ge(o_ready, c + 1)
                for f in range(8):
                    dve.wait_ge(kv_ready, 8 * c + f + 1)
                    if c == 0:
                        nc.vector.tensor_copy(state[:, f, :], psum[:, 5 + f % 2, :]).then_inc(kv_read, 1)
                    else:
                        nc.vector.scalar_tensor_tensor(out=state[:, f, :], in0=state[:, f, :], scalar=eb[:, f, CH - 1:CH],
                                                       in1=psum[:, 5 + f % 2, :], op0=ALU.mult, op1=ALU.add).then_inc(kv_read, 1)
                dve.drain().then_inc(state_done, 1)
                dve.wait_ge(o_summed, c + 1)
                nc.vector.tensor_scalar(norm_a[:], psum[:, 7, :].rearrange("p (h t) -> p h t", h=HEADS), 1.0 / DV, EPS,
                                        ALU.mult, ALU.add).then_inc(o_var, 1)
                dve.wait_ge(o_root, c + 1)
                nc.vector.reciprocal(norm_a[:], norm_a[:])
                dve.drain()
                v4 = vc[:].rearrange("p (h j) t -> p h j t", h=HEADS)
                nc.vector.tensor_tensor(v4, psum[:, 0:4, :].rearrange("p h (j t) -> p h j t", j=4),
                                        norm_a[:].unsqueeze(2).to_broadcast([P, HEADS, 4, CH]), ALU.mult).then_inc(o_read, 1)
                dve.drain()
                nc.vector.tensor_tensor(rc[:], rc[:], vc[:], ALU.mult).then_inc(o_normed, 1)
            dve.wait_ge(samples_loaded, 64)
            nc.vector.tensor_scalar(qs[:], qs[:], DK ** -0.5, None, ALU.mult).then_inc(qe_ready, 1)
            nc.vector.tensor_tensor(rs[:], rs[:], pcols[:, C_GLA:C_GLA + KT].unsqueeze(2).to_broadcast([P, KT, TS]), ALU.mult)
            dve.wait_ge(v_tok, NCH + 1)
            dve.wait_ge(eb_ready, NCH + 1)

            def one(s):
                if s >= 2:
                    dve.wait_ge(kv_ready, 8 * NCH + 8 * (s - 1))
                nc.vector.tensor_scalar(k8one[:, s % 2, :], k8[:], ident[0:TS, s:s + 1], None, ALU.mult).then_inc(one_ready, 1)

            one(0)
            for s in range(TS):
                if s + 1 < TS:
                    one(s + 1)
                dve.wait_ge(state_in[s % 2], 16 * (s // 2 + 1))
                st = states[s % 2]
                for f in range(8):
                    dve.wait_ge(kv_ready, 8 * NCH + 8 * s + f + 1)
                    nc.vector.scalar_tensor_tensor(out=st[:, f, :], in0=st[:, f, :], scalar=es[:, f, s:s + 1],
                                                   in1=psum[:, f % 4, :], op0=ALU.mult, op1=ALU.add).then_inc(kv_read, 1)
                dve.drain().then_inc(state_done, 1)
            dve.wait_ge(o_summed, NCH + 1)
            nc.vector.tensor_scalar(norm_s[:], psum[:, 7, 0:HEADS * TS].rearrange("p (h t) -> p h t", h=HEADS), 1.0 / DV, EPS,
                                    ALU.mult, ALU.add).then_inc(o_var, 1)
            dve.wait_ge(o_root, NCH + 1)
            nc.vector.reciprocal(norm_s[:], norm_s[:])
            dve.drain()
            nc.vector.tensor_tensor(sqs[:].rearrange("p (h j) s -> p h j s", h=HEADS),
                                    psum[:, 6, 0:KT * TS].rearrange("p (h j s) -> p h j s", h=HEADS, j=4),
                                    norm_s[:].unsqueeze(2).to_broadcast([P, HEADS, 4, TS]), ALU.mult).then_inc(o_read, 1)
            dve.drain()
            nc.vector.tensor_tensor(rs[:], rs[:], sqs[:], ALU.mult).then_inc(o_normed, 1)

        def act_wide(act, src):
            for q in range(4):
                nc.scalar.activation(actr[:, 0, 4 * q:4 * q + 4, :], src[:, 4 * q:4 * q + 4, :], ACT.Copy).then_inc(act_hi, 1)

        def dve_wide(dve, src, k):
            for q in range(4):
                dve.wait_ge(act_hi, k + q + 1)
                nc.vector.tensor_tensor(actr[:, 1, 4 * q:4 * q + 4, :], src[:, 4 * q:4 * q + 4, :],
                                        actr[:, 0, 4 * q:4 * q + 4, :], ALU.subtract).then_inc(act_lo, 1)

        def wide_loop(eng, n0, n1, body):
            assert n0 % 2 == 1 and (n1 - n0) % 2 == 0
            with eng.Fori(0, (n1 - n0) // 2) as i:
                for b in range(2):
                    n = n0 + b
                    body(i * 2 + n, n % 2, i + (n - n % 2) // 2, i * 2 + n + 16, i * 2 + b)

        def sp_out(sp):
            sp.wait_ge(act_lo, 9)
            sp.dma_start(x1[:], ins["xT"]).then_inc(x1_loaded, 16)
            wide_loop(sp, N_OUT, N_WQ, lambda n, slot, u, m, j: load_block(sp, n + 2, slot))
            for u in range(NCH + 1):
                rows, tok = unit(u)
                sp.wait_ge(x1_staged, u + 1)
                sp.dma_start(x1_dram[tok, :], stage_x[u % 2][0:rows, :]).then_inc(x1_stored[u % 2], 16)
            wide_loop(sp, N_WQ, N_END - 2, lambda n, slot, u, m, j: load_block(sp, n + 2, slot))
            sp.wait_ge(x1_stored[0], 48)
            sp.wait_ge(x1_stored[1], 32)
            sp.dma_start(keys[:], ins["keys"]).then_inc(keys_loaded, 16)
            sp.wait_ge(sc_staged, 1)
            for u in range(NCH + 1):
                sp.wait_ge(sc_staged, u + 1)
                sp.dma_start(sc_dram[u * P:(u + 1) * P, :], stage_s[u % 2][:]).then_inc(sc_stored[u % 2], 16)
            for u in range(NCH + 1):
                rows, tok = unit(u)
                sp.wait_ge(h2_staged, u + 1)
                sp.dma_start(h2_dram[tok, :], stage_h[u % 2][0:rows, :]).then_inc(h2_stored[u % 2], 16)
            for k in range(2):
                sp.wait_ge(sc_stored[k], 16 * (3 - k))
                sp.wait_ge(h2_stored[k], 16 * (3 - k))

        def act_out(act):
            act.wait_ge(merged_ready, 1)
            act.wait_ge(out_ready, N_OUT + 16)
            act_wide(act, merged)
            wide_loop(act, N_OUT, N_WQ, lambda n, slot, u, m, j: split_hi(act, n + 1, 1 - slot, u + 1 + slot, m))
            act.wait_ge(x1_ready, 1)
            for q in range(4):
                nc.scalar.activation(sq2[:, 4 * q:4 * q + 4, :], x1[:, 4 * q:4 * q + 4, :], ACT.Square).then_inc(squares_ready, 1)
            for u in range(NCH + 1):
                rows, tok = unit(u)
                act.wait_ge(x1_turned, u + 1)
                if u >= 2:
                    act.wait_ge(x1_stored[u % 2], 16 * (u // 2))
                nc.scalar.activation(stage_x[u % 2][0:rows, :].rearrange("p (b f) -> p b f", b=4), psum[0:rows, 0:4, :],
                                     ACT.Copy).then_inc(x1_staged, 1)
                if u == 1:
                    act.wait_ge(root_in, 3)
                    nc.scalar.activation(rstd[:], ssum[:], ACT.Sqrt).then_inc(root_out, 1)
            act.wait_ge(out_ready, N_WQ + 16)
            for q in range(4):
                act.wait_ge(normed, 6 + q)
                nc.scalar.activation(actr[:, 0, 4 * q:4 * q + 4, :], h2[:, 4 * q:4 * q + 4, :], ACT.Copy).then_inc(act_hi, 1)
            def evac(slot, m, j):
                act.wait_ge(out_ready, m + 1)
                dst = pq[:, bass.ds(j, 1), :].rearrange("p a t -> p (a t)")
                nc.scalar.activation(in_halves(dst), pair_of(m_pair(slot)), ACT.Copy).then_inc(evac_done, 1)

            def body(n, slot, u, m, j):
                split_hi(act, n + 1, 1 - slot, u + 1 + slot, m)
                evac(slot, m, j)
            wide_loop(act, N_WQ, N_END - 2, body)
            split_hi(act, N_END - 1, (N_END - 1) % 2, (N_END - 1 - (N_END - 1) % 2) // 2 + 1, N_END - 2 + 16)
            evac((N_END - 2) % 2, N_END - 2 + 16, 14)
            evac((N_END - 1) % 2, N_END - 1 + 16, 15)
            act.drain().then_inc(pq_ready, 1)
            for u in range(NCH + 1):
                rows, tok = unit(u)
                act.wait_ge(scored, u + 1)
                if u >= 2:
                    act.wait_ge(sc_stored[u % 2], 16 * (u // 2))
                if u == NCH:
                    act.wait_ge(stage_zero, 1)
                nc.scalar.activation(stage_s[u % 2][0:rows, :].rearrange("p (b f) -> p b f", b=4),
                                     psum[0:rows, 4 * (u % 2):4 * (u % 2) + 4, :], ACT.Copy).then_inc(sc_staged, 1)
            for u in range(NCH + 1):
                rows, tok = unit(u)
                act.wait_ge(h2_turned, u + 1)
                if u >= 2:
                    act.wait_ge(h2_stored[u % 2], 16 * (u // 2))
                nc.scalar.activation(stage_h[u % 2][0:rows, :].rearrange("p (b f) -> p b f", b=4),
                                     psum[0:rows, 4 * ((u + 1) % 2):4 * ((u + 1) % 2) + 4, :], ACT.Copy).then_inc(h2_staged, 1)

        def m_pair(slot):
            return slot

        def dve_out(dve):
            dve_wide(dve, merged, 9)
            dve.wait_ge(x1_loaded, 16)

            def body(n, slot, u, m, j):
                split_lo(dve, n + 1, 1 - slot)
                dve.wait_ge(out_ready, m + 1)
                at = x1[:, bass.ds(j, 1), :].rearrange("p a t -> p (a t)")
                nc.vector.tensor_tensor(in_halves(at), pair_of(m_pair(slot)), in_halves(at), ALU.add).then_inc(evac_done, 1)
            wide_loop(dve, N_OUT, N_WQ, body)
            dve.drain().then_inc(x1_ready, 1)
            dve.wait_ge(squares_ready, 9)
            for b in range(2):
                t = slice(b * HALF, (b + 1) * HALF)
                nc.vector.tensor_reduce(ssum[:, t], sq2[:, :, t].rearrange("p k t -> p t k"), AX.X, ALU.add).then_inc(sums_ready, 1)
            dve.wait_ge(spread_ready, 3)
            nc.vector.tensor_scalar(in_halves(ssum[:]), pair_of(2), 1.0 / D, EPS, ALU.mult, ALU.add).then_inc(root_in, 1)
            dve.wait_ge(root_out, 3)
            nc.vector.reciprocal(rstd[:], rstd[:])
            dve.drain()
            for q in range(4):
                for kt in range(4 * q, 4 * q + 4):
                    nc.vector.scalar_tensor_tensor(out=h2[:, kt, :], in0=x1[:, kt, :], scalar=pcols[:, C_FFN + kt:C_FFN + kt + 1],
                                                   in1=rstd[:], op0=ALU.mult, op1=ALU.mult)
                dve.drain().then_inc(normed, 1)
            dve_wide(dve, h2, 13)
            wide_loop(dve, N_WQ, N_END - 2, lambda n, slot, u, m, j: split_lo(dve, n + 1, 1 - slot))
            split_lo(dve, N_END - 1, (N_END - 1) % 2)
            dve.wait_ge(sc_stored[0], 32)
            nc.vector.memset(stage_s[0][:], 0.0)
            dve.drain().then_inc(stage_zero, 1)

        def pe_out(pe):
            pe.wait_ge(act_hi, 13)
            pe.wait_ge(act_lo, 13)

            def body(n, slot, u, m, j):
                pe.wait_ge(hi_ready, n + 1)
                pe.wait_ge(lo_ready, n + 1)
                pe.wait_ge(evac_done, m - 1)
                products(pe, slot, actr, range(KT), 0, m_pair(slot), HALF).then_inc(out_ready, 1)
            wide_loop(pe, N_OUT, N_WQ, body)
            pe.wait_ge(x1_ready, 1)
            turn_units(pe, x1, 0, x1_turned, x1_staged)
            pe.wait_ge(act_hi, 17)
            pe.wait_ge(act_lo, 17)
            pe.wait_ge(x1_staged, NCH + 1)
            wide_loop(pe, N_WQ, N_END, body)
            pe.wait_ge(keys_loaded, 16)
            pe.wait_ge(pq_ready, 1)
            for u in range(NCH + 1):
                rows, tok = unit(u)
                if u >= 2:
                    pe.wait_ge(sc_staged, u - 1)
                for c in range(KT):
                    last = nc.tensor.matmul(psum[0:rows, 4 * (u % 2) + c // 4, (c % 4) * P:(c % 4 + 1) * P],
                                            pq[:, c, tok], keys[:, c // 2, c % 2, :], start=True, stop=True)
                last.then_inc(scored, 1)
            turn_units(pe, h2, 1, h2_turned, h2_staged)

        def turn_units(pe, src, two, turned, staged):
            for u in range(NCH + 1):
                rows, tok = unit(u)
                b0 = 4 * ((u + 1) % 2) if two else 0
                if two:
                    if u < 2:
                        pe.wait_ge(sc_staged, NCH + u)
                    else:
                        pe.wait_ge(staged, u - 1)
                elif u >= 1:
                    pe.wait_ge(staged, u)
                if u == 1 and not two:
                    pe_spread(pe, 5)
                for f in range(KT):
                    last = nc.tensor.transpose(psum[0:rows, b0 + f // 4, (f % 4) * P:(f % 4 + 1) * P], src[:, f, tok], ident[:])
                last.then_inc(turned, 1)

        def top_head(dve, k, to_idx=True):
            for a in range(2):
                nc.vector.max(top_v[:, a, 0:8], sc[:, k, a, :])
            dve.drain()
            for a in range(2):
                nc.vector.max_index(top_i[:, a, 0:8], top_v[:, a, 0:8], sc[:, k, a, :])
                nc.vector.match_replace(rest[:, a, :], top_v[:, a, 0:8], sc[:, k, a, :], -3.0e38)
            dve.drain()
            for a in range(2):
                nc.vector.max(top_v[:, a, 8:16], rest[:, a, :])
            dve.drain()
            for a in range(2):
                nc.vector.max_index(top_i[:, a, 8:16], top_v[:, a, 8:16], rest[:, a, :])
            nc.vector.tensor_tensor(cand[:], top_v[:, 0, :].unsqueeze(2).to_broadcast([P, TOP, TOP]),
                                    top_v[:, 1, :].unsqueeze(1).to_broadcast([P, TOP, TOP]), ALU.add)
            dve.drain()
            c1, c2 = (c[:].rearrange("p a b -> p (a b)") for c in (cand, cand2))
            best = gate_next[:, k, :]
            nc.vector.tensor_copy(top_if[:], top_i[:])
            nc.vector.max(best[:, 0:8], c1)
            dve.drain()
            nc.vector.max_index(pos[:, 0:8], best[:, 0:8], c1)
            nc.vector.match_replace(c2, best[:, 0:8], c1, -3.0e38)
            dve.drain()
            nc.vector.max(best[:, 8:16], c2)
            dve.drain()
            nc.vector.max_index(pos[:, 8:16], best[:, 8:16], c2)
            dve.drain()
            nc.vector.tensor_scalar(pos2[:, 0, :], pos[:], 4, None, ALU.logical_shift_right)
            nc.vector.tensor_scalar(pos2[:, 1, :], pos[:], 15, None, ALU.bitwise_and)
            dve.drain()
            nc.vector.tensor_copy(pos_f[:], pos2[:])
            dve.drain()
            for a in range(2):
                nc.vector.tensor_tensor(hot[:, a], pos_f[:, a, :].unsqueeze(2).to_broadcast([P, TOP, TOP]),
                                        iota_f[:].unsqueeze(1).to_broadcast([P, TOP, TOP]), ALU.is_equal)
            dve.drain()
            for a in range(2):
                nc.vector.tensor_tensor(hot[:, a], hot[:, a], top_if[:, a, :].unsqueeze(1).to_broadcast([P, TOP, TOP]), ALU.mult)
            dve.drain()
            for a in range(2):
                nc.vector.tensor_reduce(e_f[:, a, :], hot[:, a], AX.X, ALU.add)
            dve.drain()
            nc.vector.scalar_tensor_tensor(out=idx_next[:, k * TOP:(k + 1) * TOP], in0=e_f[:, 0, :], scalar=float(NK),
                                           in1=e_f[:, 1, :], op0=ALU.mult, op1=ALU.add)
            dve.drain()

        def top_softmax(dve, count):
            nc.vector.tensor_copy(sums[:, 8:16], gate_next[:, :, 0])
            dve.drain()
            nc.vector.tensor_tensor(gate_next[:], gate_next[:], sums[:, 8:16].unsqueeze(2).to_broadcast([P, PH, TOP]),
                                    ALU.subtract).then_inc(soft_in, 1)
            dve.wait_ge(soft_exp, count)
            nc.vector.tensor_reduce(sums[:, 0:8], gate_next[:], AX.X, ALU.add)
            dve.drain()
            nc.vector.reciprocal(sums[:, 0:8], sums[:, 0:8])
            dve.drain()
            nc.vector.tensor_tensor(gate_next[:], gate_next[:], sums[:, 0:8].unsqueeze(2).to_broadcast([P, PH, TOP]), ALU.mult)
            dve.drain()

        def sp_peer(sp):
            sp.dma_start(sc[:], sc_dram[0:P, :].rearrange("t (h a k) -> t h a k", h=PH, a=2)).then_inc(sc_loaded, 16)
            sp.dma_start(gfin[:], ins["g_final"].partition_broadcast(P)).then_inc(gfin_loaded, 16)
            sp.sem_inc(y_stored, 16)
            with sp.Fori(0, NCH) as t:
                sp.wait_ge(u_used, t * SLOTS + RING)
                sp.dma_start(htok[:], h2_dram[bass.ds(t * P, P), :]).then_inc(htok_loaded, 16)
                sp.wait_ge(y_ready, t + 1)
                sp.dma_start(acc[:], x1_dram[bass.ds(t * P, P), :]).then_inc(acc_loaded, 16)
                sp.wait_ge(sc_used, t + 1)
                sp.dma_start(sc[:], sc_dram[bass.ds(t * P + P, P), :].rearrange("t (h a k) -> t h a k", h=PH, a=2)) \
                  .then_inc(sc_loaded, 16)
                sp.wait_ge(y_ready, t + 2)
                sp.dma_start(outs["y_prompt"][bass.ds(t * P, P), :], yout[:]).then_inc(y_stored, 16)
            sp.wait_ge(idx_ready, NCH + 1)
            sp.dma_start(idx_dram[:], idx_next[0:TS, :]).then_inc(packed, 16)
            sp.dma_start(gate_dram[:], gate_next[0:TS, :, :].rearrange("p h j -> p (h j)")).then_inc(packed, 16)
            sp.wait_ge(packed, 32)
            sp.dma_start(idx_s[:], idx_dram.rearrange("s (g j) -> (s g) j", j=TS)).then_inc(unpacked, 16)
            sp.dma_start(gate_s[:], gate_dram.rearrange("s (g j) -> (s g) j", j=TS)).then_inc(unpacked, 16)
            for s in range(TS):
                sp.dma_start(htok[s * 16:(s + 1) * 16, :], h2_dram[TP + s, :].partition_broadcast(16)).then_inc(unpacked, 16)
            sp.dma_start(htok2[:], x1_dram[TP:TN, :]).then_inc(acc_s_loaded, 16)
            sp.wait_ge(y_ready, NCH + 2)
            sp.dma_start(outs["y_sample"], yout[0:TS, :]).then_inc(y_stored, 16)
            sp.wait_ge(y_stored, 16 * (NCH + 2))

        def pool_peer_constants(pool):
            pool.wait_ge(stage_zero, 1)
            nc.gpsimd.iota(iota_u[:], pattern=[[1, TOP]], base=0, channel_multiplier=0)
            nc.gpsimd.memset(sel[:], 1.0)
            pool.drain()
            nc.gpsimd.tensor_copy(iota_f[:], iota_u[:])
            nc.gpsimd.affine_select(out=sel[:], in_=sel[:], pattern=[[-16, TS]], compare_op=ALU.is_ge, fill=0.0, base=0,
                                    channel_multiplier=1)
            pool.drain()
            nc.gpsimd.affine_select(out=sel[:], in_=sel[:], pattern=[[16, TS]], compare_op=ALU.is_ge, fill=0.0, base=15,
                                    channel_multiplier=-1)
            pool.drain().then_inc(peer_made, 1)

        def gather(ring, table, col, landed):
            nc.gpsimd.sem_inc(slots_granted, 1)
            return nc.gpsimd.indirect_dma_start(ring[:], None, ins[table], bass.IndirectOffsetOnAxis(ap=col, axis=0)) \
                     .then_inc(landed, 16)

        def pool_peer(pool):
            pool.wait_ge(h2_staged, NCH + 1)
            with pool.Fori(0, NCH) as t:
                pool.wait_ge(idx_ready, t + 1)
                for k in range(PH + 1):
                    for j in range(TOP):
                        if k < PH:
                            n = k * TOP + j
                            pool.wait_ge(u_used, t * SLOTS + (n + 1))
                            gather(u_ring[n % RING], "peer_u", idx_cur[:, n:n + 1], u_landed[n % RING])
                        if k > 0:
                            n = (k - 1) * TOP + j
                            pool.wait_ge(v_used, t * SLOTS + (n + 1))
                            gather(v_ring[n % RING], "peer_v", idx_cur[:, n:n + 1], v_landed[n % RING])
            pool.wait_ge(unpacked, 16 * (2 + TS))
            for table, ring, used, landed in (("peer_u", u_ring, u_used, u_landed), ("peer_v", v_ring, v_used, v_landed)):
                pool.wait_ge(used, NCH * SLOTS + RING)
                for j in range(TS):
                    gather(ring[j], table, idx_s[:, j:j + 1], landed[j])

        def act_peer(act):
            act.wait_ge(soft_in, 1)
            nc.scalar.activation(gate_next[:], gate_next[:], ACT.Exp).then_inc(soft_exp, 1)
            with act.Fori(0, NCH) as t:
                for k in range(PH):
                    act.wait_ge(dots_ready, t * PH + (k + 1))
                    q = slice(k * TOP, (k + 1) * TOP)
                    nc.scalar.activation(gelus[:, q], dots[:, q], ACT.Gelu).then_inc(gelu_ready, 1)
                act.wait_ge(soft_in, t + 2)
                nc.scalar.activation(gate_next[:], gate_next[:], ACT.Exp).then_inc(soft_exp, 1)
                act.wait_ge(acc_ready, t + 1)
                act.wait_ge(y_stored, t * 16 + 16)
                nc.scalar.activation(yout[:], acc[:], ACT.Square, accum_out=small[:, 0:1]).then_inc(y_squared, 1)
                act.wait_ge(y_var, t + 1)
                nc.scalar.activation(small[:, 2:3], small[:, 1:2], ACT.Sqrt).then_inc(y_root, 1)
            act.wait_ge(dots_ready, NCH * PH + 1)
            nc.scalar.activation(gelus[:, 0:TS], dots[:, 0:TS], ACT.Gelu).then_inc(gelu_ready, 1)
            act.wait_ge(acc_ready, NCH + 2)
            act.wait_ge(y_stored, (NCH + 1) * 16)
            nc.scalar.activation(yout[0:TS, :], htok2[:], ACT.Square, accum_out=small[0:TS, 0:1]).then_inc(y_squared, 1)
            act.wait_ge(y_var, NCH + 1)
            nc.scalar.activation(small[0:TS, 2:3], small[0:TS, 1:2], ACT.Sqrt).then_inc(y_root, 1)

        def final_norm(dve, x, rows, t):
            dve.wait_ge(y_squared, t + 1)
            nc.vector.tensor_scalar(small[0:rows, 1:2], small[0:rows, 0:1], 1.0 / D, EPS, ALU.mult, ALU.add).then_inc(y_var, 1)
            dve.wait_ge(y_root, t + 1)
            nc.vector.reciprocal(small[0:rows, 3:4], small[0:rows, 2:3])
            dve.drain()
            nc.vector.scalar_tensor_tensor(out=yout[0:rows, :], in0=x, scalar=small[0:rows, 3:4], in1=gfin[0:rows, :],
                                           op0=ALU.mult, op1=ALU.mult).then_inc(y_ready, 1)

        def dve_peer(dve):
            dve.wait_ge(peer_made, 1)
            dve.wait_ge(sc_loaded, 16)
            for k in range(PH):
                top_head(dve, k)
            dve.drain().then_inc(sc_used, 1)
            top_softmax(dve, 1)
            dve.wait_ge(gfin_loaded, 16)
            dve.drain().then_inc(u_used, RING)
            dve.drain().then_inc(v_used, RING)
            dve.drain().then_inc(y_ready, 1)
            with dve.Fori(0, NCH) as t:
                nc.vector.tensor_copy(idx_cur[:], idx_next[:])
                nc.vector.tensor_copy(gate_cur[:], gate_next[:].rearrange("p h j -> p (h j)"))
                dve.drain().then_inc(idx_ready, 1)
                dve.wait_ge(htok_loaded, t * 16 + 16)
                dve.wait_ge(acc_loaded, t * 16 + 16)
                for k in range(PH + 1):
                    if k > 0:
                        q = slice((k - 1) * TOP, k * TOP)
                        dve.wait_ge(gelu_ready, t * PH + k)
                        nc.vector.tensor_tensor(coef[:, q], gelus[:, q], gate_cur[:, q], ALU.mult)
                        dve.drain()
                    if k == 1:
                        dve.wait_ge(sc_loaded, t * 16 + 32)
                    for j in range(TOP):
                        if k < PH:
                            n = k * TOP + j
                            dve.wait_ge(u_landed[n % RING], t * (16 * SLOTS // RING) + 16 * (n // RING + 1))
                            u = u_ring[n % RING]
                            nc.vector.tensor_tensor_reduce(u[:], u[:], htok[:], 1.0, 0.0, ALU.mult, ALU.add,
                                                           dots[:, n:n + 1]).then_inc(u_used, 1)
                        if k > 0:
                            n = (k - 1) * TOP + j
                            dve.wait_ge(v_landed[n % RING], t * (16 * SLOTS // RING) + 16 * (n // RING + 1))
                            dve.wait_ge(v_used, t * SLOTS + RING + n)
                            nc.vector.scalar_tensor_tensor(out=acc[:], in0=v_ring[n % RING][:], scalar=coef[:, n:n + 1],
                                                           in1=acc[:], op0=ALU.mult, op1=ALU.add).then_inc(v_used, 1)
                    if k < PH:
                        dve.drain().then_inc(dots_ready, 1)
                    if k > 0:
                        top_head(dve, k - 1)
                    if k == PH:
                        dve.drain().then_inc(acc_ready, 1)
                        dve.drain().then_inc(sc_used, 1)
                        top_softmax_loop(dve, t)
                final_norm(dve, acc[:], P, t)
            dve.drain().then_inc(idx_ready, 1)
            dve.wait_ge(unpacked, 16 * (2 + TS))
            for j in range(TS):
                dve.wait_ge(u_landed[j], 16 * (NCH * SLOTS // RING + 1))
                nc.vector.tensor_tensor_reduce(u_ring[j][:], u_ring[j][:], htok[:], 1.0, 0.0, ALU.mult, ALU.add,
                                               dots[:, j:j + 1]).then_inc(u_used, 1)
            dve.drain().then_inc(dots_ready, 1)
            dve.wait_ge(gelu_ready, NCH * PH + 1)
            nc.vector.tensor_tensor(coef[:, 0:TS], gelus[:, 0:TS], gate_s[:], ALU.mult)
            dve.drain()
            for j in range(TS):
                dve.wait_ge(v_landed[j], 16 * (NCH * SLOTS // RING + 1))
                if j == 0:
                    nc.vector.tensor_scalar(acc[:], v_ring[j][:], coef[:, j:j + 1], None, ALU.mult)
                else:
                    nc.vector.scalar_tensor_tensor(out=acc[:], in0=v_ring[j][:], scalar=coef[:, j:j + 1], in1=acc[:],
                                                   op0=ALU.mult, op1=ALU.add)
                dve.drain()
            dve.drain().then_inc(acc_ready, 1)
            dve.wait_ge(folded, 1)
            dve.wait_ge(acc_s_loaded, 16)
            nc.vector.tensor_tensor(htok2[:].rearrange("p (b f) -> p b f", b=4), psum[0:TS, 0:4, :],
                                    htok2[:].rearrange("p (b f) -> p b f", b=4), ALU.add)
            dve.drain().then_inc(acc_ready, 1)
            final_norm(dve, htok2[:], TS, NCH)

        def top_softmax_loop(dve, t):
            top_softmax(dve, t + 2)

        def pe_peer(pe):
            pe.wait_ge(acc_ready, NCH + 1)
            for b in range(4):
                last = nc.tensor.matmul(psum[0:TS, b, :], sel[:], acc[:, b * 512:(b + 1) * 512], start=True, stop=True)
            last.then_inc(folded, 1)

        @block.sync
        def _(sp):
            sp_phase0(sp)
            sp_project(sp)
            sp_attention(sp)
            sp_merge(sp, N_BC, N_BB)
            sp_spatial(sp)
            sp_merge(sp, N_BB, N_BA)
            sp_gla(sp)
            sp_merge(sp, N_BA, N_OUT - 2)
            sp_merge(sp, N_OUT - 2, N_OUT, gates=False)
            sp_out(sp)
            sp_peer(sp)
            sp.wait_ge(state_out[0], 16 * 5)
            sp.wait_ge(state_out[1], 16 * 4)
            sp.wait_ge(vn_stored, 16)
            sp.wait_ge(out_stored, 64)

        @block.scalar
        def _(act):
            act_phase0(act)
            act_project(act)
            act_attention(act)
            act_merge(act, N_BC, N_BB)
            act_spatial(act)
            act_merge(act, N_BB, N_BA)
            act_gla(act)
            act.wait_ge(bra_loaded, 16)
            act.wait_ge(state_out[0], 16 * 5)
            act.wait_ge(state_out[1], 16 * 4)
            act_wide(act, bra)
            act_merge(act, N_BA, N_OUT)
            act_out(act)
            act_peer(act)

        @block.vector
        def _(dve):
            dve_phase0(dve)
            dve_project(dve)
            dve_attention(dve)
            dve_merge(dve, N_BC, N_BB, True)
            dve_spatial(dve)
            dve_merge(dve, N_BB, N_BA, False)
            dve_gla(dve)
            dve_wide(dve, bra, 5)
            dve_merge(dve, N_BA, N_OUT, False)
            dve.drain().then_inc(merged_ready, 1)
            dve_out(dve)
            dve_peer(dve)

        @block.tensor
        def _(pe):
            pe_phase0(pe)
            pe_project(pe)
            pe_attention(pe)
            pe.wait_ge(br_hi, 5)
            pe.wait_ge(br_lo, 5)
            pe_merge(pe, N_BC, N_BB, br2, range(8))
            pe_spatial(pe)
            pe.wait_ge(br_hi, 10)
            pe.wait_ge(br_lo, 10)
            pe_merge(pe, N_BB, N_BA, br2, range(8))
            pe_gla(pe)
            pe.wait_ge(act_hi, 9)
            pe.wait_ge(act_lo, 9)
            pe_merge(pe, N_BA, N_OUT, actr, range(KT))
            pe_out(pe)
            pe_peer(pe)

        @block.gpsimd
        def _(pool):
            pool_constants(pool)
            pool_attention(pool)
            pool_spatial(pool)
            pool_gla(pool)
            pool_peer_constants(pool)
            pool_peer(pool)


def lay_out(inputs):
    def a(name):
        return np.asarray(inputs[name])

    def feature_major(x):
        return np.ascontiguousarray(x.T.reshape(KT, P, -1).transpose(1, 0, 2))

    def blocks(w):
        k, n = w.shape
        return w.reshape(k // P, P, n // P, P).transpose(2, 1, 0, 3).reshape(n // P, P, k)

    def paired(w):
        b = blocks(w)
        return b.reshape(-1, 2, P, b.shape[2]).transpose(0, 2, 1, 3).reshape(-1, P, 2 * b.shape[2])

    w = a("w_in")[0]
    cuts = np.cumsum([0, 1024, 1024, 2048, 2048, RANK, 1024, 1024, 1024, 3 * D])
    q, k, v, r, low, gu, gv, xq, g = [w[:, cuts[i]:cuts[i + 1]] for i in range(9)]
    low = np.concatenate([low, np.zeros((D, P - RANK), w.dtype)], 1)
    stream = np.concatenate(
        [blocks(x) for x in (a("w_mem_kv")[0], xq, q, k, v, low, gu, gv, r, g[:, 2 * D:], g[:, D:2 * D], g[:, :D])]
        + [paired(a("w_br_xattn")[0]), paired(a("w_br_gmlp")[0]), blocks(a("w_br_gla")[0]),
           blocks(a("w_out")[0]), blocks(a("peer_w_q")[0])])
    assert stream.shape == (N_END, P, D)
    bg = a("b_gate")[0]
    cols = np.concatenate([a("norm_mix_g")[0], a("norm_ffn_g")[0], a("mem_norm_g")[0],
                           bg[2 * D:], bg[D:2 * D], bg[:D], a("b_alpha")[0], a("gla_norm_g")[0]])
    x = np.concatenate([a("x_prompt")[0], a("x_sample")[:, 0]])
    return {
        "xT": feature_major(x),
        "memT": feature_major(a("mem_prompt")[0]),
        "wstream": np.ascontiguousarray(stream),
        "kcache": np.ascontiguousarray(a("cache_mem_k")[0].transpose(0, 2, 3, 1).reshape(TS, 8, P, MEM).transpose(0, 2, 1, 3)),
        "vcache": np.ascontiguousarray(a("cache_mem_v")[0].reshape(TS, 2, P, 1024).transpose(0, 2, 1, 3)),
        "ln_g": a("gmlp_ln_g")[0],
        "ln_b": a("gmlp_ln_b")[0],
        "w_spatT": np.ascontiguousarray(a("gmlp_w_s")[0].transpose(2, 0, 1)),
        "b_spat": a("gmlp_b_s").reshape(1, HEADS * CH),
        "w_first": np.ascontiguousarray(a("gmlp_w_s")[0, :, 0, 0]),
        "w_up": a("w_alpha_up")[0],
        "state": a("state_gla")[0],
        "keys": np.ascontiguousarray(np.stack([a("peer_sub_k1")[0], a("peer_sub_k2")[0]]).transpose(3, 1, 0, 2)),
        "peer_u": a("peer_u")[0],
        "peer_v": a("peer_v")[0],
        "g_final": a("norm_final_g"),
        "pcols": np.ascontiguousarray(cols.reshape(-1, P).T),
    }


_OUTS = [("y_prompt", (TP, D)), ("y_sample", (TS, D)), ("gla_p", (HEADS, DK, DV)), ("gla_s", (TS, HEADS, DK, DV)),
         ("mem_k", (MEM, 1024)), ("mem_v", (MEM, 1024)), ("gmlp_v", (TS, 1024))]


def kernel(**inputs):
    import concourse.bacc as bacc
    from concourse.bass_utils import run_bass_kernel_spmd

    nc = bacc.Bacc("TRN2", target_bir_lowering=False, num_devices=1)
    arrays = {f"in_{k}": v for k, v in lay_out(inputs).items()}
    ins = {k[3:]: nc.dram_tensor(k, v.shape, mybir.dt.from_np(v.dtype), kind="ExternalInput").ap() for k, v in arrays.items()}
    outs = {k: nc.dram_tensor(f"out_{k}", shape, F32, kind="ExternalOutput").ap() for k, shape in _OUTS}
    mixer_kernel(nc, ins, outs)
    r = run_bass_kernel_spmd(nc, [arrays], core_ids=[0]).results[0]
    got = {k: r[f"out_{k}"] for k, _ in _OUTS}
    return (got["y_prompt"].reshape(1, TP, D), got["y_sample"].reshape(TS, 1, D),
            got["gla_p"].reshape(1, 1, HEADS, DK, DV), got["gla_s"].reshape(1, TS, HEADS, DK, DV),
            got["mem_k"].reshape(1, 1, MEM, HEADS, 256), got["mem_v"].reshape(1, 1, MEM, HEADS, 256),
            got["gmlp_v"].reshape(1, TS, 1, 1024))
```

```python
from contextlib import ExitStack

import numpy as np

import concourse.bass as bass
from concourse import mybir
from concourse.alu_op_type import AluOpType as ALU

ACT = mybir.ActivationFunctionType
AX = mybir.AxisListType
F32 = mybir.dt.float32
F32R = mybir.dt.float32r
U32 = mybir.dt.uint32

P = 128
D = 2048
KT = D // P
TP = 512
TS = 8
TN = TP + TS
HALF = TN // 2
MEM = 256
EPS = 1e-6
HEADS = 4
DK = 256
DV = 512
RANK = 16
CH = 128
NCH = TP // CH
SUB = 32
GATE_NORM = 16.0
CLAMP = float(np.exp(40.0))
PH = 8
NK = 128
TOP = 16
SLOTS = PH * TOP
RING = 8

N_MEM0 = 0
N_XQ = 16
N_Q = N_XQ + 8
N_K = N_Q + 8
N_V = N_K + 8
N_LOW = N_V + 16
N_GU = N_LOW + 1
N_GV = N_GU + 8
N_R = N_GV + 8
N_G = N_R + 16
N_BC = N_G + 48
N_BB = N_BC + 8
N_BA = N_BB + 8
N_OUT = N_BA + 16
N_WQ = N_OUT + 16
N_END = N_WQ + 16
N_UNITS = N_R + 4 * TS

C_MIX, C_FFN, C_MEM, C_BG, C_BA, C_GLA = 0, 16, 32, 48, 96, 104
NCOLS = 120

SBUF0 = 16512


def outputs_before(n):
    return n + max(0, min(n, N_BA) - N_BC)


def mixer_kernel(nc, ins, outs):
    ctx = ExitStack()
    with ctx:
        def sb(name, shape, dt, at):
            return nc.alloc_sbuf_tensor_at("sb_" + name, shape, dt, offset=SBUF0 + at)

        def sem(name):
            return ctx.enter_context(nc.semaphore(name))

        def dram(name, shape):
            return nc.dram_tensor("dram_" + name, shape, F32).ap()

        R_C = 49152
        R_1 = 65536
        R_2 = R_1 + 66560
        R_3 = R_2 + 33280
        R_X = R_3 + 33280
        raw = sb("raw", [P, 2, D], F32, 0)
        split = sb("split", [P, 2, 2, D], F32R, 16384)
        ident = sb("ident", [P, P], F32, R_C)
        ones = sb("ones", [P, P], F32, R_C + 512)
        tri = sb("tri", [P, P], F32, R_C + 1024)
        pcols = sb("pcols", [P, NCOLS], F32, R_C + 1536)
        zst = sb("zst", [P, 2, TN], F32, R_C + 2048)
        gt = sb("gt", [P, 2, TN], F32, R_C + 6208)
        rstd = sb("rstd", [P, TN], F32, R_C + 10368)
        ssum = sb("ssum", [P, TN], F32, R_C + 12448)
        bcur = sb("bcur", [P, 2], F32, R_C + 14528)
        small = sb("small", [P, 400], F32, R_C + 14592)

        sqx = sb("sqx", [P, KT, TN], F32, R_1)
        memx = sb("memx", [P, KT, MEM], F32, R_1 + 33280)
        sqm = sb("sqm", [P, KT, MEM], F32, R_1 + 49664)
        memr = sb("memr", [P, 2, KT, MEM], F32R, R_2)
        hx = sb("hx", [P, KT, TN], F32, R_3)
        actr = sb("actr", [P, 2, KT, TN], F32R, R_1)

        xq = sb("xq", [P, 8, TN], F32, R_1)
        kvt = sb("kvt", [P, 16, MEM], F32, R_1 + 16640)
        kvtok = sb("kvtok", [P, 2, 2048], F32, R_1 + 33024)
        prob = sb("prob", [P, 2, 4, MEM], F32, R_1 + 49408)
        probt = sb("probt", [P, 2, 2, TP], F32, R_1 + 57600)
        br2 = sb("br2", [P, 2, 8, TN], F32R, R_2)
        kcache = sb("kcache", [P, 4, 8, MEM], F32, R_3)
        vcache = sb("vcache", [P, 4, 2, 1024], F32, R_2)
        qmask = sb("qmask", [P, 2, 32 * 32], F32, R_X)
        prob_s = sb("prob_s", [32, MEM], F32, R_X + 8192)
        xqs = sb("xqs", [P, 8, TS], F32, R_X + 9216)
        merged = sb("merged", [P, KT, TN], F32, R_3)

        gv = sb("gv", [P, 8, TN], F32, R_1)
        gu = sb("gu", [P, 8, TN], F32, R_1 + 16640)
        vn = sb("vn", [P, 2, 1024], F32, R_1 + 33280)
        lnrow = sb("lnrow", [P, 2, 1024], F32, R_1 + 41472)
        wspat = sb("wspat", [P, HEADS, CH], F32, R_1 + 49664)
        gated = sb("gated", [P, 2, 8, CH], F32, R_1 + 51712)
        bspat = sb("bspat", [1, HEADS * CH], F32, R_1 + 59904)
        wfirst = sb("wfirst", [TS, HEADS], F32, R_1 + 61952)
        wdiag = sb("wdiag", [TS, HEADS, TS], F32, R_1 + 61984)
        bfirst = sb("bfirst", [1, HEADS, TS], F32, R_1 + 62112)

        state = sb("state", [P, 8, DV], F32, R_1)
        bcum = sb("bcum", [P, 8, TN], F32, R_1 + 16384)
        qc = sb("qc", [P, 8, CH], F32, R_1 + 33024)
        kc = sb("kc", [P, 8, CH], F32, R_1 + 37120)
        vc = sb("vc", [P, KT, CH], F32, R_1 + 41216)
        rc = sb("rc", [P, KT, CH], F32, R_1 + 49408)
        vtok = sb("vtok", [P, D], F32, R_1 + 57600)
        gx = sb("gx", [P, 8, TN], F32, R_2)
        gy = sb("gy", [P, 8, TN], F32, R_2 + 16640)
        qe = sb("qe", [P, 8, CH], F32, R_2)
        kd = sb("kd", [P, 8, CH], F32, R_2 + 4096)
        eb = sb("eb", [P, 8, CH], F32, R_2 + 8192)
        ki = sb("ki", [P, 2, 8, CH], F32, R_2 + 12288)
        kdtok = sb("kdtok", [P, 1024], F32, R_2 + 20480)
        scores_t = sb("scores_t", [P, HEADS, CH], F32, R_2 + 24576)
        qi = sb("qi", [P, 2, 8, SUB], F32, R_2 + 26624)
        norm_a = sb("norm_a", [P, HEADS, CH], F32, R_X + 11168)
        low = sb("low", [RANK, TN], F32, R_X)
        w_up = sb("w_up", [RANK, 1024], F32, R_X + 2080)
        keep = sb("keep", [P, TP], F32, R_X + 6176)
        states = [sb(f"states{i}", [P, 2, DV], F32, R_2 + 4096 * i) for i in range(2)]
        vrow = sb("vrow", [P, D], F32, R_2 + 8192)
        v8 = sb("v8", [TS, D], F32, R_2 + 16384)
        gxs = sb("gxs", [P, 8, TS], F32, R_2 + 24576)
        gys = sb("gys", [P, 8, TS], F32, R_2 + 24832)
        low_s = sb("low_s", [RANK, TS], F32, R_2 + 25088)
        ks_cur = sb("ks_cur", [P, 8, 1], F32, R_2 + 25120)
        es_cur = sb("es_cur", [P, 8, 1], F32, R_2 + 25152)
        qs = sb("qs", [P, 8, TS], F32, R_X + 8224)
        ks = sb("ks", [P, 8, TS], F32, R_X + 8480)
        vs = sb("vs", [P, KT, TS], F32, R_X + 8736)
        rs = sb("rs", [P, KT, TS], F32, R_X + 9248)
        es = sb("es", [P, 8, TS], F32, R_X + 9760)
        os_ = sb("os_", [P, KT, TS], F32, R_X + 10656)
        sqs = sb("sqs", [P, KT, TS], F32, R_X + 10016)
        norm_s = sb("norm_s", [P, HEADS, TS], F32, R_X + 10528)
        bra = sb("bra", [P, KT, TN], F32, R_2)

        x1 = sb("x1", [P, KT, TN], F32, R_2)
        sq2 = sb("sq2", [P, TN], F32, R_3)
        h2 = sb("h2", [P, KT, TN], F32, R_3)
        pq = sb("pq", [P, KT, TN], F32, R_2)
        keys = sb("keys", [P, PH, 2, NK], F32, R_X)
        stage_x = [sb("stage_x0", [P, D], F32, R_X), sb("stage_x1", [P, D], F32, R_C + 2048)]
        stage_s = [sb("stage_s0", [P, D], F32, 0), sb("stage_s1", [P, D], F32, 8192)]
        stage_h = [sb("stage_h0", [P, D], F32, 16384), sb("stage_h1", [P, D], F32, 40960)]

        u_ring = [sb(f"u_ring{i}", [P, D], F32, 65536 + 8192 * i) for i in range(RING)]
        v_ring = [sb(f"v_ring{i}", [P, D], F32, 65536 + 8192 * (RING + i)) for i in range(RING)]
        htok2 = sb("htok2", [TS, D], F32, 0)
        htok = sb("htok", [P, D], F32, 65536 + 8192 * 2 * RING)
        gfin = sb("gfin", [P, D], F32, 16384)
        sc = sb("sc", [P, PH, 2, NK], F32, 24576)
        acc = sb("acc", [P, D], F32, 32768)
        yout = sb("yout", [P, D], F32, 40960)
        R_S = R_X + 8192
        top_v = sb("top_v", [P, 2, TOP], F32, R_S)
        top_i = sb("top_i", [P, 2, TOP], U32, R_S + 128)
        top_if = sb("top_if", [P, 2, TOP], F32, R_S + 256)
        rest = sb("rest", [P, 2, NK], F32, R_S + 384)
        cand = sb("cand", [P, TOP, TOP], F32, R_S + 1408)
        hot = sb("hot", [P, 2, TOP, TOP], F32, R_S + 2432)
        pos = sb("pos", [P, TOP], U32, R_S + 4480)
        pos2 = sb("pos2", [P, 2, TOP], U32, R_S + 4544)
        pos_f = sb("pos_f", [P, 2, TOP], F32, R_S + 4672)
        e_f = sb("e_f", [P, 2, TOP], F32, R_S + 4800)
        iota_u = sb("iota_u", [P, TOP], U32, R_S + 4928)
        iota_f = sb("iota_f", [P, TOP], F32, R_S + 4992)
        sel = sb("sel", [P, TS], F32, R_S + 5056)
        sums = sb("sums", [P, 16], F32, R_S + 5088)
        dots = sb("dots", [P, SLOTS], F32, R_C + 10368)
        gelus = sb("gelus", [P, SLOTS], F32, R_C + 10880)
        coef = sb("coef", [P, SLOTS], F32, R_C + 11392)
        cand2 = sb("cand2", [P, TOP, TOP], F32, R_C + 11904)
        idx_next = sb("idx_next", [P, SLOTS], U32, R_C + 2048)
        idx_cur = sb("idx_cur", [P, SLOTS], U32, R_C + 2560)
        gate_next = sb("gate_next", [P, PH, TOP], F32, R_C + 3072)
        gate_cur = sb("gate_cur", [P, SLOTS], F32, R_C + 3584)
        idx_s = sb("idx_s", [P, TS], U32, R_C + 4096)
        gate_s = sb("gate_s", [P, TS], F32, R_C + 4128)

        psum = ctx.enter_context(nc.psum_tensor("psum", [P, 8, 512], F32))

        z = dram("z", [N_BC, P, TN])

        v_dram = dram("v", [TS, D])
        bra_dram = dram("bra", [P, KT, TN])
        x1_dram = dram("x1", [TN, D])
        h2_dram = dram("h2", [TN, D])
        sc_dram = dram("sc", [(NCH + 1) * P, D])
        idx_dram = nc.dram_tensor("dram_idx", [TS, SLOTS], U32).ap()
        gate_dram = dram("gate", [TS, SLOTS])
        const_loaded = sem("const_loaded")
        mem_loaded = sem("mem_loaded")
        x_loaded = sem("x_loaded")
        const_made = sem("const_made")
        raw_landed = [sem("raw_landed0"), sem("raw_landed1")]
        hi_ready = sem("hi_ready")
        lo_ready = sem("lo_ready")
        out_ready = sem("out_ready")
        evac_done = sem("evac_done")
        z_stored = [sem("z_stored0"), sem("z_stored1")]
        squares_ready = sem("squares_ready")
        SQUARES_GLA, SQUARES_Y = 5, 5 + NCH + 1
        sums_ready = sem("sums_ready")
        spread_ready = sem("spread_ready")
        root_in = sem("root_in")
        root_out = sem("root_out")
        ROOTS_SP, ROOTS_GLA, ROOTS_X1, ROOTS_Y = 2, NCH + 3, 2 * NCH + 4, 2 * NCH + 5
        normed = sem("normed")
        act_hi = sem("act_hi")
        act_lo = sem("act_lo")

        gate_landed = [sem("gate_landed0"), sem("gate_landed1")]
        xq_loaded = sem("xq_loaded")
        kvt_loaded = sem("kvt_loaded")
        kc_landed = [sem(f"kc_landed{i}") for i in range(4)]
        vc_landed = [sem(f"vc_landed{i}") for i in range(4)]
        kc_used = sem("kc_used")
        vc_used = sem("vc_used")
        qm_zeroed = sem("qm_zeroed")
        qm_ready = sem("qm_ready")
        att_scores = sem("att_scores")
        att_max = sem("att_max")
        att_exp = sem("att_exp")
        att_prob = sem("att_prob")
        att_turned = sem("att_turned")
        att_probt = sem("att_probt")
        att_out = sem("att_out")
        samp_copied = sem("samp_copied")
        samp_turned = sem("samp_turned")
        kv_turned = sem("kv_turned")
        kv_tok = sem("kv_tok")
        out_stored = sem("out_stored")
        br_hi = sem("br_hi")
        br_lo = sem("br_lo")

        gv_loaded = sem("gv_loaded")
        gu_loaded = sem("gu_loaded")
        sp_loaded = sem("sp_loaded")
        sp_masked = sem("sp_masked")
        sp_turned = sem("sp_turned")
        sp_vn = sem("sp_vn")
        sp_mixed = sem("sp_mixed")
        sp_gated = sem("sp_gated")
        vn_stored = sem("vn_stored")
        low_loaded = sem("low_loaded")
        keep_made = sem("keep_made")
        up_ready = sem("up_ready")
        up_read = sem("up_read")
        gx_ready = sem("gx_ready")
        gy_ready = sem("gy_ready")
        bcum_ready = sem("bcum_ready")
        chunk_loaded = sem("chunk_loaded")
        chunk_stored = sem("chunk_stored")
        eb_ready = sem("eb_ready")
        qe_ready = sem("qe_ready")
        kd_in = sem("kd_in")
        kd_exp = sem("kd_exp")
        kd_ready = sem("kd_ready")
        sub_in = sem("sub_in")
        sub_exp = sem("sub_exp")
        sub_ready = sem("sub_ready")
        sub_scored = sem("sub_scored")
        sc_ready = sem("sc_ready")
        v_turned = sem("v_turned")
        v_tok = sem("v_tok")
        kd_turned = sem("kd_turned")
        kd_tok = sem("kd_tok")
        o_ready = sem("o_ready")
        o_summed = sem("o_summed")
        o_normed = sem("o_normed")
        o_read = sem("o_read")
        kv_ready = sem("kv_ready")
        kv_read = sem("kv_read")
        state_done = sem("state_done")
        state_stored = sem("state_stored")
        vc_loaded = sem("vc_loaded")
        st_in = [sem(f"st_in{i}") for i in range(2)]
        st_out = [sem(f"st_out{i}") for i in range(2)]
        st_scaled = sem("st_scaled")
        st_done = sem("st_done")
        st_read = sem("st_read")
        vrow_loaded = sem("vrow_loaded")
        os_read = sem("os_read")
        rc_gained = sem("rc_gained")
        samples_loaded = sem("samples_loaded")
        bra_loaded = sem("bra_loaded")

        pq_ready = sem("pq_ready")
        acc_s_loaded = sem("acc_s_loaded")
        merged_ready = sem("merged_ready")
        x1_loaded = sem("x1_loaded")
        x1_ready = sem("x1_ready")
        x1_turned = sem("x1_turned")
        x1_staged = sem("x1_staged")
        x1_stored = [sem("x1_stored0"), sem("x1_stored1")]
        sc_stored = x1_stored
        X1_STORES = (48, 32)
        keys_loaded = sem("keys_loaded")
        scored = sem("scored")
        sc_staged = sem("sc_staged")
        h2_turned = sem("h2_turned")
        h2_staged = sem("h2_staged")
        h2_stored = [sem("h2_stored0"), sem("h2_stored1")]
        gfin_loaded = sem("gfin_loaded")
        peer_made = sem("peer_made")
        sc_loaded = sem("sc_loaded")
        sc_used = sem("sc_used")
        soft_in = sem("soft_in")
        soft_exp = sem("soft_exp")
        idx_ready = sem("idx_ready")
        htok_loaded = sem("htok_loaded")
        acc_loaded = sem("acc_loaded")
        u_landed = [sem(f"u_landed{i}") for i in range(RING)]
        v_landed = [sem(f"v_landed{i}") for i in range(RING)]
        slots_granted = sem("slots_granted")
        u_used = sem("u_used")
        v_used = sem("v_used")
        dots_ready = sem("dots_ready")
        gelu_ready = sem("gelu_ready")
        acc_ready = sem("acc_ready")
        y_ready = sem("y_ready")
        y_stored = sem("y_stored")
        packed = sem("packed")
        unpacked = sem("unpacked")
        folded = sem("folded")

        block = ctx.enter_context(nc.Block())

        def load_block(sp, n, slot):
            if not isinstance(n, int) or n >= 2:
                sp.wait_ge(hi_ready, n - 1)
                sp.wait_ge(lo_ready, n - 1)
            src = ins["wstream"][bass.ds(n, 1), :, :].rearrange("a p c -> (a p) c")
            sp.dma_start(raw[:, slot, :], src).then_inc(raw_landed[slot], 16)

        def split_hi(act, n, slot, use, outs_done):
            act.wait_ge(raw_landed[slot], 16 * use)
            if not isinstance(outs_done, int) or outs_done > 0:
                act.wait_ge(out_ready, outs_done)
            nc.scalar.activation(split[:, slot, 0, :], raw[:, slot, :], ACT.Copy).then_inc(hi_ready, 1)

        def split_lo(dve, n, slot):
            dve.wait_ge(hi_ready, n + 1)
            nc.vector.tensor_tensor(split[:, slot, 1, :], raw[:, slot, :], split[:, slot, 0, :],
                                    ALU.subtract).then_inc(lo_ready, 1)

        def wait_piece(pe, kt, k):
            if kt % 4 == 0:
                pe.wait_ge(act_hi, k + kt // 4 + 1)
                pe.wait_ge(act_lo, k + kt // 4 + 1)

        def products(pe, slot, acts, kts, w0, pair, ntok, halves=2, ready=None):
            for i, kt in enumerate(kts):
                if ready is not None:
                    ready(kt)
                w = [split[:, slot, x, w0 + i * P:w0 + (i + 1) * P] for x in range(2)]
                for a, b in ((0, 0), (0, 1), (1, 0)):
                    for half in range(halves):
                        last = nc.tensor.matmul(
                            psum[:, 2 * pair + half, 0:ntok], w[a], acts[:, b, kt, half * ntok:(half + 1) * ntok],
                            start=(i == 0 and a == 0 and b == 0), stop=(i == len(kts) - 1 and a == 1))
            return last

        def pair_of(pair, ntok=HALF):
            return psum[:, 2 * pair:2 * pair + 2, 0:ntok]

        def in_halves(ap):
            return ap.rearrange("p (h t) -> p h t", h=2)

        PLAIN = [(N_MEM0, N_XQ, ACT.Copy, MEM), (N_XQ, N_LOW, ACT.Copy, TN), (N_LOW, N_GU, ACT.Copy, TN),
                 (N_GU, N_GV, ACT.Gelu, TN), (N_GV, N_R, ACT.Gelu, TN), (N_R, N_G, ACT.Silu, TN),
                 (N_G, N_UNITS - 4, ACT.Sigmoid, TN), (N_UNITS - 4, N_UNITS, ACT.Sigmoid, TN),
                 (N_UNITS, N_BC, ACT.Sigmoid, TN)]

        def seg_loop(eng, n0, n1, body):
            if n1 - n0 == 1 or n0 == 0:
                k = 1 if n1 - n0 == 1 else 2
                for n in range(n0, n0 + k):
                    body(n, n % 2, (n - n % 2) // 2)
                n0 += k
            assert (n1 - n0) % 2 == 0
            if n0 < n1:
                with eng.Fori(0, (n1 - n0) // 2) as i:
                    for b in range(2):
                        n = n0 + b
                        body(i * 2 + n, n % 2, i + (n - n % 2) // 2)

        def unit_loop(eng, n0, n1, body):
            assert (n0 - N_R) % 4 == 0 and (n1 - n0) % 4 == 0
            with eng.Fori(0, (n1 - n0) // 4) as i:
                for h in range(HEADS):
                    n = n0 + h
                    body(i * 4 + n, n % 2, i * 2 + (n - n % 2) // 2, i + (n0 - N_R) // 4, h)

        def with_units(n0):
            return N_R <= n0 < N_UNITS

        def sp_samples_first(sp):
            sp.wait_ge(z_stored[0], 16 * ((N_GU + 1) // 2))
            sp.wait_ge(z_stored[1], 16 * (N_GU // 2))
            sp.dma_start(low_s[:], z[N_LOW, 0:RANK, TP:TN]).then_inc(low_loaded, 16)
            sp.dma_start(w_up[:], ins["w_up"]).then_inc(low_loaded, 16)
            for dst, n, k in ((qs, N_Q, 8), (ks, N_K, 8), (vs, N_V, 16)):
                sp.dma_start(dst[:], z[n:n + k, :, TP:TN].rearrange("n p t -> p n t")).then_inc(samples_loaded, 16)

        def sp_samples_start(sp):
            sp.dma_start(states[0][:], state_of(ins["state"], 0, 0)).then_inc(st_in[0], 16)
            sp.dma_start(states[1][:], state_of(ins["state"], 0, 1)).then_inc(st_in[1], 16)
            sp.wait_ge(v_tok, 2)
            sp.dma_start(v_dram[:], v8[:]).then_inc(samples_loaded, 16)
            sp.wait_ge(samples_loaded, 64)
            sp.dma_start(vrow[:], row_of(0)).then_inc(vrow_loaded, 16)

        def row_of(s):
            return v_dram[bass.ds(s, 1), :].rearrange("a f -> (a f)").partition_broadcast(P)

        def state_of(table, s, h):
            return table[bass.ds(s, 1), h].rearrange("a (k p) v -> p (a k) v", p=P)

        def sp_unit(sp, n, s, h, last):
            unit = n - N_R
            sp.wait_ge(st_done, unit + 1)
            sp.dma_start(state_of(outs["gla_s"], s, h), states[h % 2][:]).then_inc(st_out[h % 2], 16)
            if h == HEADS - 1 and not last:
                sp.dma_start(vrow[:], row_of(s + 1)).then_inc(vrow_loaded, 16)
            if h < 2 or not last:
                src = ins["state"].rearrange("s h k v -> (s h) k v")[bass.ds(s * HEADS + (h + 2), 1)] \
                                  .rearrange("a (k p) v -> p (a k) v", p=P)
                sp.wait_ge(st_out[h % 2], s * 32 + 16 * (h // 2 + 1))
                sp.wait_ge(st_read, unit + 1)
                sp.dma_start(states[h % 2][:], src).then_inc(st_in[h % 2], 16)

        def act_samples_start(act):
            act.wait_ge(gx_ready, 1)
            act.wait_ge(evac_done, N_XQ)
            nc.scalar.activation(gys[:], gxs[:], ACT.Abs)
            act.drain()
            nc.scalar.activation(gys[:], gys[:], ACT.Exp, scale=-1.0)
            act.drain()
            nc.scalar.activation(gys[:], gys[:], ACT.Ln, bias=1.0).then_inc(gy_ready, 1)
            act.wait_ge(v_turned, 1)
            for b in range(4):
                last = nc.scalar.activation(v8[:, b * 512:(b + 1) * 512], psum[0:TS, 6 + b % 2, :], ACT.Copy)
                if b == 1:
                    last.then_inc(v_tok, 1)
                    act.wait_ge(v_turned, 2)
            last.then_inc(v_tok, 1)
            act.wait_ge(gx_ready, 2)
            nc.scalar.activation(es[:], gxs[:], ACT.Exp, scale=1.0 / GATE_NORM)
            act.drain()
            act.sem_inc(os_read, 2)

        def act_unit(act, n, s, h):
            unit = n - N_R
            if h == 0:
                nc.scalar.activation(es_cur[:], es[:, :, bass.ds(s, 1)], ACT.Copy)
                act.drain()
            act.wait_ge(st_in[h % 2], s * 32 + 16 * (h // 2 + 1))
            for dt in range(2):
                last = nc.scalar.activation(states[h % 2][:, dt, :], states[h % 2][:, dt, :], ACT.Copy,
                                            scale=es_cur[:, 2 * h + dt, :])
            last.then_inc(st_scaled, 1)

        def act_unit_out(act, n, s, h):
            act.wait_ge(st_read, n - N_R + 1)
            nc.scalar.activation(os_[:, 4 * h:4 * h + 4, bass.ds(s, 1)], psum[:, 4 + h % 2, 0:4].unsqueeze(2),
                                 ACT.Copy).then_inc(os_read, 1)

        def dve_samples_first(dve):
            dve.wait_ge(up_ready, 1)
            nc.vector.tensor_tensor(gxs[:], psum[:, 4, 0:64].rearrange("p (f s) -> p f s", f=8),
                                    pcols[:, C_BA:C_BA + 8].unsqueeze(2).to_broadcast([P, 8, TS]), ALU.add).then_inc(gx_ready, 1)
            dve.wait_ge(samples_loaded, 48)
            nc.vector.tensor_scalar(qs[:], qs[:], DK ** -0.5, None, ALU.mult).then_inc(qe_ready, 1)

        def dve_samples_start(dve):
            dve.wait_ge(gy_ready, 1)
            nc.vector.scalar_tensor_tensor(out=gxs[:], in0=gxs[:], scalar=0.0, in1=gys[:], op0=ALU.min,
                                           op1=ALU.subtract).then_inc(gx_ready, 1)

        def dve_unit(dve, n, s, h):
            if h == 0:
                nc.vector.tensor_copy(ks_cur[:], ks[:, :, bass.ds(s, 1)])
                dve.drain()
                dve.wait_ge(vrow_loaded, s * 16 + 16)
            dve.wait_ge(st_scaled, n - N_R + 1)
            for dt in range(2):
                st = states[h % 2][:, dt, :]
                last = nc.vector.scalar_tensor_tensor(out=st, in0=vrow[:, h * DV:(h + 1) * DV],
                                                      scalar=ks_cur[:, 2 * h + dt, :], in1=st, op0=ALU.mult, op1=ALU.add)
            last.then_inc(st_done, 1)

        def pe_samples_first(pe):
            pe.wait_ge(low_loaded, 32)
            for f in range(8):
                last = nc.tensor.matmul(psum[:, 4, f * TS:(f + 1) * TS], w_up[:, f * P:(f + 1) * P], low_s[:],
                                        start=True, stop=True)
            last.then_inc(up_ready, 1)

        def pe_samples_turn(pe, half):
            pe.wait_ge(samples_loaded, 48)
            if half == 1:
                pe.wait_ge(v_tok, 1)
            for f in range(8 * half, 8 * half + 8):
                last = nc.tensor.transpose(psum[0:TS, 6 + (f // 4) % 2, (f % 4) * P:(f % 4 + 1) * P], vs[:, f, :], ident[:])
            last.then_inc(v_turned, 1)

        def pe_unit(pe, n, s, h):
            pe.wait_ge(st_done, n - N_R + 1)
            pe.wait_ge(os_read, n - N_R + 1)
            for j in range(4):
                for dt in range(2):
                    last = nc.tensor.matmul(psum[:, 4 + h % 2, j:j + 1], states[h % 2][:, dt, j * P:(j + 1) * P],
                                            qs[:, 2 * h + dt, bass.ds(s, 1)], start=(dt == 0), stop=(dt == 1))
            last.then_inc(st_read, 1)

        def sp_attention(sp):
            sp.wait_ge(z_stored[0], 16 * ((N_BC + 1) // 2))
            sp.wait_ge(z_stored[1], 16 * (N_BC // 2))
            sp.dma_start(xq[:], z[N_XQ:N_Q].rearrange("n p t -> p n t")).then_inc(xq_loaded, 16)
            sp.dma_start(kvt[:], z[0:16, :, 0:MEM].rearrange("n p t -> p n t")).then_inc(kvt_loaded, 16)
            for s in range(4, TS):
                sp.wait_ge(kc_used, s - 3)
                sp.dma_start(kcache[:, s % 4], ins["kcache"][s]).then_inc(kc_landed[s % 4], 16)
            for s in range(4, TS):
                sp.wait_ge(vc_used, s - 3)
                sp.dma_start(vcache[:, s % 4], ins["vcache"][s]).then_inc(vc_landed[s % 4], 16)
            sp.wait_ge(kv_tok, 8)
            for mt in range(2):
                sp.dma_start(outs["mem_k"][mt * P:(mt + 1) * P, :], kvtok[:, mt, 0:1024]).then_inc(out_stored, 16)
                sp.dma_start(outs["mem_v"][mt * P:(mt + 1) * P, :], kvtok[:, mt, 1024:2048]).then_inc(out_stored, 16)
            load_gates_ahead(sp, N_BC)

        def load_gates_ahead(sp, first):
            for m in (first, first + 1):
                load_gate(sp, m, m % 2)

        def load_gate(sp, m, slot):
            src = z[bass.ds(m + (N_G - N_BC), 1), :, :].rearrange("a p t -> (a p) t")
            sp.dma_start(gt[:, slot, :], src).then_inc(gate_landed[slot], 16)

        def pool_constants(pool):
            nc.gpsimd.memset(ident[:], 0.0)
            nc.gpsimd.memset(tri[:], DK ** -0.5)
            pool.drain()
            nc.gpsimd.affine_select(out=ident[:], in_=ident[:], pattern=[[-1, P]], compare_op=ALU.not_equal,
                                    fill=1.0, base=0, channel_multiplier=1).then_inc(const_made, 1)
            nc.gpsimd.affine_select(out=tri[:], in_=tri[:], pattern=[[1, P]], compare_op=ALU.is_ge,
                                    fill=0.0, base=0, channel_multiplier=-1).then_inc(const_made, 1)

        def pool_attention(pool):
            pool.wait_ge(evac_done, N_UNITS)
            nc.gpsimd.memset(qmask[:], 0.0).then_inc(qm_zeroed, 1)

        def pe_attention(pe):
            pe.wait_ge(qm_ready, 1)
            for s in range(TS):
                pe.wait_ge(kc_landed[s % 4], 16 * (s // 4 + 1))
                for h in range(HEADS):
                    for dt in range(2):
                        i = s * HEADS + h
                        last = nc.tensor.matmul(psum[0:32, 7, 0:MEM], qmask[:, dt, i * 32:(i + 1) * 32],
                                                kcache[:, s % 4, 2 * h + dt, :],
                                                start=(i == 0 and dt == 0), stop=(i == 31 and dt == 1))
                last.then_inc(kc_used, 1)
            last = None
            pe.wait_ge(evac_done, N_BC)
            pe.wait_ge(kvt_loaded, 16)
            pe.wait_ge(xq_loaded, 32)
            pe.wait_ge(const_made, 3)
            for g in range(8):
                mt, f0 = g % 2, 4 * (g // 2)
                if g >= 2:
                    pe.wait_ge(kv_tok, g - 1)
                for j in range(4):
                    last = nc.tensor.transpose(psum[:, 4 + g % 2, j * P:(j + 1) * P],
                                               kvt[:, f0 + j, mt * P:(mt + 1) * P], ident[:])
                last.then_inc(kv_turned, 1)

            def scores(h):
                if h >= 2:
                    pe.wait_ge(att_exp, h)
                for tt in range(4):
                    for dt in range(2):
                        last = nc.tensor.matmul(
                            psum[:, 2 * (h % 2) + tt // 2, (tt % 2) * MEM:(tt % 2 + 1) * MEM],
                            xq[:, 2 * h + dt, tt * P:(tt + 1) * P], kvt[:, 2 * h + dt, :],
                            start=(dt == 0), stop=(dt == 1))
                last.then_inc(att_scores, 1)

            scores(0)
            scores(1)
            pe.wait_ge(att_prob, 1)
            pe.wait_ge(kv_tok, 8)
            for mt in range(2):
                last = nc.tensor.transpose(psum[:, 4, mt * 32:(mt + 1) * 32], prob_s[:, mt * P:(mt + 1) * P],
                                           ident[0:32, 0:32])
            last.then_inc(att_turned, 1)
            pe.wait_ge(att_probt, 1)
            for s in range(TS):
                pe.wait_ge(vc_landed[s % 4], 16 * (s // 4 + 1))
                for h in range(HEADS):
                    for mt in range(2):
                        i = s * HEADS + h
                        last = nc.tensor.matmul(psum[0:32, 7, 0:MEM], qmask[:, mt, i * 32:(i + 1) * 32],
                                                vcache[:, s % 4, mt, h * 256:(h + 1) * 256],
                                                start=(i == 0 and mt == 0), stop=(i == 31 and mt == 1))
                last.then_inc(vc_used, 1)
            pe.wait_ge(samp_copied, 1)
            for dt in range(2):
                last = nc.tensor.transpose(psum[:, 7, dt * 32:(dt + 1) * 32], prob_s[:, dt * P:(dt + 1) * P], ident[0:32, 0:32])
            last.then_inc(samp_turned, 1)
            for h in range(HEADS):
                pe.wait_ge(att_prob, h + 2)
                for mt in range(2):
                    for tt in range(4):
                        last = nc.tensor.transpose(psum[:, 4 + mt, tt * P:(tt + 1) * P],
                                                   prob[:, h % 2, tt, mt * P:(mt + 1) * P], ident[:])
                last.then_inc(att_turned, 1)
                if h + 2 < HEADS:
                    scores(h + 2)
                pe.wait_ge(att_probt, h + 2)
                pe.wait_ge(br_hi, h + 1)
                pe.wait_ge(br_lo, h + 1)
                for dt in range(2):
                    c0 = 1024 + h * 256 + dt * P
                    for mt in range(2):
                        last = nc.tensor.matmul(psum[:, 6 + dt, :], kvtok[:, mt, c0:c0 + P], probt[:, h % 2, mt, :],
                                                start=(mt == 0), stop=(mt == 1))
                last.then_inc(att_out, 1)

        def samples_out(h):
            return psum[:, 7, 0:64].rearrange("p (d s h) -> p d s h", d=2, h=HEADS)[:, :, :, h]

        def act_attention(act):
            act.wait_ge(att_max, 1)
            nc.scalar.activation(prob_s[:], psum[0:32, 7, 0:MEM], ACT.Exp, bias=small[0:32, 0:1], scale=1.0 / 16,
                                 accum_out=small[0:32, 8:9]).then_inc(att_exp, 1)
            def exps(h):
                act.wait_ge(att_max, h + 2)
                if h >= 2:
                    act.wait_ge(att_turned, h)
                for tt in range(4):
                    c = 16 + 16 * (h % 2) + tt
                    last = nc.scalar.activation(prob[:, h % 2, tt, :],
                                                psum[:, 2 * (h % 2) + tt // 2, (tt % 2) * MEM:(tt % 2 + 1) * MEM],
                                                ACT.Exp, bias=small[:, c:c + 1], scale=1.0 / 16,
                                                accum_out=small[:, c + 8:c + 9])
                last.then_inc(att_exp, 1)

            exps(0)
            exps(1)
            act.wait_ge(att_turned, 1)
            nc.scalar.activation(qmask[:, :, ::33], psum[:, 4, 0:64].rearrange("p (m i) -> p m i", m=2),
                                 ACT.Copy).then_inc(att_probt, 1)
            act.wait_ge(vc_used, TS)
            nc.scalar.activation(prob_s[:], psum[0:32, 7, 0:MEM], ACT.Copy).then_inc(samp_copied, 1)
            act.wait_ge(samp_turned, 1)
            for h in range(HEADS):
                last = nc.scalar.activation(br2[:, 0, 2 * h:2 * h + 2, TP:TN], samples_out(h), ACT.Copy)
            last.then_inc(br_hi, 1)
            for h in range(HEADS):
                act.wait_ge(att_turned, h + 2)
                nc.scalar.activation(probt[:, h % 2], psum[:, 4:6, :], ACT.Copy).then_inc(att_probt, 1)
                if h + 2 < HEADS:
                    exps(h + 2)
                act.wait_ge(att_out, h + 1)
                nc.scalar.activation(br2[:, 0, 2 * h:2 * h + 2, 0:TP], psum[:, 6:8, :], ACT.Copy).then_inc(br_hi, 1)

        def dve_attention(dve):
            dve.wait_ge(qm_zeroed, 1)
            dve.wait_ge(xq_loaded, 16)
            for dt in range(2):
                last = nc.vector.tensor_copy(
                    qmask[:, dt, ::33].rearrange("p (s h) -> p s h", h=HEADS),
                    xqs[:, dt::2, :].rearrange("p h s -> p s h"))
            last.then_inc(qm_ready, 1)
            dve.wait_ge(kc_used, TS)
            nc.vector.tensor_reduce(small[0:32, 4:5], psum[0:32, 7, 0:MEM], AX.X, ALU.max, negate=True)
            dve.drain()
            nc.vector.tensor_scalar(small[0:32, 0:1], small[0:32, 4:5], 1.0 / 16, None, ALU.mult).then_inc(att_max, 1)
            for g in range(8):
                dve.wait_ge(kv_turned, g + 1)
                nc.vector.tensor_copy(kvtok[:, g % 2, 512 * (g // 2):512 * (g // 2 + 1)],
                                      psum[:, 4 + g % 2, :]).then_inc(kv_tok, 1)
            dve.wait_ge(att_exp, 1)
            nc.vector.reciprocal(small[0:32, 8:9], small[0:32, 8:9])
            dve.drain()
            nc.vector.tensor_scalar(prob_s[:], prob_s[:], small[0:32, 8:9], None, ALU.mult).then_inc(att_prob, 1)

            def maxima(h):
                c = 16 + 16 * (h % 2)
                dve.wait_ge(att_scores, h + 1)
                nc.vector.tensor_reduce(small[:, c + 4:c + 8],
                                        psum[:, 2 * (h % 2):2 * (h % 2) + 2, :].rearrange("p b (u m) -> p (b u) m", m=MEM),
                                        AX.X, ALU.max, negate=True)
                dve.drain()
                nc.vector.tensor_scalar(small[:, c:c + 4], small[:, c + 4:c + 8], 1.0 / 16, None,
                                        ALU.mult).then_inc(att_max, 1)

            def divide(h):
                c = 16 + 16 * (h % 2)
                dve.wait_ge(att_exp, h + 2)
                nc.vector.reciprocal(small[:, c + 8:c + 12], small[:, c + 8:c + 12])
                dve.drain()
                nc.vector.tensor_tensor(prob[:, h % 2], prob[:, h % 2],
                                        small[:, c + 8:c + 12].unsqueeze(2).to_broadcast([P, 4, MEM]),
                                        ALU.mult).then_inc(att_prob, 1)

            maxima(0)
            maxima(1)
            divide(0)
            divide(1)
            dve.wait_ge(br_hi, 1)
            for h in range(HEADS):
                last = nc.vector.tensor_tensor(br2[:, 1, 2 * h:2 * h + 2, TP:TN], samples_out(h),
                                               br2[:, 0, 2 * h:2 * h + 2, TP:TN], ALU.subtract)
            last.then_inc(br_lo, 1)
            for h in range(HEADS):
                if h + 2 < HEADS:
                    maxima(h + 2)
                    divide(h + 2)
                dve.wait_ge(br_hi, h + 2)
                nc.vector.tensor_tensor(br2[:, 1, 2 * h:2 * h + 2, 0:TP], psum[:, 6:8, :],
                                        br2[:, 0, 2 * h:2 * h + 2, 0:TP], ALU.subtract).then_inc(br_lo, 1)

        def merge_loop(eng, n0, n1, body):
            wide = n0 >= N_BA
            with eng.Fori(0, (n1 - n0) // 2) as i:
                for b in range(2):
                    n = n0 + b
                    if wide:
                        m = n + 16
                        o = [(i * 2 + m, m % 2, 0, i * 2 + b, i + (m - N_BC) // 2)]
                    else:
                        m = 2 * n - N_BC
                        o = [(i * 4 + m + j, (m + j) % 2, j * 1024, i * 4 + 2 * b + j, i * 2 + (m + j - N_BC) // 2)
                             for j in range(2)]
                    body(i * 2 + n, n % 2, i + (n - n % 2) // 2, o)

        def sp_merge(sp, n0, n1, gates=(True, True)):
            def body(n, slot, u, outs_):
                load_block(sp, n + 2, slot)
                for m, pair, _, _, _ in outs_:
                    sp.wait_ge(evac_done, m + 1)
                    if gates[slot]:
                        load_gate(sp, m + 2, pair)
            merge_loop(sp, n0, n1, body)

        def act_merge(act, n0, n1):
            def body(n, slot, u, outs_):
                split_hi(act, n + 1, 1 - slot, u + 1 + slot, outs_[0][0])
            merge_loop(act, n0, n1, body)

        def dve_merge(dve, n0, n1, first):
            def body(n, slot, u, outs_):
                split_lo(dve, n + 1, 1 - slot)
                for m, pair, _, j, use in outs_:
                    dve.wait_ge(out_ready, m + 1)
                    dve.wait_ge(gate_landed[pair], (use + 1) * 16)
                    at = merged[:, bass.ds(j, 1), :].rearrange("p a t -> p (a t)")
                    dst = at if first else zst[:, pair, :]
                    nc.vector.tensor_tensor(in_halves(dst), pair_of(pair), in_halves(gt[:, pair, :]),
                                            ALU.mult).then_inc(evac_done, 1)
                    if not first:
                        dve.drain()
                        nc.vector.tensor_tensor(at, at, zst[:, pair, :], ALU.add)
            merge_loop(dve, n0, n1, body)

        def pe_merge(pe, n0, n1, acts, kts, ready=None):
            def body(n, slot, u, outs_, ready=None):
                pe.wait_ge(hi_ready, n + 1)
                pe.wait_ge(lo_ready, n + 1)
                for m, pair, w0, _, _ in outs_:
                    pe.wait_ge(evac_done, m - 1)
                    products(pe, slot, acts, kts, w0, pair, HALF, ready=ready).then_inc(out_ready, 1)
            if ready is not None:
                for n in (n0, n0 + 1):
                    body(n, n % 2, None, [(n + 16, n % 2, 0, n - n0, None)], ready if n == n0 else None)
                n0 += 2
            merge_loop(pe, n0, n1, body)

        def sp_phase0(sp):
            sp.dma_start(memx[:], ins["memT"]).then_inc(mem_loaded, 16)
            sp.dma_start(pcols[:], ins["pcols"]).then_inc(const_loaded, 16)
            load_block(sp, 0, 0)
            load_block(sp, 1, 1)
            sp.dma_start(hx[:], ins["xT"]).then_inc(x_loaded, 16)

        def sp_project(sp):
            for n0, n1, func, ntok in PLAIN:
                if n0 == N_GU:
                    sp_samples_first(sp)
                if n0 == N_R:
                    sp_samples_start(sp)
                def body(n, slot, u, ntok=ntok):
                    load_block(sp, n + 2, slot)
                    sp.wait_ge(evac_done, n + 1)
                    dst = z[bass.ds(n, 1), :, 0:ntok].rearrange("a p t -> (a p) t")
                    sp.dma_start(dst, zst[:, slot, 0:ntok]).then_inc(z_stored[slot], 16)
                if with_units(n0):
                    def both(n, slot, u, s, h, last=n1 == N_UNITS, body=body):
                        body(n, slot, u)
                        sp_unit(sp, n, s, h, last)
                    unit_loop(sp, n0, n1, both)
                elif n0 == N_UNITS:
                    sp.wait_ge(act_lo, 5)
                    sp.wait_ge(st_read, TS * HEADS)
                    sp.dma_start(xqs[:], z[N_XQ:N_Q, :, TP:TN].rearrange("n p t -> p n t")).then_inc(xq_loaded, 16)
                    for stored in st_out:
                        sp.wait_ge(stored, 16 * TS * HEADS // 2)
                    for k in range(8):
                        seg_loop(sp, n0 + 2 * k, n0 + 2 * k + 2, body)
                        cache, landed = ((kcache, kc_landed), (vcache, vc_landed))[k // 4]
                        src = ins[("kcache", "vcache")[k // 4]][k % 4]
                        sp.dma_start(cache[:, k % 4], src).then_inc(landed[k % 4], 16)
                    seg_loop(sp, n0 + 16, n1, body)
                else:
                    seg_loop(sp, n0, n1, body)

        def act_phase0(act):
            act.wait_ge(mem_loaded, 16)
            nc.scalar.activation(sqm[:], memx[:], ACT.Square).then_inc(squares_ready, 1)
            split_hi(act, 0, 0, 1, 0)
            act.wait_ge(root_in, 1)
            nc.scalar.activation(rstd[:, 0:MEM], ssum[:, 0:MEM], ACT.Sqrt).then_inc(root_out, 1)
            act.wait_ge(normed, 1)
            nc.scalar.activation(memr[:, 0], memx[:], ACT.Copy).then_inc(act_hi, 1)

        def act_norm_x(act, n):
            if n == 0:
                act.wait_ge(x_loaded, 16)
            if n < 4:
                nc.scalar.activation(sqx[:, 4 * n:4 * n + 4, :], hx[:, 4 * n:4 * n + 4, :], ACT.Square).then_inc(squares_ready, 1)
            if n == 6:
                act.wait_ge(root_in, 2)
                nc.scalar.activation(rstd[:], ssum[:], ACT.Sqrt).then_inc(root_out, 1)
            if 8 <= n < 12:
                act.wait_ge(normed, 2 + n - 8)
                q = slice(4 * (n - 8), 4 * (n - 8) + 4)
                nc.scalar.activation(actr[:, 0, q, :], hx[:, q, :], ACT.Copy).then_inc(act_hi, 1)

        def act_project(act):
            for n0, n1, func, ntok in PLAIN:
                if n0 == N_R:
                    act_samples_start(act)

                def body(n, slot, u, s=None, h=None, func=func, ntok=ntok, n0=n0):
                    split_hi(act, n + 1, 1 - slot, u + 1 + slot, n)
                    if func == ACT.Sigmoid:
                        nc.scalar.activation(bcur[:, slot:slot + 1], pcols[:, bass.ds(n + (C_BG - N_G), 1)], ACT.Copy)
                        act.drain()
                    if h is not None:
                        act_unit(act, n, s, h)
                    act.wait_ge(out_ready, n + 1)
                    if not isinstance(n, int) or n >= 2:
                        act.wait_ge(z_stored[slot], u * 16)
                    if ntok == MEM:
                        o, i = zst[:, slot, 0:MEM], psum[:, 2 * slot, 0:MEM]
                    else:
                        o, i = in_halves(zst[:, slot, :]), pair_of(slot)
                    bias = bcur[:, slot:slot + 1] if func == ACT.Sigmoid else 0.0
                    nc.scalar.activation(o, i, func, bias=bias).then_inc(evac_done, 1)
                    if h is not None:
                        act_unit_out(act, n, s, h)
                    if n0 == 0:
                        act_norm_x(act, n)
                if n0 == 0:
                    for n in range(n1):
                        body(n, n % 2, n // 2)
                elif with_units(n0):
                    unit_loop(act, n0, n1, body)
                else:
                    seg_loop(act, n0, n1, body)

        def dve_phase0(dve):
            nc.vector.memset(ones[:], 1.0).then_inc(const_made, 1)
            split_lo(dve, 0, 0)
            dve.wait_ge(const_loaded, 16)
            dve.wait_ge(squares_ready, 1)
            nc.vector.tensor_reduce(ssum[:, 0:MEM], sqm[:].rearrange("p k t -> p t k"), AX.X, ALU.add).then_inc(sums_ready, 1)
            dve.wait_ge(spread_ready, 1)
            nc.vector.tensor_scalar(ssum[:, 0:MEM], psum[:, 4, 0:MEM], 1.0 / D, EPS, ALU.mult, ALU.add).then_inc(root_in, 1)
            dve.wait_ge(root_out, 1)
            nc.vector.reciprocal(rstd[:, 0:MEM], rstd[:, 0:MEM])
            dve.drain()
            for kt in range(KT):
                scale_tile(memx, kt, C_MEM, MEM)
            dve.drain().then_inc(normed, 1)
            dve.wait_ge(act_hi, 1)
            nc.vector.tensor_tensor(memr[:, 1], memx[:], memr[:, 0], ALU.subtract).then_inc(act_lo, 1)

        def scale_tile(src, kt, gain, n):
            nc.vector.scalar_tensor_tensor(out=src[:, kt, :], in0=src[:, kt, :], scalar=pcols[:, gain + kt:gain + kt + 1],
                                           in1=rstd[:, 0:n], op0=ALU.mult, op1=ALU.mult)

        def dve_norm_x(dve, n):
            if n in (4, 5):
                dve.wait_ge(squares_ready, 5)
                t = slice((n - 4) * HALF, (n - 3) * HALF)
                nc.vector.tensor_reduce(ssum[:, t], sqx[:, :, t].rearrange("p k t -> p t k"), AX.X, ALU.add).then_inc(sums_ready, 1)
            if n == 6:
                dve.wait_ge(spread_ready, 2)
                nc.vector.tensor_scalar(in_halves(ssum[:]), pair_of(2), 1.0 / D, EPS, ALU.mult, ALU.add).then_inc(root_in, 1)
            if n == 7:
                dve.wait_ge(root_out, 2)
                nc.vector.reciprocal(rstd[:], rstd[:])
                dve.drain()
                dve.wait_ge(act_lo, 1)
            if 8 <= n < 12:
                for kt in range(4 * (n - 8), 4 * (n - 8) + 4):
                    scale_tile(hx, kt, C_MIX, TN)
                dve.drain().then_inc(normed, 1)
            if 9 <= n < 13:
                q = slice(4 * (n - 9), 4 * (n - 9) + 4)
                dve.wait_ge(act_hi, 2 + n - 9)
                nc.vector.tensor_tensor(actr[:, 1, q, :], hx[:, q, :], actr[:, 0, q, :], ALU.subtract).then_inc(act_lo, 1)

        def dve_project(dve):
            for n0, n1, func, ntok in PLAIN:
                if n0 == 0:
                    for n in range(n1):
                        split_lo(dve, n + 1, 1 - n % 2)
                        dve_norm_x(dve, n)
                elif with_units(n0):
                    if n0 == N_R:
                        dve_samples_start(dve)

                    def body(n, slot, u, s, h):
                        split_lo(dve, n + 1, 1 - slot)
                        dve_unit(dve, n, s, h)
                    unit_loop(dve, n0, n1, body)
                else:
                    if n0 == N_GV:
                        dve_samples_first(dve)
                    seg_loop(dve, n0, n1, lambda n, slot, u: split_lo(dve, n + 1, 1 - slot))

        def pe_phase0(pe):
            pe.wait_ge(const_made, 3)
            pe.wait_ge(sums_ready, 1)
            nc.tensor.matmul(psum[:, 4, 0:MEM], ones[:], ssum[:, 0:MEM], start=True, stop=True).then_inc(spread_ready, 1)
            pe.wait_ge(act_hi, 1)
            pe.wait_ge(act_lo, 1)

        def pe_spread(pe, reduced):
            pe.wait_ge(sums_ready, reduced)
            for half in range(2):
                last = nc.tensor.matmul(psum[:, 4 + half, 0:HALF], ones[:], ssum[:, half * HALF:(half + 1) * HALF],
                                        start=True, stop=True)
            last.then_inc(spread_ready, 1)

        def pe_project(pe):
            for n0, n1, func, ntok in PLAIN:
                def body(n, slot, u, ntok=ntok):
                    pe.wait_ge(hi_ready, n + 1)
                    pe.wait_ge(lo_ready, n + 1)
                    if not isinstance(n, int) or n >= 2:
                        pe.wait_ge(evac_done, n - 1)
                    if ntok == MEM:
                        products(pe, slot, memr, range(KT), 0, slot, MEM, 1).then_inc(out_ready, 1)
                    else:
                        products(pe, slot, actr, range(KT), 0, slot, HALF).then_inc(out_ready, 1)
                if n0 == 0:
                    seg_loop(pe, 0, 6, body)
                    pe_spread(pe, 3)
                    seg_loop(pe, 6, N_XQ, body)
                    continue
                if n0 == N_XQ:
                    pe.wait_ge(act_hi, 5)
                    pe.wait_ge(act_lo, 5)
                if n0 == N_GV:
                    pe_samples_first(pe)
                    pe_samples_turn(pe, 0)
                if with_units(n0):
                    if n0 == N_R:
                        pe_samples_turn(pe, 1)

                    def both(n, slot, u, s, h, body=body):
                        body(n, slot, u)
                        pe_unit(pe, n, s, h)
                    unit_loop(pe, n0, n1, both)
                else:
                    seg_loop(pe, n0, n1, body)

        def unit(u):
            return (CH, slice(u * CH, (u + 1) * CH)) if u < NCH else (TS, slice(TP, TN))

        def sp_spatial(sp):
            sp.wait_ge(att_out, HEADS)
            sp.wait_ge(out_stored, 64)
            sp.dma_start(gv[:], z[N_GV:N_R].rearrange("n p t -> p n t")).then_inc(gv_loaded, 16)
            sp.dma_start(gu[:], z[N_GU:N_GV].rearrange("n p t -> p n t")).then_inc(gu_loaded, 16)
            sp.dma_start(lnrow[:, 0, :], ins["ln_g"].partition_broadcast(P)).then_inc(sp_loaded, 16)
            sp.dma_start(lnrow[:, 1, :], ins["ln_b"].partition_broadcast(P)).then_inc(sp_loaded, 16)
            sp.dma_start(wspat[:], ins["w_spatT"]).then_inc(sp_loaded, 16)
            sp.dma_start(bspat[:], ins["b_spat"]).then_inc(sp_loaded, 16)
            sp.dma_start(wfirst[:], ins["w_first"].partition_broadcast(TS)).then_inc(sp_loaded, 16)
            sp.wait_ge(sp_vn, 5)
            sp.dma_start(outs["gmlp_v"], vn[0:TS, 0, :]).then_inc(vn_stored, 16)

        def pool_spatial(pool):
            pool.wait_ge(sp_loaded, 80)
            nc.gpsimd.affine_select(out=wspat[:], in_=wspat[:], pattern=[[0, HEADS], [1, CH]], compare_op=ALU.is_ge,
                                    fill=0.0, base=0, channel_multiplier=-1).then_inc(sp_masked, 1)

        def pe_spatial(pe):
            pe.wait_ge(evac_done, outputs_before(N_BB))
            pe.wait_ge(gv_loaded, 16)

            def turn(u):
                rows, tok = unit(u)
                if u >= 2:
                    pe.wait_ge(sp_vn, u - 1)
                for f in range(8):
                    last = nc.tensor.transpose(psum[0:rows, 2 * (u % 2) + f // 4, (f % 4) * P:(f % 4 + 1) * P],
                                               gv[:, f, tok], ident[:])
                last.then_inc(sp_turned, 1)

            def mix(u):
                rows, tok = unit(u)
                pe.wait_ge(sp_vn, u + 1)
                if u >= 2:
                    pe.wait_ge(sp_gated, u - 1)
                for f in range(8):
                    g = f // 2
                    at = psum[:, 4 + 2 * (u % 2) + f // 4, (f % 4) * P:(f % 4) * P + rows]
                    w = wspat[:, g, :] if u < NCH else wdiag[:, g, :]
                    b = bspat[0:1, g * CH:(g + 1) * CH] if u < NCH else bfirst[0:1, g, :]
                    nc.tensor.matmul(at, vn[0:rows, u % 2, f * P:(f + 1) * P], w, start=True, stop=False)
                    last = nc.tensor.matmul(at, ones[0:1, :], b, start=False, stop=True)
                last.then_inc(sp_mixed, 1)

            turn(0)
            turn(1)
            pe.wait_ge(sp_masked, 2)
            for u in range(NCH + 1):
                mix(u)
                if u + 2 <= NCH:
                    turn(u + 2)

        def act_spatial(act):
            for u in range(NCH + 1):
                rows, tok = unit(u)
                act.wait_ge(root_in, ROOTS_SP + u + 1)
                nc.scalar.activation(small[0:rows, 14:15], small[0:rows, 13:14], ACT.Sqrt).then_inc(root_out, 1)
                if u >= 1:
                    gated_hi(act, u - 1)
            gated_hi(act, NCH)

        def gated_hi(act, u):
            rows, tok = unit(u)
            act.wait_ge(sp_gated, u + 1)
            act.wait_ge(out_ready, outputs_before(N_BB))
            nc.scalar.activation(br2[:, 0, :, tok], gated[:, u % 2, :, 0:rows], ACT.Copy).then_inc(br_hi, 1)

        def dve_spatial(dve):
            dve.wait_ge(sp_loaded, 80)
            nc.vector.tensor_tensor(wdiag[:], ident[0:TS, 0:TS].unsqueeze(1).to_broadcast([TS, HEADS, TS]),
                                    wfirst[:].unsqueeze(2).to_broadcast([TS, HEADS, TS]), ALU.mult)
            nc.vector.tensor_copy(bfirst[:], bspat[:].rearrange("a (g t) -> a g t", t=CH)[:, :, 0:1]
                                  .to_broadcast([1, HEADS, TS]))
            dve.drain().then_inc(sp_masked, 1)

            def norm(u):
                rows, tok = unit(u)
                dve.wait_ge(sp_turned, u + 1)
                src = psum[0:rows, 2 * (u % 2):2 * (u % 2) + 2, :]
                for b in range(2):
                    nc.vector.bn_stats(small[0:rows, 6 * b:6 * b + 6], src[:, b, :])
                dve.drain()
                nc.vector.bn_aggr(small[0:rows, 12:14], small[0:rows, 0:12])
                dve.drain()
                nc.vector.tensor_scalar(small[0:rows, 13:14], small[0:rows, 13:14], EPS, None, ALU.add).then_inc(root_in, 1)
                dve.wait_ge(root_out, ROOTS_SP + u + 1)
                nc.vector.reciprocal(small[0:rows, 15:16], small[0:rows, 14:15])
                dve.drain()
                if u >= 2:
                    dve.wait_ge(sp_mixed, u - 1)
                v = vn[0:rows, u % 2, :]
                nc.vector.tensor_scalar(v.rearrange("p (b f) -> p b f", b=2), src, small[0:rows, 12:13], small[0:rows, 15:16],
                                        ALU.subtract, ALU.mult)
                dve.drain()
                nc.vector.tensor_tensor(v, v, lnrow[0:rows, 0, :], ALU.mult)
                dve.drain()
                nc.vector.tensor_tensor(v, v, lnrow[0:rows, 1, :], ALU.add).then_inc(sp_vn, 1)

            def gate(u):
                rows, tok = unit(u)
                dve.wait_ge(sp_mixed, u + 1)
                if u >= 2:
                    dve.wait_ge(br_hi, 5 + u - 1)
                src = psum[:, 4 + 2 * (u % 2):6 + 2 * (u % 2), :].rearrange("p b (f t) -> p (b f) t", t=P)
                nc.vector.tensor_tensor(gated[:, u % 2, :, 0:rows], src[:, :, 0:rows], gu[:, :, tok],
                                        ALU.mult).then_inc(sp_gated, 1)

            def gated_lo(u):
                rows, tok = unit(u)
                dve.wait_ge(br_hi, 5 + u + 1)
                nc.vector.tensor_tensor(br2[:, 1, :, tok], gated[:, u % 2, :, 0:rows], br2[:, 0, :, tok],
                                        ALU.subtract).then_inc(br_lo, 1)

            dve.wait_ge(gu_loaded, 16)
            norm(0)
            for u in range(NCH + 1):
                if u < NCH:
                    norm(u + 1)
                if u >= 1:
                    gated_lo(u - 1)
                gate(u)
            gated_lo(NCH)

        def rows_of(i):
            return (32, 64, 128, 128)[i]

        def sp_gla(sp):
            sp.wait_ge(out_ready, outputs_before(N_BA))
            sp.wait_ge(vn_stored, 16)
            sp.dma_start(low[:], z[N_LOW, 0:RANK, :]).then_inc(low_loaded, 16)
            sp.dma_start(w_up[:], ins["w_up"]).then_inc(low_loaded, 16)
            sp.dma_start(rs[:], z[N_R:N_G, :, TP:TN].rearrange("n p t -> p n t")).then_inc(samples_loaded, 16)
            sp.wait_ge(br_lo, 10)
            load_chunk(sp, 0, ((qc, N_Q, 8), (kc, N_K, 8)), chunk_loaded)
            load_chunk(sp, 0, ((vc, N_V, 16), (rc, N_R, 16)), vc_loaded)
            sp.wait_ge(o_normed, 1)
            sp.dma_start(bra_dram[:, :, TP:TN], rs[:]).then_inc(chunk_stored, 16)
            for c in range(NCH):
                if c + 1 < NCH:
                    sp.wait_ge(kd_ready, c + 1)
                    sp.wait_ge(sub_ready, 4 * c + 4)
                    sp.wait_ge(qe_ready, c + 2)
                    load_chunk(sp, c + 1, ((qc, N_Q, 8), (kc, N_K, 8)), chunk_loaded)
                if c + 1 < NCH:
                    sp.wait_ge(o_normed, c + 2)
                    sp.dma_start(bra_dram[:, :, c * CH:(c + 1) * CH], rc[:]).then_inc(chunk_stored, 16)
                    sp.wait_ge(chunk_stored, 16 * (c + 2))
                    load_chunk(sp, c + 1, ((vc, N_V, 16), (rc, N_R, 16)), vc_loaded)
            sp.wait_ge(state_done, NCH)
            for t in (slice(0, TP - CH), slice(TP, TN)):
                sp.dma_start(bra[:, :, t], bra_dram[:, :, t]).then_inc(bra_loaded, 16)
            sp.dma_start(outs["gla_p"].rearrange("h (k p) v -> p (h k) v", p=P), state[:]).then_inc(state_stored, 16)

        def load_chunk(sp, c, what, loaded):
            t = slice(c * CH, (c + 1) * CH)
            for dst, n, k in what:
                sp.dma_start(dst[:], z[n:n + k, :, t].rearrange("n p t -> p n t")).then_inc(loaded, 16)

        def pool_gla(pool):
            pool.wait_ge(br_lo, 10)
            nc.gpsimd.memset(keep[:], 1.0)
            nc.gpsimd.memset(state[:], 0.0)
            pool.drain()
            nc.gpsimd.memset(keep[:].rearrange("p (c t) -> p c t", t=CH)[:, :, 0:1], 0.0).then_inc(keep_made, 1)
            pool.wait_ge(bcum_ready, 1)
            for c in range(NCH):
                b = bcum[:, :, c * CH:(c + 1) * CH]
                if c > 0:
                    pool.wait_ge(kd_turned, c)
                nc.gpsimd.tensor_tensor(kd[:], b[:, :, CH - 1:CH].to_broadcast([P, 8, CH]), b,
                                        ALU.subtract).then_inc(kd_in, 1)
                pool.wait_ge(vc_loaded, 32 * (c + 1))
                nc.gpsimd.tensor_tensor(rc[:], rc[:], pcols[:, C_GLA:C_GLA + KT].unsqueeze(2).to_broadcast([P, KT, CH]),
                                        ALU.mult).then_inc(rc_gained, 1)

        def pe_gla(pe):
            pe.wait_ge(evac_done, outputs_before(N_BA))
            pe.wait_ge(low_loaded, 64)
            for f in range(8):
                if f >= 4:
                    pe.wait_ge(up_read, f - 3)
                for half in range(2):
                    last = nc.tensor.matmul(psum[:, 2 * (f % 4) + half, 0:HALF], w_up[:, f * P:(f + 1) * P],
                                            low[:, half * HALF:(half + 1) * HALF], start=True, stop=True)
                last.then_inc(up_ready, 1)
            pe.wait_ge(up_read, 8)
            pe.wait_ge(squares_ready, SQUARES_GLA + 1)
            for h in range(HEADS):
                for j in range(4):
                    last = nc.tensor.matmul(psum[:, 7, h * TS:(h + 1) * TS], ones[:], sqs[:, 4 * h + j, :],
                                            start=(j == 0), stop=(j == 3))
            last.then_inc(o_summed, 1)
            for c in range(NCH):
                for i in range(4):
                    rows = rows_of(i)
                    pe.wait_ge(sub_ready, 4 * c + i + 1)
                    if i == 0 and c > 0:
                        pe.wait_ge(sc_ready, c)
                    for h in range(HEADS):
                        for dt in range(2):
                            last = nc.tensor.matmul(psum[0:rows, 4, h * CH + i * SUB:h * CH + (i + 1) * SUB],
                                                    ki[:, i % 2, 2 * h + dt, 0:rows], qi[:, i % 2, 2 * h + dt, :],
                                                    start=(dt == 0), stop=(dt == 1))
                    last.then_inc(sub_scored, 1)
                pe.wait_ge(kd_ready, c + 1)
                if c > 0:
                    pe.wait_ge(state_done, c)
                for f in range(8):
                    last = nc.tensor.transpose(psum[:, 5 + f // 4, (f % 4) * P:(f % 4 + 1) * P], kd[:, f, :], ident[:])
                last.then_inc(kd_turned, 1)
                pe.wait_ge(vc_loaded, 32 * (c + 1))
                if c > 0:
                    pe.wait_ge(o_read, c)
                for f in range(KT):
                    last = nc.tensor.transpose(psum[:, f // 4, (f % 4) * P:(f % 4 + 1) * P], vc[:, f, :], ident[:])
                last.then_inc(v_turned, 1)
                pe.wait_ge(sc_ready, c + 1)
                pe.wait_ge(qe_ready, c + 2)
                pe.wait_ge(v_tok, c + 3)
                for h in range(HEADS):
                    for j in range(4):
                        at = psum[:, h, j * P:(j + 1) * P]
                        nc.tensor.matmul(at, vtok[:, h * DV + j * P:h * DV + (j + 1) * P], scores_t[:, h, :],
                                         start=True, stop=False)
                        for dt in range(2):
                            last = nc.tensor.matmul(at, state[:, 2 * h + dt, j * P:(j + 1) * P],
                                                    qe[:, 2 * h + dt, :], start=False, stop=(dt == 1))
                last.then_inc(o_ready, 1)
                pe.wait_ge(kd_tok, c + 1)
                for f in range(8):
                    if f >= 2:
                        pe.wait_ge(kv_read, 8 * c + f - 1)
                    nc.tensor.matmul(psum[:, 5 + f % 2, :], kdtok[:, f * P:(f + 1) * P],
                                     vtok[:, (f // 2) * DV:(f // 2 + 1) * DV], start=True, stop=True).then_inc(kv_ready, 1)
                pe.wait_ge(squares_ready, SQUARES_GLA + c + 2)
                pe.wait_ge(root_in, ROOTS_GLA + c + 1)
                for h in range(HEADS):
                    for j in range(4):
                        last = nc.tensor.matmul(psum[:, 7, h * CH:(h + 1) * CH], ones[:], vc[:, 4 * h + j, :],
                                                start=(j == 0), stop=(j == 3))
                last.then_inc(o_summed, 1)

        def act_gla(act):
            nc.scalar.activation(sqs[:], os_[:], ACT.Square).then_inc(squares_ready, 1)
            for k in range(2):
                act.wait_ge(gx_ready, 3 + k)
                nc.scalar.activation(gy[:, 4 * k:4 * k + 4], gx[:, 4 * k:4 * k + 4], ACT.Abs)
            act.drain()
            for k in range(2):
                nc.scalar.activation(gy[:, 4 * k:4 * k + 4], gy[:, 4 * k:4 * k + 4], ACT.Exp, scale=-1.0)
            act.drain()
            for k in range(2):
                nc.scalar.activation(gy[:, 4 * k:4 * k + 4], gy[:, 4 * k:4 * k + 4], ACT.Ln, bias=1.0).then_inc(gy_ready, 1)
            act.wait_ge(root_in, ROOTS_GLA + 1)
            nc.scalar.activation(norm_s[:], norm_s[:], ACT.Sqrt).then_inc(root_out, 1)
            act.wait_ge(bcum_ready, 1)

            def sub_exps(c, i):
                act.wait_ge(sub_in, 4 * c + i + 1)
                nc.scalar.activation(qi[:, i % 2], qi[:, i % 2], ACT.Exp, scale=1.0 / GATE_NORM)
                nc.scalar.activation(ki[:, i % 2, :, 0:rows_of(i)], ki[:, i % 2, :, 0:rows_of(i)], ACT.Exp,
                                     scale=1.0 / GATE_NORM).then_inc(sub_exp, 1)

            def exps_ahead(c):
                sub_exps(c, 0)
                sub_exps(c, 1)
                act.wait_ge(kd_in, c + 1)
                nc.scalar.activation(kd[:], kd[:], ACT.Exp, scale=1.0 / GATE_NORM).then_inc(kd_exp, 1)

            exps_ahead(0)
            for c in range(NCH):
                t = slice(c * CH, (c + 1) * CH)
                if c > 0:
                    act.wait_ge(qe_ready, c + 1)
                    act.wait_ge(state_done, c)
                nc.scalar.activation(eb[:], bcum[:, :, t], ACT.Exp, scale=1.0 / GATE_NORM).then_inc(eb_ready, 1)
                sub_exps(c, 2)
                sub_exps(c, 3)
                act.wait_ge(kd_turned, c + 1)
                nc.scalar.activation(kdtok[:].rearrange("p (b f) -> p b f", b=2), psum[:, 5:7, :], ACT.Copy).then_inc(kd_tok, 1)
                act.wait_ge(v_turned, c + 3)
                if c > 0:
                    act.wait_ge(kv_ready, 8 * c)
                nc.scalar.activation(vtok[:].rearrange("p (b f) -> p b f", b=4), psum[:, 0:4, :], ACT.Copy).then_inc(v_tok, 1)
                if c + 1 < NCH:
                    exps_ahead(c + 1)
                act.wait_ge(o_ready, c + 1)
                nc.scalar.activation(vc[:].rearrange("p (h j) t -> p h (j t)", h=4), psum[:, 0:4, :],
                                     ACT.Square).then_inc(squares_ready, 1)
                act.wait_ge(root_in, ROOTS_GLA + c + 2)
                nc.scalar.activation(norm_a[:], norm_a[:], ACT.Sqrt).then_inc(root_out, 1)

        def dve_gla(dve):
            for f in range(8):
                dve.wait_ge(up_ready, f + 2)
                nc.vector.tensor_scalar(in_halves(gx[:, f, :]), pair_of(f % 4), pcols[:, C_BA + f:C_BA + f + 1], None,
                                        ALU.add).then_inc(up_read, 1)
                if f % 4 == 3:
                    dve.drain().then_inc(gx_ready, 1)
            dve.wait_ge(samples_loaded, 80)
            nc.vector.tensor_tensor(rs[:], rs[:], pcols[:, C_GLA:C_GLA + KT].unsqueeze(2).to_broadcast([P, KT, TS]), ALU.mult)
            dve.wait_ge(keep_made, 1)
            for k in range(2):
                dve.wait_ge(gy_ready, 2 + k)
                q = slice(4 * k, 4 * k + 4)
                nc.vector.scalar_tensor_tensor(out=gx[:, q], in0=gx[:, q], scalar=0.0, in1=gy[:, q], op0=ALU.min,
                                               op1=ALU.subtract)
                dve.drain()
                for f in range(4 * k, 4 * k + 4):
                    nc.vector.tensor_tensor_scan(bcum[:, f, 0:TP], keep[:], gx[:, f, 0:TP], 0.0, ALU.mult, ALU.add)
            dve.drain().then_inc(bcum_ready, 1)
            dve.wait_ge(o_summed, 1)
            nc.vector.tensor_scalar(norm_s[:], psum[:, 7, 0:HEADS * TS].rearrange("p (h t) -> p h t", h=HEADS), 1.0 / DV, EPS,
                                    ALU.mult, ALU.add).then_inc(root_in, 1)
            dve.wait_ge(root_out, ROOTS_GLA + 1)
            nc.vector.reciprocal(norm_s[:], norm_s[:])
            dve.drain()
            nc.vector.tensor_tensor(sqs[:].rearrange("p (h j) s -> p h j s", h=HEADS),
                                    os_[:].rearrange("p (h j) s -> p h j s", h=HEADS),
                                    norm_s[:].unsqueeze(2).to_broadcast([P, HEADS, 4, TS]), ALU.mult)
            dve.drain()
            nc.vector.tensor_tensor(rs[:], rs[:], sqs[:], ALU.mult).then_inc(o_normed, 1)
            nc.vector.memset(scores_t[:], 0.0)
            dve.drain()

            def sub_exponents(c, i):
                rows, t0 = rows_of(i), c * CH
                mid = bcum[:, :, t0 + i * SUB + SUB // 2 - 1:t0 + i * SUB + SUB // 2]
                if 4 * c + i >= 2:
                    dve.wait_ge(sub_scored, 4 * c + i - 1)
                nc.vector.tensor_tensor(qi[:, i % 2], bcum[:, :, t0 + i * SUB:t0 + (i + 1) * SUB],
                                        mid.to_broadcast([P, 8, SUB]), ALU.subtract)
                nc.vector.tensor_tensor(ki[:, i % 2, :, 0:rows], mid.to_broadcast([P, 8, rows]),
                                        bcum[:, :, t0:t0 + rows], ALU.subtract)
                dve.drain().then_inc(sub_in, 1)

            def sub_products(c, i):
                rows = rows_of(i)
                dve.wait_ge(sub_exp, 4 * c + i + 1)
                nc.vector.scalar_tensor_tensor(out=qi[:, i % 2], in0=qi[:, i % 2], scalar=CLAMP,
                                               in1=qc[:, :, i * SUB:(i + 1) * SUB], op0=ALU.min, op1=ALU.mult)
                nc.vector.scalar_tensor_tensor(out=ki[:, i % 2, :, 0:rows], in0=ki[:, i % 2, :, 0:rows], scalar=CLAMP,
                                               in1=kc[:, :, 0:rows], op0=ALU.min, op1=ALU.mult)
                dve.drain().then_inc(sub_ready, 1)

            def products_ahead(c):
                dve.wait_ge(chunk_loaded, 32 * (c + 1))
                sub_products(c, 0)
                sub_products(c, 1)
                dve.wait_ge(kd_exp, c + 1)
                nc.vector.tensor_tensor(kd[:], kd[:], kc[:], ALU.mult).then_inc(kd_ready, 1)

            sub_exponents(0, 0)
            sub_exponents(0, 1)
            products_ahead(0)
            for c in range(NCH):
                dve.wait_ge(eb_ready, c + 1)
                if c > 0:
                    dve.wait_ge(o_ready, c)
                nc.vector.scalar_tensor_tensor(out=qe[:], in0=qc[:], scalar=DK ** -0.5, in1=eb[:], op0=ALU.mult,
                                               op1=ALU.mult).then_inc(qe_ready, 1)
                sub_exponents(c, 2)
                sub_exponents(c, 3)
                sub_products(c, 2)
                sub_products(c, 3)
                dve.wait_ge(sub_scored, 4 * c + 4)
                for i in range(4):
                    rows = rows_of(i)
                    sl = slice(i * SUB, (i + 1) * SUB)
                    nc.vector.tensor_tensor(scores_t[0:rows, :, sl],
                                            psum[0:rows, 4, :].rearrange("p (h t) -> p h t", h=HEADS)[:, :, sl],
                                            tri[0:rows, sl].unsqueeze(1).to_broadcast([rows, HEADS, SUB]), ALU.mult)
                dve.drain().then_inc(sc_ready, 1)
                if c + 1 < NCH:
                    sub_exponents(c + 1, 0)
                    sub_exponents(c + 1, 1)
                dve.wait_ge(o_ready, c + 1)
                for f in range(8):
                    dve.wait_ge(kv_ready, 8 * c + f + 1)
                    nc.vector.scalar_tensor_tensor(out=state[:, f, :], in0=state[:, f, :], scalar=eb[:, f, CH - 1:CH],
                                                   in1=psum[:, 5 + f % 2, :], op0=ALU.mult, op1=ALU.add).then_inc(kv_read, 1)
                dve.drain().then_inc(state_done, 1)
                if c + 1 < NCH:
                    products_ahead(c + 1)
                dve.wait_ge(o_summed, c + 2)
                nc.vector.tensor_scalar(norm_a[:], psum[:, 7, :].rearrange("p (h t) -> p h t", h=HEADS), 1.0 / DV, EPS,
                                        ALU.mult, ALU.add).then_inc(root_in, 1)
                dve.wait_ge(root_out, ROOTS_GLA + c + 2)
                nc.vector.reciprocal(norm_a[:], norm_a[:])
                dve.drain()
                v4 = vc[:].rearrange("p (h j) t -> p h j t", h=HEADS)
                nc.vector.tensor_tensor(v4, psum[:, 0:4, :].rearrange("p h (j t) -> p h j t", j=4),
                                        norm_a[:].unsqueeze(2).to_broadcast([P, HEADS, 4, CH]), ALU.mult).then_inc(o_read, 1)
                dve.drain()
                dve.wait_ge(rc_gained, c + 1)
                dst = rc[:] if c + 1 < NCH else bra[:, :, c * CH:(c + 1) * CH]
                nc.vector.tensor_tensor(dst, rc[:], vc[:], ALU.mult).then_inc(o_normed, 1)

        def act_wide(act, src):
            for q in range(4):
                nc.scalar.activation(actr[:, 0, 4 * q:4 * q + 4, :], src[:, 4 * q:4 * q + 4, :], ACT.Copy).then_inc(act_hi, 1)

        def dve_wide(dve, src, k):
            for q in range(4):
                dve.wait_ge(act_hi, k + q + 1)
                nc.vector.tensor_tensor(actr[:, 1, 4 * q:4 * q + 4, :], src[:, 4 * q:4 * q + 4, :],
                                        actr[:, 0, 4 * q:4 * q + 4, :], ALU.subtract).then_inc(act_lo, 1)

        def wide_loop(eng, n0, n1, body):
            assert n0 % 2 == 1 and (n1 - n0) % 2 == 0
            with eng.Fori(0, (n1 - n0) // 2) as i:
                for b in range(2):
                    n = n0 + b
                    body(i * 2 + n, n % 2, i + (n - n % 2) // 2, i * 2 + n + 16, i * 2 + b)

        def sp_out(sp):
            sp.wait_ge(act_lo, 9)
            sp.dma_start(x1[:], ins["xT"]).then_inc(x1_loaded, 16)
            wide_loop(sp, N_OUT, N_WQ, lambda n, slot, u, m, j: load_block(sp, n + 2, slot))
            for u in range(NCH + 1):
                rows, tok = unit(u)
                sp.wait_ge(x1_staged, u + 1)
                sp.dma_start(x1_dram[tok, :], stage_x[u % 2][0:rows, :]).then_inc(x1_stored[u % 2], 16)
            wide_loop(sp, N_WQ, N_END - 2, lambda n, slot, u, m, j: load_block(sp, n + 2, slot))
            sp.wait_ge(x1_stored[0], 48)
            sp.wait_ge(x1_stored[1], 32)
            sp.dma_start(keys[:], ins["keys"]).then_inc(keys_loaded, 16)
            for u in range(1, NCH + 1):
                rows, tok = unit(u)
                sp.wait_ge(sc_staged, u + 1)
                sp.dma_start(sc_dram[u * P:u * P + rows, :], stage_s[u % 2][0:rows, :]).then_inc(sc_stored[u % 2], 16)
                if u == 2:
                    sp.dma_start(sc_dram[NCH * P + TS:(NCH + 1) * P, :], stage_s[0][TS:P, :]).then_inc(sc_stored[0], 16)
            for u in range(NCH + 1):
                rows, tok = unit(u)
                sp.wait_ge(h2_staged, u + 1)
                sp.dma_start(h2_dram[tok, :], stage_h[u % 2][0:rows, :]).then_inc(h2_stored[u % 2], 16)
            for k in range(2):
                sp.wait_ge(sc_stored[k], X1_STORES[k] + 16 * (3 - k))
                sp.wait_ge(h2_stored[k], 16 * (3 - k))

        def act_out(act):
            act.wait_ge(merged_ready, 1)
            act.wait_ge(out_ready, N_OUT + 16)
            act_wide(act, merged)
            wide_loop(act, N_OUT, N_WQ, lambda n, slot, u, m, j: split_hi(act, n + 1, 1 - slot, u + 1 + slot, m))
            act.wait_ge(x1_ready, 1)
            act.wait_ge(root_in, ROOTS_X1 + 1)
            nc.scalar.activation(rstd[:], ssum[:], ACT.Sqrt).then_inc(root_out, 1)
            for u in range(NCH + 1):
                rows, tok = unit(u)
                act.wait_ge(x1_turned, u + 1)
                if u >= 2:
                    act.wait_ge(x1_stored[u % 2], 16 * (u // 2))
                nc.scalar.activation(stage_x[u % 2][0:rows, :].rearrange("p (b f) -> p b f", b=4), psum[0:rows, 0:4, :],
                                     ACT.Copy).then_inc(x1_staged, 1)
                if u >= 1:
                    q = u - 1
                    act.wait_ge(out_ready, N_WQ + 16)
                    act.wait_ge(normed, 6 + q)
                    nc.scalar.activation(actr[:, 0, 4 * q:4 * q + 4, :], h2[:, 4 * q:4 * q + 4, :], ACT.Copy).then_inc(act_hi, 1)
            def evac(slot, m, j):
                act.wait_ge(out_ready, m + 1)
                dst = pq[:, bass.ds(j, 1), :].rearrange("p a t -> p (a t)")
                nc.scalar.activation(in_halves(dst), pair_of(m_pair(slot)), ACT.Copy).then_inc(evac_done, 1)

            def body(n, slot, u, m, j):
                split_hi(act, n + 1, 1 - slot, u + 1 + slot, m)
                evac(slot, m, j)
            wide_loop(act, N_WQ, N_END - 2, body)
            split_hi(act, N_END - 1, (N_END - 1) % 2, (N_END - 1 - (N_END - 1) % 2) // 2 + 1, N_END - 2 + 16)
            evac((N_END - 2) % 2, N_END - 2 + 16, 14)
            evac((N_END - 1) % 2, N_END - 1 + 16, 15)
            act.drain().then_inc(pq_ready, 1)
            for u in range(NCH + 1):
                rows, tok = unit(u)
                act.wait_ge(scored, u + 1)
                if u >= 3:
                    act.wait_ge(sc_stored[u % 2], X1_STORES[u % 2] + (16 if u == 3 else 32))
                dst = stage_s[u % 2][0:rows, :] if u > 0 else sc[:].rearrange("p h a k -> p (h a k)")
                nc.scalar.activation(dst.rearrange("p (b f) -> p b f", b=4),
                                     psum[0:rows, 4 * (u % 2):4 * (u % 2) + 4, :], ACT.Copy).then_inc(sc_staged, 1)
            for u in range(NCH + 1):
                rows, tok = unit(u)
                act.wait_ge(h2_turned, u + 1)
                if u >= 2:
                    act.wait_ge(h2_stored[u % 2], 16 * (u // 2))
                nc.scalar.activation(stage_h[u % 2][0:rows, :].rearrange("p (b f) -> p b f", b=4),
                                     psum[0:rows, 4 * ((u + 1) % 2):4 * ((u + 1) % 2) + 4, :], ACT.Copy).then_inc(h2_staged, 1)

        def m_pair(slot):
            return slot

        def dve_out(dve):
            dve_wide(dve, merged, 9)
            dve.wait_ge(x1_loaded, 16)

            def body(n, slot, u, m, j):
                split_lo(dve, n + 1, 1 - slot)
                dve.wait_ge(out_ready, m + 1)
                at = x1[:, bass.ds(j, 1), :].rearrange("p a t -> p (a t)")
                nc.vector.tensor_tensor(in_halves(at), pair_of(m_pair(slot)), in_halves(at), ALU.add).then_inc(evac_done, 1)
                dve.drain()
                nc.vector.tensor_tensor(sq2[:], at, at, ALU.mult)
                dve.drain()
                nc.vector.tensor_tensor(ssum[:], ssum[:], sq2[:], ALU.add)
            nc.vector.memset(ssum[:], 0.0)
            dve.drain()
            wide_loop(dve, N_OUT, N_WQ, body)
            dve.drain().then_inc(sums_ready, 1)
            dve.drain().then_inc(x1_ready, 1)
            dve.wait_ge(spread_ready, 3)
            nc.vector.tensor_scalar(in_halves(ssum[:]), pair_of(2), 1.0 / D, EPS, ALU.mult, ALU.add).then_inc(root_in, 1)
            dve.wait_ge(root_out, ROOTS_X1 + 1)
            nc.vector.reciprocal(rstd[:], rstd[:])
            dve.drain()
            for q in range(4):
                for kt in range(4 * q, 4 * q + 4):
                    nc.vector.scalar_tensor_tensor(out=h2[:, kt, :], in0=x1[:, kt, :], scalar=pcols[:, C_FFN + kt:C_FFN + kt + 1],
                                                   in1=rstd[:], op0=ALU.mult, op1=ALU.mult)
                dve.drain().then_inc(normed, 1)
            dve_wide(dve, h2, 13)
            wide_loop(dve, N_WQ, N_END - 2, lambda n, slot, u, m, j: split_lo(dve, n + 1, 1 - slot))
            split_lo(dve, N_END - 1, (N_END - 1) % 2)

        def pe_out(pe):
            def body(n, slot, u, m, j, ready=None):
                pe.wait_ge(hi_ready, n + 1)
                pe.wait_ge(lo_ready, n + 1)
                pe.wait_ge(evac_done, m - 1)
                products(pe, slot, actr, range(KT), 0, m_pair(slot), HALF, ready=ready).then_inc(out_ready, 1)
            body(N_OUT, N_OUT % 2, None, N_OUT + 16, 0, ready=lambda kt: wait_piece(pe, kt, 9))
            body(N_OUT + 1, (N_OUT + 1) % 2, None, N_OUT + 17, 1)
            wide_loop(pe, N_OUT + 2, N_WQ, body)
            pe.wait_ge(x1_ready, 1)
            pe_spread(pe, 4)
            turn_units(pe, x1, 0, x1_turned, x1_staged)
            pe.wait_ge(x1_staged, NCH + 1)
            body(N_WQ, N_WQ % 2, None, N_WQ + 16, 0, ready=lambda kt: wait_piece(pe, kt, 13))
            body(N_WQ + 1, (N_WQ + 1) % 2, None, N_WQ + 17, 1)
            wide_loop(pe, N_WQ + 2, N_END, body)
            pe.wait_ge(keys_loaded, 16)
            pe.wait_ge(pq_ready, 1)
            for u in range(NCH + 1):
                rows, tok = unit(u)
                if u >= 2:
                    pe.wait_ge(sc_staged, u - 1)
                for c in range(KT):
                    last = nc.tensor.matmul(psum[0:rows, 4 * (u % 2) + c // 4, (c % 4) * P:(c % 4 + 1) * P],
                                            pq[:, c, tok], keys[:, c // 2, c % 2, :], start=True, stop=True)
                last.then_inc(scored, 1)
            turn_units(pe, h2, 1, h2_turned, h2_staged)

        def turn_units(pe, src, two, turned, staged):
            for u in range(NCH + 1):
                rows, tok = unit(u)
                b0 = 4 * ((u + 1) % 2) if two else 0
                if two:
                    if u < 2:
                        pe.wait_ge(sc_staged, NCH + u)
                    else:
                        pe.wait_ge(staged, u - 1)
                elif u >= 1:
                    pe.wait_ge(staged, u)
                for f in range(KT):
                    last = nc.tensor.transpose(psum[0:rows, b0 + f // 4, (f % 4) * P:(f % 4 + 1) * P], src[:, f, tok], ident[:])
                last.then_inc(turned, 1)

        def top_head(dve, k, to_idx=True):
            for a in range(2):
                nc.vector.max(top_v[:, a, 0:8], sc[:, k, a, :])
            dve.drain()
            for a in range(2):
                nc.vector.max_index(top_i[:, a, 0:8], top_v[:, a, 0:8], sc[:, k, a, :])
                nc.vector.match_replace(rest[:, a, :], top_v[:, a, 0:8], sc[:, k, a, :], -3.0e38)
            dve.drain()
            for a in range(2):
                nc.vector.max(top_v[:, a, 8:16], rest[:, a, :])
            dve.drain()
            for a in range(2):
                nc.vector.max_index(top_i[:, a, 8:16], top_v[:, a, 8:16], rest[:, a, :])
            nc.vector.tensor_tensor(cand[:], top_v[:, 0, :].unsqueeze(2).to_broadcast([P, TOP, TOP]),
                                    top_v[:, 1, :].unsqueeze(1).to_broadcast([P, TOP, TOP]), ALU.add)
            dve.drain()
            c1, c2 = (c[:].rearrange("p a b -> p (a b)") for c in (cand, cand2))
            best = gate_next[:, k, :]
            nc.vector.tensor_copy(top_if[:], top_i[:])
            nc.vector.max(best[:, 0:8], c1)
            dve.drain()
            nc.vector.max_index(pos[:, 0:8], best[:, 0:8], c1)
            nc.vector.match_replace(c2, best[:, 0:8], c1, -3.0e38)
            dve.drain()
            nc.vector.max(best[:, 8:16], c2)
            dve.drain()
            nc.vector.max_index(pos[:, 8:16], best[:, 8:16], c2)
            dve.drain()
            nc.vector.tensor_scalar(pos2[:, 0, :], pos[:], 4, None, ALU.logical_shift_right)
            nc.vector.tensor_scalar(pos2[:, 1, :], pos[:], 15, None, ALU.bitwise_and)
            dve.drain()
            nc.vector.tensor_copy(pos_f[:], pos2[:])
            dve.drain()
            for a in range(2):
                nc.vector.tensor_tensor(hot[:, a], pos_f[:, a, :].unsqueeze(2).to_broadcast([P, TOP, TOP]),
                                        iota_f[:].unsqueeze(1).to_broadcast([P, TOP, TOP]), ALU.is_equal)
            dve.drain()
            for a in range(2):
                nc.vector.tensor_tensor(hot[:, a], hot[:, a], top_if[:, a, :].unsqueeze(1).to_broadcast([P, TOP, TOP]), ALU.mult)
            dve.drain()
            for a in range(2):
                nc.vector.tensor_reduce(e_f[:, a, :], hot[:, a], AX.X, ALU.add)
            dve.drain()
            nc.vector.scalar_tensor_tensor(out=idx_next[:, k * TOP:(k + 1) * TOP], in0=e_f[:, 0, :], scalar=float(NK),
                                           in1=e_f[:, 1, :], op0=ALU.mult, op1=ALU.add)
            dve.drain()

        def top_softmax(dve, count):
            nc.vector.tensor_copy(sums[:, 8:16], gate_next[:, :, 0])
            dve.drain()
            nc.vector.tensor_tensor(gate_next[:], gate_next[:], sums[:, 8:16].unsqueeze(2).to_broadcast([P, PH, TOP]),
                                    ALU.subtract).then_inc(soft_in, 1)
            dve.wait_ge(soft_exp, count)
            nc.vector.tensor_reduce(sums[:, 0:8], gate_next[:], AX.X, ALU.add)
            dve.drain()
            nc.vector.reciprocal(sums[:, 0:8], sums[:, 0:8])
            dve.drain()
            nc.vector.tensor_tensor(gate_next[:], gate_next[:], sums[:, 0:8].unsqueeze(2).to_broadcast([P, PH, TOP]), ALU.mult)
            dve.drain()

        def sp_peer(sp):
            sp.sem_inc(y_stored, 16)

            def tile(t, first=False, last=False):
                sp.wait_ge(u_used, t * SLOTS + RING)
                sp.dma_start(htok[:], h2_dram[bass.ds(t * P, P), :]).then_inc(htok_loaded, 16)
                sp.wait_ge(y_ready, t + 1)
                sp.dma_start(acc[:], x1_dram[bass.ds(t * P, P), :]).then_inc(acc_loaded, 16)
                if first:
                    sp.dma_start(gfin[:], ins["g_final"].partition_broadcast(P)).then_inc(gfin_loaded, 16)
                sp.wait_ge(sc_used, t + 1)
                sp.dma_start(sc[:], sc_dram[bass.ds(t * P + P, P), :].rearrange("t (h a k) -> t h a k", h=PH, a=2)) \
                  .then_inc(sc_loaded, 16)
                if last:
                    samples_experts()
                sp.wait_ge(y_ready, t + 2)
                sp.dma_start(outs["y_prompt"][bass.ds(t * P, P), :], yout[:]).then_inc(y_stored, 16)

            def samples_experts():
                sp.wait_ge(idx_ready, PH + 2 * NCH - 1)
                sp.dma_start(idx_dram[:], idx_next[0:TS, :]).then_inc(packed, 16)
                sp.dma_start(gate_dram[:], gate_next[0:TS, :, :].rearrange("p h j -> p (h j)")).then_inc(packed, 16)
                sp.wait_ge(packed, 32)
                sp.dma_start(idx_s[:], idx_dram.rearrange("s (g j) -> (s g) j", j=TS)).then_inc(unpacked, 16)
                sp.dma_start(gate_s[:], gate_dram.rearrange("s (g j) -> (s g) j", j=TS)).then_inc(unpacked, 16)
                sp.wait_ge(u_used, NCH * SLOTS + RING)
                for s in range(TS):
                    sp.dma_start(htok[s * 16:(s + 1) * 16, :], h2_dram[TP + s, :].partition_broadcast(16)).then_inc(unpacked, 16)

            tile(0, first=True)
            with sp.Fori(1, NCH - 1) as t:
                tile(t)
            tile(NCH - 1, last=True)
            sp.dma_start(htok2[:], x1_dram[TP:TN, :]).then_inc(acc_s_loaded, 16)
            sp.wait_ge(y_ready, NCH + 2)
            sp.dma_start(outs["y_sample"], yout[0:TS, :]).then_inc(y_stored, 16)
            sp.wait_ge(y_stored, 16 * (NCH + 2))

        def pool_peer_constants(pool):
            pool.wait_ge(out_ready, N_OUT + 16)
            nc.gpsimd.iota(iota_u[:], pattern=[[1, TOP]], base=0, channel_multiplier=0)
            nc.gpsimd.memset(sel[:], 1.0)
            pool.drain()
            nc.gpsimd.tensor_copy(iota_f[:], iota_u[:])
            nc.gpsimd.affine_select(out=sel[:], in_=sel[:], pattern=[[-16, TS]], compare_op=ALU.is_ge, fill=0.0, base=0,
                                    channel_multiplier=1)
            pool.drain()
            nc.gpsimd.affine_select(out=sel[:], in_=sel[:], pattern=[[16, TS]], compare_op=ALU.is_ge, fill=0.0, base=15,
                                    channel_multiplier=-1)
            pool.drain().then_inc(peer_made, 1)

        def gather(ring, table, col, landed):
            nc.gpsimd.sem_inc(slots_granted, 1)
            return nc.gpsimd.indirect_dma_start(ring[:], None, ins[table], bass.IndirectOffsetOnAxis(ap=col, axis=0)) \
                     .then_inc(landed, 16)

        def pool_peer(pool):
            pool.wait_ge(out_ready, N_END + 16)
            for n in range(SLOTS):
                if n % TOP == 0:
                    pool.wait_ge(idx_ready, n // TOP + 1)
                pool.wait_ge(u_used, n + 1)
                gather(u_ring[n % RING], "peer_u", idx_cur[:, n:n + 1], u_landed[n % RING])
            pool.wait_ge(h2_staged, NCH + 1)
            for n in range(SLOTS):
                pool.wait_ge(v_used, n + 1)
                gather(v_ring[n % RING], "peer_v", idx_cur[:, n:n + 1], v_landed[n % RING])
            with pool.Fori(1, NCH) as t:
                pool.wait_ge(idx_ready, t * 2 + (PH - 1))
                for k in range(PH + 1):
                    if k == PH - 1:
                        pool.wait_ge(idx_ready, t * 2 + PH)
                    for j in range(TOP):
                        if k < PH:
                            n = k * TOP + j
                            pool.wait_ge(u_used, t * SLOTS + (n + 1))
                            gather(u_ring[n % RING], "peer_u", idx_cur[:, n:n + 1], u_landed[n % RING])
                        if k > 0:
                            n = (k - 1) * TOP + j
                            pool.wait_ge(v_used, t * SLOTS + (n + 1))
                            gather(v_ring[n % RING], "peer_v", idx_cur[:, n:n + 1], v_landed[n % RING])
            pool.wait_ge(unpacked, 16 * (2 + TS))
            for table, ring, used, landed in (("peer_u", u_ring, u_used, u_landed), ("peer_v", v_ring, v_used, v_landed)):
                pool.wait_ge(used, NCH * SLOTS + RING)
                for j in range(TS):
                    gather(ring[j], table, idx_s[:, j:j + 1], landed[j])

        def act_peer(act):
            def tile(t):
                for k in range(PH):
                    if isinstance(t, int) and k == PH - 1:
                        act.wait_ge(soft_in, 1)
                        nc.scalar.activation(gate_next[:], gate_next[:], ACT.Exp).then_inc(soft_exp, 1)
                    act.wait_ge(dots_ready, t * PH + (k + 1))
                    q = slice(k * TOP, (k + 1) * TOP)
                    nc.scalar.activation(gelus[:, q], dots[:, q], ACT.Gelu).then_inc(gelu_ready, 1)
                act.wait_ge(soft_in, t + 2)
                nc.scalar.activation(gate_next[:], gate_next[:], ACT.Exp).then_inc(soft_exp, 1)
                act.wait_ge(acc_ready, t + 1)
                act.wait_ge(y_stored, t * 16 + 16)
                nc.scalar.activation(yout[:], acc[:], ACT.Square, accum_out=small[:, 0:1]).then_inc(squares_ready, 1)
                act.wait_ge(root_in, t + (ROOTS_Y + 1))
                nc.scalar.activation(small[:, 2:3], small[:, 1:2], ACT.Sqrt).then_inc(root_out, 1)
            tile(0)
            with act.Fori(1, NCH) as t:
                tile(t)
            act.wait_ge(dots_ready, NCH * PH + 1)
            nc.scalar.activation(gelus[:, 0:TS], dots[:, 0:TS], ACT.Gelu).then_inc(gelu_ready, 1)
            act.wait_ge(acc_ready, NCH + 2)
            act.wait_ge(y_stored, (NCH + 1) * 16)
            nc.scalar.activation(yout[0:TS, :], htok2[:], ACT.Square, accum_out=small[0:TS, 0:1]).then_inc(squares_ready, 1)
            act.wait_ge(root_in, ROOTS_Y + NCH + 1)
            nc.scalar.activation(small[0:TS, 2:3], small[0:TS, 1:2], ACT.Sqrt).then_inc(root_out, 1)

        def final_norm(dve, x, rows, t):
            dve.wait_ge(squares_ready, t + (SQUARES_Y + 1))
            nc.vector.tensor_scalar(small[0:rows, 1:2], small[0:rows, 0:1], 1.0 / D, EPS, ALU.mult, ALU.add).then_inc(root_in, 1)
            dve.wait_ge(root_out, t + (ROOTS_Y + 1))
            nc.vector.reciprocal(small[0:rows, 3:4], small[0:rows, 2:3])
            dve.drain()
            nc.vector.scalar_tensor_tensor(out=yout[0:rows, :], in0=x, scalar=small[0:rows, 3:4], in1=gfin[0:rows, :],
                                           op0=ALU.mult, op1=ALU.mult).then_inc(y_ready, 1)

        def dve_peer(dve):
            dve.wait_ge(peer_made, 1)
            dve.drain().then_inc(u_used, RING)
            dve.drain().then_inc(v_used, RING)
            dve.drain().then_inc(y_ready, 1)
            dve.wait_ge(x1_stored[1], X1_STORES[1])
            dve.wait_ge(sc_staged, 1)

            def dot(t, n):
                dve.wait_ge(u_landed[n % RING], t * (16 * SLOTS // RING) + 16 * (n // RING + 1))
                u = u_ring[n % RING]
                nc.vector.tensor_tensor_reduce(u[:], u[:], htok[:], 1.0, 0.0, ALU.mult, ALU.add,
                                               dots[:, n:n + 1]).then_inc(u_used, 1)

            def accumulate(t, n):
                dve.wait_ge(v_landed[n % RING], t * (16 * SLOTS // RING) + 16 * (n // RING + 1))
                dve.wait_ge(v_used, t * SLOTS + RING + n)
                nc.vector.scalar_tensor_tensor(out=acc[:], in0=v_ring[n % RING][:], scalar=coef[:, n:n + 1],
                                               in1=acc[:], op0=ALU.mult, op1=ALU.add).then_inc(v_used, 1)

            def weigh(t, k):
                q = slice(k * TOP, (k + 1) * TOP)
                dve.wait_ge(gelu_ready, t * PH + (k + 1))
                nc.vector.tensor_tensor(coef[:, q], gelus[:, q], gate_cur[:, q], ALU.mult)
                dve.drain()

            def experts_ahead():
                dve.drain().then_inc(sc_used, 1)
                nc.vector.tensor_copy(idx_cur[:, 0:SLOTS - TOP], idx_next[:, 0:SLOTS - TOP])
                dve.drain().then_inc(idx_ready, 1)

            for k in range(PH + 1):
                if k < PH:
                    top_head(dve, k)
                    q = slice(k * TOP, (k + 1) * TOP)
                    nc.vector.tensor_copy(idx_cur[:, q], idx_next[:, q])
                    dve.drain().then_inc(idx_ready, 1)
                if k == PH - 1:
                    dve.drain().then_inc(sc_used, 1)
                if k == 1:
                    dve.wait_ge(htok_loaded, 16)
                if k > 0:
                    for j in range(TOP):
                        dot(0, (k - 1) * TOP + j)
                    dve.drain().then_inc(dots_ready, 1)
                if k == PH - 1:
                    top_softmax(dve, 1)
                    nc.vector.tensor_copy(gate_cur[:], gate_next[:].rearrange("p h j -> p (h j)"))
                    dve.drain()
            dve.wait_ge(acc_loaded, 16)
            dve.wait_ge(sc_loaded, 16)
            for k in range(PH):
                if k == PH - 1:
                    experts_ahead()
                weigh(0, k)
                for j in range(TOP):
                    accumulate(0, k * TOP + j)
                if k < PH - 1:
                    top_head(dve, k)
                if k == PH - 2:
                    top_head(dve, k + 1)
                    top_softmax(dve, 2)
            dve.drain().then_inc(acc_ready, 1)
            dve.wait_ge(gfin_loaded, 16)
            final_norm(dve, acc[:], P, 0)
            with dve.Fori(1, NCH) as t:
                nc.vector.tensor_copy(idx_cur[:, SLOTS - TOP:SLOTS], idx_next[:, SLOTS - TOP:SLOTS])
                nc.vector.tensor_copy(gate_cur[:], gate_next[:].rearrange("p h j -> p (h j)"))
                dve.drain().then_inc(idx_ready, 1)
                dve.wait_ge(htok_loaded, t * 16 + 16)
                for k in range(PH + 1):
                    if k == PH:
                        experts_ahead()
                    if k > 0:
                        weigh(t, k - 1)
                    if k == 1:
                        dve.wait_ge(acc_loaded, t * 16 + 16)
                        dve.wait_ge(sc_loaded, t * 16 + 16)
                    for j in range(TOP):
                        if k < PH:
                            dot(t, k * TOP + j)
                        if k > 0:
                            accumulate(t, (k - 1) * TOP + j)
                    if k < PH:
                        dve.drain().then_inc(dots_ready, 1)
                    if 0 < k < PH:
                        top_head(dve, k - 1)
                    if k == PH - 1:
                        top_head(dve, k)
                        top_softmax(dve, t + 2)
                dve.drain().then_inc(acc_ready, 1)
                final_norm(dve, acc[:], P, t)
            dve.wait_ge(unpacked, 16 * (2 + TS))
            for j in range(TS):
                dve.wait_ge(u_landed[j], 16 * (NCH * SLOTS // RING + 1))
                nc.vector.tensor_tensor_reduce(u_ring[j][:], u_ring[j][:], htok[:], 1.0, 0.0, ALU.mult, ALU.add,
                                               dots[:, j:j + 1]).then_inc(u_used, 1)
            dve.drain().then_inc(dots_ready, 1)
            dve.wait_ge(gelu_ready, NCH * PH + 1)
            nc.vector.tensor_tensor(coef[:, 0:TS], gelus[:, 0:TS], gate_s[:], ALU.mult)
            dve.drain()
            for j in range(TS):
                dve.wait_ge(v_landed[j], 16 * (NCH * SLOTS // RING + 1))
                if j == 0:
                    nc.vector.tensor_scalar(acc[:], v_ring[j][:], coef[:, j:j + 1], None, ALU.mult)
                else:
                    nc.vector.scalar_tensor_tensor(out=acc[:], in0=v_ring[j][:], scalar=coef[:, j:j + 1], in1=acc[:],
                                                   op0=ALU.mult, op1=ALU.add)
                dve.drain()
            dve.drain().then_inc(acc_ready, 1)
            dve.wait_ge(folded, 1)
            dve.wait_ge(acc_s_loaded, 16)
            nc.vector.tensor_tensor(htok2[:].rearrange("p (b f) -> p b f", b=4), psum[0:TS, 0:4, :],
                                    htok2[:].rearrange("p (b f) -> p b f", b=4), ALU.add)
            dve.drain().then_inc(acc_ready, 1)
            final_norm(dve, htok2[:], TS, NCH)

        def pe_peer(pe):
            pe.wait_ge(acc_ready, NCH + 1)
            for b in range(4):
                last = nc.tensor.matmul(psum[0:TS, b, :], sel[:], acc[:, b * 512:(b + 1) * 512], start=True, stop=True)
            last.then_inc(folded, 1)

        @block.sync
        def _(sp):
            sp_phase0(sp)
            sp_project(sp)
            sp_attention(sp)
            sp_merge(sp, N_BC, N_BB)
            sp_spatial(sp)
            sp_merge(sp, N_BB, N_BA)
            sp_gla(sp)
            sp_merge(sp, N_BA, N_OUT - 2)
            sp_merge(sp, N_OUT - 2, N_OUT, gates=(False, False))
            sp_out(sp)
            sp_peer(sp)
            sp.wait_ge(state_stored, 16)
            for stored in st_out:
                sp.wait_ge(stored, 16 * TS * HEADS // 2)
            sp.wait_ge(vn_stored, 16)
            sp.wait_ge(out_stored, 64)

        @block.scalar
        def _(act):
            act_phase0(act)
            act_project(act)
            act_attention(act)
            act_merge(act, N_BC, N_BB)
            act_spatial(act)
            act_merge(act, N_BB, N_BA)
            act_gla(act)
            act.wait_ge(bra_loaded, 32)
            act.wait_ge(o_normed, NCH + 1)
            act.wait_ge(state_stored, 16)
            act_wide(act, bra)
            act_merge(act, N_BA, N_OUT)
            act_out(act)
            act_peer(act)

        @block.vector
        def _(dve):
            dve_phase0(dve)
            dve_project(dve)
            dve_attention(dve)
            dve_merge(dve, N_BC, N_BB, True)
            dve_spatial(dve)
            dve_merge(dve, N_BB, N_BA, False)
            dve_gla(dve)
            dve_wide(dve, bra, 5)
            dve_merge(dve, N_BA, N_OUT, False)
            dve.drain().then_inc(merged_ready, 1)
            dve_out(dve)
            dve_peer(dve)

        @block.tensor
        def _(pe):
            pe_phase0(pe)
            pe_project(pe)
            pe_attention(pe)
            pe.wait_ge(br_hi, 5)
            pe.wait_ge(br_lo, 5)
            pe_merge(pe, N_BC, N_BB, br2, range(8))
            pe_spatial(pe)
            pe.wait_ge(br_hi, 10)
            pe.wait_ge(br_lo, 10)
            pe_merge(pe, N_BB, N_BA, br2, range(8))
            pe_gla(pe)
            pe_merge(pe, N_BA, N_OUT, actr, range(KT), ready=lambda kt: wait_piece(pe, kt, 5))
            pe_out(pe)
            pe_peer(pe)

        @block.gpsimd
        def _(pool):
            pool_constants(pool)
            pool_attention(pool)
            pool_spatial(pool)
            pool_gla(pool)
            pool_peer_constants(pool)
            pool_peer(pool)


def lay_out(inputs):
    def a(name):
        return np.asarray(inputs[name])

    def feature_major(x):
        return np.ascontiguousarray(x.T.reshape(KT, P, -1).transpose(1, 0, 2))

    def blocks(w):
        k, n = w.shape
        return w.reshape(k // P, P, n // P, P).transpose(2, 1, 0, 3).reshape(n // P, P, k)

    def paired(w):
        b = blocks(w)
        return b.reshape(-1, 2, P, b.shape[2]).transpose(0, 2, 1, 3).reshape(-1, P, 2 * b.shape[2])

    w = a("w_in")[0]
    cuts = np.cumsum([0, 1024, 1024, 2048, 2048, RANK, 1024, 1024, 1024, 3 * D])
    q, k, v, r, low, gu, gv, xq, g = [w[:, cuts[i]:cuts[i + 1]] for i in range(9)]
    low = np.concatenate([low, np.zeros((D, P - RANK), w.dtype)], 1)
    stream = np.concatenate(
        [blocks(x) for x in (a("w_mem_kv")[0], xq, q, k, v, low, gu, gv, r, g[:, 2 * D:], g[:, D:2 * D], g[:, :D])]
        + [paired(a("w_br_xattn")[0]), paired(a("w_br_gmlp")[0]), blocks(a("w_br_gla")[0]),
           blocks(a("w_out")[0]), blocks(a("peer_w_q")[0])])
    assert stream.shape == (N_END, P, D)
    bg = a("b_gate")[0]
    cols = np.concatenate([a("norm_mix_g")[0], a("norm_ffn_g")[0], a("mem_norm_g")[0],
                           bg[2 * D:], bg[D:2 * D], bg[:D], a("b_alpha")[0], a("gla_norm_g")[0]])
    x = np.concatenate([a("x_prompt")[0], a("x_sample")[:, 0]])
    return {
        "xT": feature_major(x),
        "memT": feature_major(a("mem_prompt")[0]),
        "wstream": np.ascontiguousarray(stream),
        "kcache": np.ascontiguousarray(a("cache_mem_k")[0].transpose(0, 2, 3, 1).reshape(TS, 8, P, MEM).transpose(0, 2, 1, 3)),
        "vcache": np.ascontiguousarray(a("cache_mem_v")[0].reshape(TS, 2, P, 1024).transpose(0, 2, 1, 3)),
        "ln_g": a("gmlp_ln_g")[0],
        "ln_b": a("gmlp_ln_b")[0],
        "w_spatT": np.ascontiguousarray(a("gmlp_w_s")[0].transpose(2, 0, 1)),
        "b_spat": a("gmlp_b_s").reshape(1, HEADS * CH),
        "w_first": np.ascontiguousarray(a("gmlp_w_s")[0, :, 0, 0]),
        "w_up": a("w_alpha_up")[0],
        "state": a("state_gla")[0],
        "keys": np.ascontiguousarray(np.stack([a("peer_sub_k1")[0], a("peer_sub_k2")[0]]).transpose(3, 1, 0, 2)),
        "peer_u": a("peer_u")[0],
        "peer_v": a("peer_v")[0],
        "g_final": a("norm_final_g"),
        "pcols": np.ascontiguousarray(cols.reshape(-1, P).T),
    }


_OUTS = [("y_prompt", (TP, D)), ("y_sample", (TS, D)), ("gla_p", (HEADS, DK, DV)), ("gla_s", (TS, HEADS, DK, DV)),
         ("mem_k", (MEM, 1024)), ("mem_v", (MEM, 1024)), ("gmlp_v", (TS, 1024))]


def kernel(**inputs):
    import concourse.bacc as bacc
    from concourse.bass_utils import run_bass_kernel_spmd

    nc = bacc.Bacc("TRN2", target_bir_lowering=False, num_devices=1)
    arrays = {f"in_{k}": v for k, v in lay_out(inputs).items()}
    ins = {k[3:]: nc.dram_tensor(k, v.shape, mybir.dt.from_np(v.dtype), kind="ExternalInput").ap() for k, v in arrays.items()}
    outs = {k: nc.dram_tensor(f"out_{k}", shape, F32, kind="ExternalOutput").ap() for k, shape in _OUTS}
    mixer_kernel(nc, ins, outs)
    r = run_bass_kernel_spmd(nc, [arrays], core_ids=[0]).results[0]
    got = {k: r[f"out_{k}"] for k, _ in _OUTS}
    return (got["y_prompt"].reshape(1, TP, D), got["y_sample"].reshape(TS, 1, D),
            got["gla_p"].reshape(1, 1, HEADS, DK, DV), got["gla_s"].reshape(1, TS, HEADS, DK, DV),
            got["mem_k"].reshape(1, 1, MEM, HEADS, 256), got["mem_v"].reshape(1, 1, MEM, HEADS, 256),
            got["gmlp_v"].reshape(1, TS, 1, 1024))
```
